# Optimizing a Trainium2 kernel written in Bass

```python
import jax
import jax.numpy as jnp
from jax import lax
import numpy as np

D_MODEL = 1024
BATCH = 1
SEQ = 256
DEPTH = 1
DEC_BATCH = 8
DEC_SEQ = 1
PAST_LEN = 256
PAGE_SIZE = 128

HEAD_DIM = 64
NSA_HEADS = 8
NSA_KV_HEADS = 2
NSA_GROUP = NSA_HEADS // NSA_KV_HEADS
CMP_BLOCK = 32
CMP_STRIDE = 16
CMP_HIDDEN = 256
SEL_BLOCK = 64
N_SEL = 8
WINDOW = 512
NSA_Q_BLOCK = 64
MOBA_HEADS = 8
MOBA_BLOCK = 256
MOBA_TOPK = 3
MOBA_Q_BLOCK = 32
N_EXPERTS = 32
TOP_K = 4
D_FF = D_MODEL
SWIGLU_LIMIT = 7.0
SWIGLU_ALPHA = 1.702
MOE_BLOCK = 128
ROPE_THETA = 10000.0
EPS = 1e-6
NEG = -1e30
POS_BIG = 1e30

kernel_name = 'nsa_moba_gated_hybrid_moe_step'

def in_proj_widths():
    qa = NSA_HEADS * HEAD_DIM
    kva = NSA_KV_HEADS * HEAD_DIM
    qb = MOBA_HEADS * HEAD_DIM
    return [qa, kva, kva, kva, kva, kva, kva, 3 * NSA_HEADS, qb, qb, qb, 2 * D_MODEL]

def rms_norm(x, g):
    xf = x.astype(jnp.float32)
    y = xf * lax.rsqrt(jnp.mean(xf * xf, axis=-1, keepdims=True) + EPS)
    return (y * g.astype(jnp.float32)).astype(x.dtype)

def rope(x, pos):
    half = HEAD_DIM // 2
    inv = ROPE_THETA ** (-jnp.arange(half, dtype=jnp.float32) / half)
    ang = pos.astype(jnp.float32)[:, None] * inv[None, :]
    cos = jnp.cos(ang)[None, :, None, :]
    sin = jnp.sin(ang)[None, :, None, :]
    xf = x.astype(jnp.float32)
    x1, x2 = xf[..., :half], xf[..., half:]
    return jnp.concatenate([x1 * cos - x2 * sin, x2 * cos + x1 * sin], axis=-1).astype(x.dtype)

def masked_softmax(s, mask):
    s = jnp.where(mask, s, NEG)
    m = jnp.max(s, axis=-1, keepdims=True)
    e = jnp.where(mask, jnp.exp(s - m), 0.0)
    return e / jnp.maximum(jnp.sum(e, axis=-1, keepdims=True), 1e-30)

def mixer_inputs(x, pos, norm_attn, w_in, g_qa, g_ka, g_qb, g_kb):
    B, T, _ = x.shape
    cuts = [int(c) for c in np.cumsum(in_proj_widths())[:-1]]
    parts = jnp.split(rms_norm(x, norm_attn) @ w_in, cuts, axis=-1)
    q_a, k_c, v_c, k_s, v_s, k_w, v_w, g_nsa, q_b, k_b, v_b, g_mrg = parts
    heads = lambda t, h: t.reshape(B, T, h, HEAD_DIM)
    qk = lambda t, h, g: rope(rms_norm(heads(t, h), g), pos)
    return {
        'q_a': qk(q_a, NSA_HEADS, g_qa),
        'k_c': qk(k_c, NSA_KV_HEADS, g_ka[0]), 'v_c': heads(v_c, NSA_KV_HEADS),
        'k_s': qk(k_s, NSA_KV_HEADS, g_ka[1]), 'v_s': heads(v_s, NSA_KV_HEADS),
        'k_w': qk(k_w, NSA_KV_HEADS, g_ka[2]), 'v_w': heads(v_w, NSA_KV_HEADS),
        'g_nsa': jax.nn.sigmoid(g_nsa).reshape(B, T, NSA_HEADS, 3),
        'q_b': qk(q_b, MOBA_HEADS, g_qb), 'k_b': qk(k_b, MOBA_HEADS, g_kb), 'v_b': heads(v_b, MOBA_HEADS),
        'g_mrg': jax.nn.sigmoid(g_mrg),
    }

def compress(k, pos_emb, w1, w2):
    B, T, G, _ = k.shape
    n_c = (T - CMP_BLOCK) // CMP_STRIDE + 1
    idx = jnp.arange(n_c)[:, None] * CMP_STRIDE + jnp.arange(CMP_BLOCK)[None, :]
    blk = k[:, idx] + pos_emb[None, None, :, None, :].astype(k.dtype)
    flat = blk.transpose(0, 1, 3, 2, 4).reshape(B, n_c, G, CMP_BLOCK * HEAD_DIM)
    return jax.nn.gelu(flat @ w1) @ w2

def to_blocks(k, size):
    B, T, H, _ = k.shape
    n = -(-T // size)
    k = jnp.pad(k, ((0, 0), (0, n * size - T), (0, 0), (0, 0)))
    return k.reshape(B, n, size, H, HEAD_DIM).transpose(0, 3, 1, 2, 4)

def nsa_attend(q, gates, q_pos, kc, vc, k_blk, v_blk, k_win, v_win, win_pos):
    B, Tq = q.shape[:2]
    scale = HEAD_DIM ** -0.5
    qg = q.reshape(B, Tq, NSA_KV_HEADS, NSA_GROUP, HEAD_DIM)
    t = q_pos[:, None]
    n_c = kc.shape[1]
    cmp_end = jnp.arange(n_c) * CMP_STRIDE + CMP_BLOCK - 1
    s_c = jnp.einsum('bqgrd,bcgd->bqgrc', qg, kc).astype(jnp.float32) * scale
    p_c = masked_softmax(s_c, (cmp_end[None, :] <= t)[None, :, None, None, :])
    o_c = jnp.einsum('bqgrc,bcgd->bqgrd', p_c.astype(vc.dtype), vc)
    n_s = k_blk.shape[2]
    ci = jnp.arange(n_c)[:, None] * CMP_STRIDE
    sj = jnp.arange(n_s)[None, :] * SEL_BLOCK
    overlap = ((ci < sj + SEL_BLOCK) & (ci + CMP_BLOCK > sj)).astype(jnp.float32)
    imp = jnp.einsum('bqgrc,cs->bqgs', p_c, overlap)
    blk = jnp.arange(n_s)[None, :]
    cur = t // SEL_BLOCK
    forced = (blk == 0) | (blk == cur) | (blk == cur - 1)
    score = jnp.where(forced[None, :, None, :], POS_BIG,
                      jnp.where((blk <= cur)[None, :, None, :], imp, NEG))
    _, top = lax.top_k(score, min(N_SEL, n_s))
    n = top.shape[-1]
    ok = top <= cur[None, :, :, None]
    bi = jnp.arange(B)[:, None, None, None]
    gi = jnp.arange(NSA_KV_HEADS)[None, None, :, None]
    ks = k_blk[bi, gi, top]
    vs = v_blk[bi, gi, top]
    kpos = top[..., None] * SEL_BLOCK + jnp.arange(SEL_BLOCK)
    m_s = ok[..., None] & (kpos <= q_pos[None, :, None, None, None])
    s_s = jnp.einsum('bqgrd,bqgnsd->bqgrns', qg, ks).astype(jnp.float32) * scale
    p_s = masked_softmax(s_s.reshape(B, Tq, NSA_KV_HEADS, NSA_GROUP, n * SEL_BLOCK),
                         m_s.reshape(B, Tq, NSA_KV_HEADS, 1, n * SEL_BLOCK))
    o_s = jnp.einsum('bqgrk,bqgkd->bqgrd', p_s.astype(vs.dtype),
                     vs.reshape(B, Tq, NSA_KV_HEADS, n * SEL_BLOCK, HEAD_DIM))
    wp = win_pos[None, :]
    m_w = (wp >= 0) & (wp <= t) & (wp > t - WINDOW)
    s_w = jnp.einsum('bqgrd,bkgd->bqgrk', qg, k_win).astype(jnp.float32) * scale
    p_w = masked_softmax(s_w, m_w[None, :, None, None, :])
    o_w = jnp.einsum('bqgrk,bkgd->bqgrd', p_w.astype(v_win.dtype), v_win)
    g = gates.reshape(B, Tq, NSA_KV_HEADS, NSA_GROUP, 3)
    o = g[..., 0:1] * o_c + g[..., 1:2] * o_s + g[..., 2:3] * o_w
    return o.reshape(B, Tq, NSA_HEADS * HEAD_DIM)

def nsa_prompt(q, gates, kc, vc, k_blk, v_blk, k_win, v_win):
    B, T = q.shape[:2]
    pad = ((0, 0), (WINDOW, 0), (0, 0), (0, 0))
    kw = jnp.pad(k_win, pad)
    vw = jnp.pad(v_win, pad)
    span = WINDOW + NSA_Q_BLOCK

    def body(b):
        s = b * NSA_Q_BLOCK
        return nsa_attend(lax.dynamic_slice_in_dim(q, s, NSA_Q_BLOCK, 1),
                          lax.dynamic_slice_in_dim(gates, s, NSA_Q_BLOCK, 1),
                          s + jnp.arange(NSA_Q_BLOCK, dtype=jnp.int32), kc, vc, k_blk, v_blk,
                          lax.dynamic_slice_in_dim(kw, s, span, 1),
                          lax.dynamic_slice_in_dim(vw, s, span, 1),
                          s - WINDOW + jnp.arange(span, dtype=jnp.int32))

    o = lax.map(body, jnp.arange(T // NSA_Q_BLOCK, dtype=jnp.int32))
    return o.transpose(1, 0, 2, 3).reshape(B, T, NSA_HEADS * HEAD_DIM)

def moba_attend(q, q_pos, k_blk, v_blk, k_mean):
    B, Tq = q.shape[:2]
    n_b = k_blk.shape[2]
    scale = HEAD_DIM ** -0.5
    cur = q_pos[:, None] // MOBA_BLOCK
    past = jnp.arange(n_b)[None, :] < cur
    s_g = jnp.einsum('bqhd,bhnd->bqhn', q.astype(jnp.float32), k_mean)
    s_g = jnp.where(past[None, :, None, :], s_g, NEG)
    _, top = lax.top_k(s_g, min(MOBA_TOPK, n_b))
    own = jnp.broadcast_to(cur[None, :, :, None], (B, Tq, MOBA_HEADS, 1)).astype(top.dtype)
    sel = jnp.concatenate([top, own], axis=-1)
    ok = jnp.concatenate([top < cur[None, :, :, None], jnp.ones_like(own, dtype=bool)], axis=-1)
    n = sel.shape[-1]
    bi = jnp.arange(B)[:, None, None, None]
    hi = jnp.arange(MOBA_HEADS)[None, None, :, None]
    ks = k_blk[bi, hi, sel]
    vs = v_blk[bi, hi, sel]
    kpos = sel[..., None] * MOBA_BLOCK + jnp.arange(MOBA_BLOCK)
    mask = ok[..., None] & (kpos <= q_pos[None, :, None, None, None])
    s = jnp.einsum('bqhd,bqhnsd->bqhns', q, ks).astype(jnp.float32) * scale
    p = masked_softmax(s.reshape(B, Tq, MOBA_HEADS, n * MOBA_BLOCK),
                       mask.reshape(B, Tq, MOBA_HEADS, n * MOBA_BLOCK))
    o = jnp.einsum('bqhk,bqhkd->bqhd', p.astype(vs.dtype),
                   vs.reshape(B, Tq, MOBA_HEADS, n * MOBA_BLOCK, HEAD_DIM))
    return o.reshape(B, Tq, MOBA_HEADS * HEAD_DIM)

def block_means(k_blk):
    return jnp.mean(k_blk.astype(jnp.float32), axis=3)

def moba_prompt(q, k, v):
    B, T = q.shape[:2]
    k_blk = to_blocks(k, MOBA_BLOCK)
    v_blk = to_blocks(v, MOBA_BLOCK)
    k_mean = block_means(k_blk)

    def body(b):
        s = b * MOBA_Q_BLOCK
        return moba_attend(lax.dynamic_slice_in_dim(q, s, MOBA_Q_BLOCK, 1),
                           s + jnp.arange(MOBA_Q_BLOCK, dtype=jnp.int32), k_blk, v_blk, k_mean)

    o = lax.map(body, jnp.arange(T // MOBA_Q_BLOCK, dtype=jnp.int32))
    return o.transpose(1, 0, 2, 3).reshape(B, T, MOBA_HEADS * HEAD_DIM)

def merge_branches(x, o_a, o_b, g_mrg, w_up_a, w_up_b, w_out):
    g_a, g_b = jnp.split(g_mrg, 2, axis=-1)
    return x + (g_a * (o_a @ w_up_a) + g_b * (o_b @ w_up_b)) @ w_out

def moe_ffn(x, norm_ffn, w_router, b_router, w_gu, b_gu, w_down, b_down):
    n_tok = x.shape[0]
    xn = rms_norm(x, norm_ffn)
    logits = (xn @ w_router).astype(jnp.float32) + b_router.astype(jnp.float32)
    top_v, top_e = lax.top_k(logits, TOP_K)
    gates = jax.nn.softmax(top_v, axis=-1)
    n_as = n_tok * TOP_K
    flat_e = top_e.reshape(-1)
    flat_t = jnp.arange(n_as, dtype=jnp.int32) // TOP_K
    order = jnp.argsort(flat_e)
    se = flat_e[order]
    counts = jnp.bincount(flat_e, length=N_EXPERTS)
    padded = (counts + MOE_BLOCK - 1) // MOE_BLOCK * MOE_BLOCK
    pend = jnp.cumsum(padded)
    slot = (pend - padded)[se] + jnp.arange(n_as) - (jnp.cumsum(counts) - counts)[se]
    n_blocks = -(-n_as // MOE_BLOCK) + N_EXPERTS
    cap = n_blocks * MOE_BLOCK
    slot_tok = jnp.zeros((cap,), jnp.int32).at[slot].set(flat_t[order])
    slot_gate = jnp.zeros((cap,), x.dtype).at[slot].set(gates.reshape(-1)[order].astype(x.dtype))
    block_e = jnp.minimum(jnp.searchsorted(pend, jnp.arange(n_blocks) * MOE_BLOCK, side='right'),
                          N_EXPERTS - 1)

    def expert_block(args):
        tok, e = args
        h = xn[tok] @ w_gu[e] + b_gu[e]
        gate = jnp.minimum(h[:, :D_FF], SWIGLU_LIMIT)
        up = jnp.clip(h[:, D_FF:], -SWIGLU_LIMIT, SWIGLU_LIMIT)
        return ((up + 1.0) * gate * jax.nn.sigmoid(SWIGLU_ALPHA * gate)) @ w_down[e] + b_down[e]

    y = lax.map(expert_block, (slot_tok.reshape(n_blocks, MOE_BLOCK), block_e))
    out = jnp.zeros_like(x).at[slot_tok].add(y.reshape(cap, -1) * slot_gate[:, None])
    return x + out

def setup_inputs(seed: int = 0) -> dict:
    key = jax.random.key(seed)
    ks = jax.random.split(key, 40)
    f32 = jnp.float32

    def rnd(i, shape, scale=1.0):
        return scale * jax.random.normal(ks[i], shape, f32)

    def gain(i, shape):
        return 1.0 + rnd(i, shape, 0.01)

    n_pages = PAST_LEN // PAGE_SIZE
    used = DEC_BATCH * n_pages
    n_pool = used + max(1, used // 4)
    win_buf = min(WINDOW, PAST_LEN)
    kva = (n_pool, PAGE_SIZE, NSA_KV_HEADS, HEAD_DIM)
    kvb = (n_pool, PAGE_SIZE, MOBA_HEADS, HEAD_DIM)
    winb = (DEC_BATCH, win_buf, NSA_KV_HEADS, HEAD_DIM)
    page_table = jax.random.permutation(ks[39], n_pool)[:used].reshape(DEC_BATCH, n_pages).astype(jnp.int32)
    w_in_cols = int(sum(in_proj_widths()))
    lk = CMP_BLOCK * HEAD_DIM
    wa = NSA_HEADS * HEAD_DIM
    wb = MOBA_HEADS * HEAD_DIM
    return {
        'x_prompt': rnd(0, (BATCH, SEQ, D_MODEL)),
        'x_sample': rnd(1, (DEC_BATCH, DEC_SEQ, D_MODEL)),
        'cache_nsa_cmp_k': rnd(2, kva), 'cache_nsa_cmp_v': rnd(3, kva),
        'cache_nsa_sel_k': rnd(4, kva), 'cache_nsa_sel_v': rnd(5, kva),
        'cache_nsa_win_k': rnd(6, winb), 'cache_nsa_win_v': rnd(7, winb),
        'cache_moba_k': rnd(8, kvb), 'cache_moba_v': rnd(9, kvb),
        'page_table': page_table,
        'norm_attn': gain(10, (D_MODEL,)),
        'w_in': rnd(11, (D_MODEL, w_in_cols), D_MODEL ** -0.5),
        'g_qa': gain(12, (HEAD_DIM,)),
        'g_ka': gain(13, (3, HEAD_DIM)),
        'g_kc': gain(14, (HEAD_DIM,)),
        'cmp_pos_k': rnd(15, (CMP_BLOCK, HEAD_DIM), 0.1),
        'cmp_w1_k': rnd(16, (lk, CMP_HIDDEN), lk ** -0.5),
        'cmp_w2_k': rnd(17, (CMP_HIDDEN, HEAD_DIM), CMP_HIDDEN ** -0.5),
        'cmp_pos_v': rnd(18, (CMP_BLOCK, HEAD_DIM), 0.1),
        'cmp_w1_v': rnd(19, (lk, CMP_HIDDEN), lk ** -0.5),
        'cmp_w2_v': rnd(20, (CMP_HIDDEN, HEAD_DIM), CMP_HIDDEN ** -0.5),
        'g_qb': gain(21, (HEAD_DIM,)),
        'g_kb': gain(22, (HEAD_DIM,)),
        'w_up_a': rnd(23, (wa, D_MODEL), wa ** -0.5),
        'w_up_b': rnd(24, (wb, D_MODEL), wb ** -0.5),
        'w_out': rnd(25, (D_MODEL, D_MODEL), D_MODEL ** -0.5),
        'norm_ffn': gain(26, (D_MODEL,)),
        'w_router': rnd(27, (D_MODEL, N_EXPERTS), D_MODEL ** -0.5),
        'b_router': rnd(28, (N_EXPERTS,), 0.01),
        'w_gu': rnd(29, (N_EXPERTS, D_MODEL, 2 * D_FF), D_MODEL ** -0.5),
        'b_gu': rnd(30, (N_EXPERTS, 2 * D_FF), 0.01),
        'w_down': rnd(31, (N_EXPERTS, D_FF, D_MODEL), D_FF ** -0.5),
        'b_down': rnd(32, (N_EXPERTS, D_MODEL), 0.01),
    }

def reference(x_prompt, x_sample, cache_nsa_cmp_k, cache_nsa_cmp_v, cache_nsa_sel_k, cache_nsa_sel_v,
              cache_nsa_win_k, cache_nsa_win_v, cache_moba_k, cache_moba_v, page_table,
              norm_attn, w_in, g_qa, g_ka, g_kc, cmp_pos_k, cmp_w1_k, cmp_w2_k, cmp_pos_v, cmp_w1_v, cmp_w2_v,
              g_qb, g_kb, w_up_a, w_up_b, w_out, norm_ffn, w_router, b_router, w_gu, b_gu, w_down, b_down):
    B, T, _ = x_prompt.shape
    DB, DS, _ = x_sample.shape
    past = page_table.shape[1] * PAGE_SIZE
    pos_p = jnp.arange(T, dtype=jnp.int32)
    pos_s = past + jnp.arange(DS, dtype=jnp.int32)
    P = mixer_inputs(x_prompt, pos_p, norm_attn, w_in, g_qa, g_ka, g_qb, g_kb)
    S = mixer_inputs(x_sample, pos_s, norm_attn, w_in, g_qa, g_ka, g_qb, g_kb)

    def cmp_kv(k_raw, v_raw):
        kc = rms_norm(compress(k_raw, cmp_pos_k, cmp_w1_k, cmp_w2_k), g_kc)
        vc = compress(v_raw, cmp_pos_v, cmp_w1_v, cmp_w2_v)
        return kc, vc

    def paged(cache, new):
        rows = cache[page_table].reshape((DB, past) + cache.shape[2:])
        return jnp.concatenate([rows, new], axis=1)

    kc_p, vc_p = cmp_kv(P['k_c'], P['v_c'])
    o_a_p = nsa_prompt(P['q_a'], P['g_nsa'], kc_p, vc_p, to_blocks(P['k_s'], SEL_BLOCK),
                       to_blocks(P['v_s'], SEL_BLOCK), P['k_w'], P['v_w'])
    o_b_p = moba_prompt(P['q_b'], P['k_b'], P['v_b'])
    h_p = merge_branches(x_prompt, o_a_p, o_b_p, P['g_mrg'], w_up_a, w_up_b, w_out)

    kc_s, vc_s = cmp_kv(paged(cache_nsa_cmp_k, S['k_c']), paged(cache_nsa_cmp_v, S['v_c']))
    kw_all = jnp.concatenate([cache_nsa_win_k, S['k_w']], axis=1)
    vw_all = jnp.concatenate([cache_nsa_win_v, S['v_w']], axis=1)
    win_pos = past - cache_nsa_win_k.shape[1] + jnp.arange(kw_all.shape[1], dtype=jnp.int32)
    o_a_s = nsa_attend(S['q_a'], S['g_nsa'], pos_s, kc_s, vc_s,
                       to_blocks(paged(cache_nsa_sel_k, S['k_s']), SEL_BLOCK),
                       to_blocks(paged(cache_nsa_sel_v, S['v_s']), SEL_BLOCK),
                       kw_all, vw_all, win_pos)
    kb_blk = to_blocks(paged(cache_moba_k, S['k_b']), MOBA_BLOCK)
    vb_blk = to_blocks(paged(cache_moba_v, S['v_b']), MOBA_BLOCK)
    o_b_s = moba_attend(S['q_b'], pos_s, kb_blk, vb_blk, block_means(kb_blk))
    h_s = merge_branches(x_sample, o_a_s, o_b_s, S['g_mrg'], w_up_a, w_up_b, w_out)

    y = moe_ffn(jnp.concatenate([h_p.reshape(-1, D_MODEL), h_s.reshape(-1, D_MODEL)], axis=0),
                norm_ffn, w_router, b_router, w_gu, b_gu, w_down, b_down)
    y_prompt = y[:B * T].reshape(B, T, D_MODEL)
    y_sample = y[B * T:].reshape(DB, DS, D_MODEL)
    wp = min(WINDOW, T)
    ws = min(WINDOW, kw_all.shape[1])
    return (y_prompt, y_sample,
            P['k_c'], P['v_c'], P['k_s'], P['v_s'], P['k_w'][:, T - wp:], P['v_w'][:, T - wp:], P['k_b'], P['v_b'],
            S['k_c'], S['v_c'], S['k_s'], S['v_s'], kw_all[:, -ws:], vw_all[:, -ws:], S['k_b'], S['v_b'])


_drawn_inputs = setup_inputs


def setup_inputs(seed=0):
    import zlib

    import numpy as np

    out = dict(_drawn_inputs(seed))
    spreads = {}
    factors = {'norm_attn': 3.36,
     'g_qa': 5.181,
     'g_ka': 3.582,
     'g_kc': 37.943,
     'g_qb': 8.0,
     'g_kb': 3.968,
     'b_gu': 8.0,
     'b_down': 59.761,
     'norm_ffn': 4.159,
     'b_router': 5.291}
    for name, (base, spread) in spreads.items():
        noise = np.random.default_rng([zlib.crc32(name.encode()), seed]).standard_normal(out[name].shape)
        drawn = base * np.exp(spread * noise) if base else spread * noise
        out[name] = jnp.asarray(drawn.astype(out[name].dtype))
    for name, factor in factors.items():
        out[name] = (out[name] * factor).astype(out[name].dtype)
    return out
```

```python
from contextlib import ExitStack

import numpy as np

import concourse.bass as bass
from concourse import mybir

F32 = mybir.dt.float32
I32 = mybir.dt.int32
U32 = mybir.dt.uint32
ALU = mybir.AluOpType
ACT = mybir.ActivationFunctionType
X = mybir.AxisListType.X

P = 128
D = 1024
KC = D // P
SEQ = 256
DB = 8
TOK = SEQ + DB
NT = 3
ROWS = [P, P, DB]
PAGE = 128
N_PAGES = 2
HD = 64
HALF = HD // 2
NSA_H, NSA_G, GRP = 8, 2, 4
MOBA_H = 8
KVA = NSA_G * HD
NC = 15
CST_R = 16
HID = 256
NEXP, TOPK = 32, 4
CAP = 64
ROUNDS = -(-TOK // CAP)
EPS = 1e-6
BIG = 1e30
LIMIT, ALPHA = 7.0, 1.702
QSCALE = -(HD ** -0.5)
SLOT = 4096
RING = 6
BLOCK_AT = [0, 512, 1024, 1304, 1816, 2328]
BLOCK_W = [512, 512, 280, 512, 512, 512]
GATES_AT = 2840


def constants():
    p = np.arange(P)
    parts = {}
    parts["ident"] = np.eye(P)
    pos = np.zeros((P, NT))
    pos[:, 0], pos[:, 1], pos[:, 2] = p, p + P, SEQ
    half = HD // 2
    inv = (np.float32(10000.0) ** (-np.arange(half, dtype=np.float32) / np.float32(half))).astype(np.float32)
    ang = pos.astype(np.float32)[:, :, None] * inv
    cos, sin = np.cos(ang.astype(np.float32)), np.sin(ang.astype(np.float32))
    parts["cos"] = np.concatenate([cos, cos], -1)
    parts["sin"] = np.concatenate([-sin, sin], -1)
    parts["causal"] = np.concatenate([np.zeros((P, P)), np.where(p[None, :] > p[:, None], BIG, 0.0)], 1)
    valid = (np.arange(NC) * 16 + 31)[None, None, :] <= pos[:, :2, None]
    parts["cmp_out"] = np.where(valid, 0.0, BIG)
    parts["cmp_in"] = np.where(valid, 1.0, 0.0)
    r = p % 64
    b, h, br = r // 8, r % 8, p // 64
    parts["dec_cmp"] = np.where((np.arange(120) // NC)[None, :] == b[:, None], 0.0, BIG)
    hc = np.arange(24)
    parts["gate_sel"] = (hc // 3 == h[:, None]) & (hc % 3 == 1 + br[:, None])
    parts["gate_cmp"] = (hc // 3 == h[:, None]) & (hc % 3 == 0)
    parts["own_nsa"] = np.arange(8)[None, :] == b[:, None]
    q = p % 32
    parts["own_moba"] = (np.arange(8)[None, :] == (q // 2)[:, None]) & (q < 16)[:, None]
    parts["req_rows"] = p[:, None] == b[None, :]
    rz = np.zeros((P, 4, P))
    for j in range(4):
        rz[np.arange(NC), j, 32 * j + np.arange(NC)] = 1.0
    parts["spread"] = rz
    parts["over_expert"] = (p % NEXP)[:, None]
    parts["over_base"] = np.broadcast_to((CAP * (p // NEXP + 1))[:, None], (P, P))
    parts["over_past"] = (CAP * (p // NEXP + 1))[:, None]
    parts["slots"] = np.broadcast_to((p % CAP)[None, :], (P, P))
    parts["before"] = p[:, None] < p[None, :]
    parts["ones"] = np.ones((P, P))
    parts["iota"] = np.broadcast_to(np.arange(P)[None, :], (P, P))
    at, cols = {}, 0
    for name, a in parts.items():
        n = int(np.prod(a.shape[1:]))
        at[name] = (cols, a.shape[1:])
        cols += n
    packed = np.concatenate([np.asarray(a, np.float32).reshape(P, -1) for a in parts.values()], 1)
    return at, np.ascontiguousarray(packed, dtype=np.float32)


def build(nc, t, const_at, const_w):
    ctx = ExitStack()
    with ctx:
        total = 53200
        arena = ctx.enter_context(nc.sbuf_tensor("arena", [P, total], F32))
        banks = ctx.enter_context(nc.psum_tensor("banks", [P, 8, 512], F32))

        def sem(name):
            return ctx.enter_context(nc.semaphore(name))

        dve_chain, chained = sem("dve_chain"), [0]

        def settle(ins):
            ins.then_inc(dve_chain, 1)
            chained[0] += 1
            nc.vector.wait_ge(dve_chain, chained[0])

        taken = [0]

        def at(offset, *dims):
            n = int(np.prod(dims))
            assert offset + n <= total, (offset, n)
            v = arena[:, offset:offset + n]
            if len(dims) == 1:
                return v
            names = "abcd"[:len(dims)]
            return v.rearrange(f"p ({' '.join(names)}) -> p {' '.join(names)}",
                               **{k: d for k, d in zip(names[1:], dims[1:])})

        def take(*dims):
            offset = taken[0]
            taken[0] += int(np.prod(dims))
            return at(offset, *dims)

        def region(n):
            offset = taken[0]
            taken[0] += n
            return offset

        ring = take(RING, SLOT)
        cst = take(const_w)
        moe_at = taken[0]
        xnT = take(KC, TOK)
        blk_at = region(2 * 1536 + 1536)
        v_sel, v_win = take(NT, KVA), take(NT, KVA)
        v_moba = take(NT, 512)
        g_nsa = take(NT, 24)
        qaT, qbT, kbT = take(4, TOK), take(4, TOK), take(4, TOK)
        ksT, kwT = take(TOK), take(TOK)
        kcT = take(NC + 120)
        small = take(64)
        out_at = region(2 * 4 * TOK)
        k_at = region(19 * P * 2)
        d_at = region(2 * 9 * 256 + 2 * 540)
        assert taken[0] <= total, taken[0]

        def const(name):
            c, shape = const_at[name]
            v = cst[:, c:c + int(np.prod(shape))]
            if len(shape) == 2:
                v = v.rearrange("p (a b) -> p a b", b=shape[1])
            return v

        ident, cos, sin = const("ident"), const("cos"), const("sin")
        causal, ones = const("causal"), const("ones")

        w_in = t["w_in"].rearrange("(c p) n -> p c n", p=P)

        def proj_item(a, w):
            return lambda s: (ring[:, s, 0:KC * w].rearrange("p (c n) -> p c n", c=KC), w_in[:, :, a:a + w])

        def rows_item(src, chunks, width):
            view = src.rearrange("(c p) n -> p c n", p=P)
            return lambda s: (ring[:, s, 0:chunks * width].rearrange("p (c n) -> p c n", c=chunks), view)

        items = [proj_item(a, w) for a, w in zip(BLOCK_AT, BLOCK_W)]
        items += [rows_item(t["cmp_w1_k"], 16, HID), rows_item(t["cmp_w1_v"], 16, HID)]
        items += [proj_item(GATES_AT + 512 * i, 512) for i in range(4)]
        up_a = t["w_up_a"].rearrange("(g j d) n -> g d j n", g=NSA_G, j=GRP)
        items += ["up_a", rows_item(t["w_up_b"], 4, D)]
        items += [rows_item(t["w_out"][512 * i:512 * i + 512], 4, D) for i in range(2)]
        N_DENSE = len(items)
        ring_in = [sem(f"ring_in{s}") for s in range(RING)]
        ring_count = [0] * RING
        landed = {}

        def load_item(eng, n):
            s = n % RING
            if items[n] == "up_a":
                for g in range(NSA_G):
                    dst = ring[64 * g:64 * g + 64, s, :].rearrange("p (c n) -> p c n", c=4)
                    eng.dma_start(dst, up_a[g]).then_inc(ring_in[s], 16)
                ring_count[s] += 32
            else:
                dst, src = items[n](s)
                eng.dma_start(dst, src).then_inc(ring_in[s], 16)
                ring_count[s] += 16
            landed[n] = ring_count[s]

        def slot(n, chunks):
            width = SLOT // chunks
            return ring[:, n % RING, 0:chunks * width].rearrange("p (c n) -> p c n", c=chunks)

        def promise():
            count = [0] * RING
            for n, item in enumerate(items):
                count[n % RING] += 32 if item == "up_a" else 16
                landed[n] = count[n % RING]
            return count
        dense_count = promise()

        const_in, rows_in, vec_in = sem("const_in"), sem("rows_in"), sem("vec_in")
        pages_in, ffn_gain_in = sem("pages_in"), sem("ffn_gain_in")
        stored, store_count = {}, {}

        def store(eng, dst, src, group):
            if group not in stored:
                stored[group], store_count[group] = sem(f"stored_{group}"), 0
            eng.dma_start(dst, src).then_inc(stored[group], 16)
            store_count[group] += 16

        def norm_phase(tag, src, dst, gain, scratch, first):
            sq_done, mean_done, root_done = sem(tag + "sq"), sem(tag + "mean"), sem(tag + "root")
            scaled = sem(tag + "scaled")
            turned, copied = sem(tag + "turned"), sem(tag + "copied")
            sumsq, rstd = small[:, 0:3], small[:, 4:7]
            cleared = sem(tag + "cleared") if first else None
            with nc.Block() as block:
                @block.sync
                def _(sp):
                    if not first:
                        sp.dma_start(gain, t["norm_ffn"].partition_broadcast(P)).then_inc(ffn_gain_in, 16)
                    if first:
                        sp.wait_ge(cleared, 1)
                        sp.dma_start(src[:, 0:2, :], t["x_prompt"].rearrange("a (t p) d -> p (a t) d", p=P)).then_inc(rows_in, 16)
                        sp.dma_start(src[0:DB, 2, :], t["x_sample"].rearrange("a b d -> (a b) d")).then_inc(rows_in, 16)
                        sp.dma_start(gain, t["norm_attn"].partition_broadcast(P)).then_inc(vec_in, 16)
                        sp.dma_start(cst, t["const"]).then_inc(const_in, 16)
                        for i, v in enumerate([t["g_qa"], t["g_ka"][0], t["g_ka"][1], t["g_ka"][2], t["g_qb"], t["g_kb"], t["g_kc"]]):
                            sp.dma_start(head_gain[:, i, :], v.partition_broadcast(P)).then_inc(vec_in, 16)
                        for n in range(RING):
                            load_item(sp, n)

                @block.scalar
                def _(act):
                    if first:
                        act.wait_ge(rows_in, 32)
                    for i in range(NT):
                        nc.scalar.activation(scratch, src[:, i, :], ACT.Square, accum_out=sumsq[:, i:i + 1]).then_inc(sq_done, 1)
                        act.wait_ge(sq_done, i + 1)
                    act.wait_ge(mean_done, 1)
                    nc.scalar.activation(rstd, rstd, ACT.Sqrt).then_inc(root_done, 1)
                    for c in range(1, KC, 2):
                        act.wait_ge(turned, c + 1)
                        nc.scalar.copy(xnT[:, c, :], banks[:, c, 0:TOK]).then_inc(copied, 1)

                @block.vector
                def _(dve):
                    if first:
                        nc.vector.memset(src[:, 2, :], 0.0).then_inc(cleared, 1)
                        dve.wait_ge(vec_in, 16 * 8)
                    else:
                        dve.wait_ge(ffn_gain_in, 16)
                    dve.wait_ge(sq_done, NT)
                    nc.vector.tensor_scalar(rstd, sumsq, 1.0 / D, EPS, ALU.mult, ALU.add).then_inc(mean_done, 1)
                    dve.wait_ge(root_done, 1)
                    settle(nc.vector.reciprocal(rstd, rstd))
                    for i in range(NT):
                        nc.vector.scalar_tensor_tensor(dst[:, i, :], src[:, i, :], rstd[:, i:i + 1], gain, ALU.mult, ALU.mult).then_inc(scaled, 1)
                    if first:
                        for i in (0, 4):
                            settle(nc.vector.tensor_scalar(head_gain[:, i, :], head_gain[:, i, :], QSCALE, None, ALU.mult))
                    for c in range(0, KC, 2):
                        dve.wait_ge(turned, c + 1)
                        nc.vector.tensor_copy(xnT[:, c, :], banks[:, c, 0:TOK]).then_inc(copied, 1)

                @block.tensor
                def _(pe):
                    if first:
                        pe.wait_ge(const_in, 16)
                    pe.wait_ge(scaled, NT)
                    for c in range(KC):
                        for i in range(NT):
                            r = ROWS[i]
                            mm = nc.tensor.transpose(banks[:, c, P * i:P * i + r], dst[0:r, i, P * c:P * c + P], ident[0:r, 0:r])
                        mm.then_inc(turned, 1)

        head_gain = at(out_at, 7, HD)
        x_at = k_at
        norm_phase("n1_", at(x_at, NT, D), at(x_at, NT, D), at(d_at, D), at(d_at + D, D), True)

        proj_done, proj_evac, sq_done, ss_done = sem("proj_done"), sem("proj_evac"), sem("p_sq"), sem("p_ss")
        ms_done, root_done, rope_done, v_copied = sem("p_ms"), sem("p_root"), sem("p_rope"), sem("p_vcopied")
        p_turned, p_copied = sem("p_turned"), sem("p_copied")
        cache_in, rows_cleared = sem("cache_in"), sem("rows_cleared")
        raw = [at(blk_at + 1536 * i, NT, 512) for i in range(2)]
        squares, xcos, xsin = at(blk_at + 3072, 1536), at(k_at, 1536), at(k_at + 1536, 1536)
        head_ss = at(k_at + 3072, 24)
        segs = [(0, 0, 8, 0), (1, 0, 2, 1), (1, 256, 2, 2), (2, 0, 2, 3), (3, 0, 8, 4), (4, 0, 8, 5)]
        turns = {
            0: [(qaT[:, j, :], P * j) for j in range(4)],
            1: [(ksT, 256)],
            2: [(kwT, 0)],
            3: [(qbT[:, j, :], P * j) for j in range(4)],
            4: [(kbT[:, j, :], P * j) for j in range(4)],
        }
        turns_before = [0, 4, 5, 6, 10, 14]
        stores = {1: [("k_c", 0, KVA), ("v_c", 128, KVA), ("k_s", 256, KVA), ("v_s", 384, KVA)],
                  2: [("k_w", 0, KVA), ("v_w", 128, KVA)],
                  4: [("k_b", 0, 512)], 5: [("v_b", 0, 512)]}
        for n in stores:
            stored[n], store_count[n] = sem(f"stored_{n}"), 0
        cmp_rows = [at(d_at + 2304 * i, 9, NSA_G, 2 * HD).rearrange("p s g (two d) -> p s g two d", two=2) for i in range(2)]

        with nc.Block() as block:
            @block.sync
            def _(sp):
                pages = at(k_at + 3100, 16).bitcast(I32)
                sp.dma_start(pages[0:1, :], t["page_table"].rearrange("a b -> (a b)").unsqueeze(0)).then_inc(pages_in, 16)
                sp.wait_ge(pages_in, 16)
                for b in range(DB):
                    for g in range(N_PAGES):
                        page = sp.value_load(pages[0:1, 2 * b + g:2 * b + g + 1], min_val=0, max_val=t["cache_nsa_cmp_k"].shape[0] - 1)
                        for kv, name in enumerate(("cache_nsa_cmp_k", "cache_nsa_cmp_v")):
                            for group in range(NSA_G):
                                sp.dma_start(cmp_rows[kv][64 * g:64 * g + 64, 1 + b, group],
                                             t[name][page].rearrange("(p two) g d -> p g two d", two=2)[:, group]).then_inc(cache_in, 16)
                for n in range(6):
                    sp.wait_ge(proj_done, 3 * (n + 1))
                    load_item(sp, n + RING)
                    if n in stores:
                        sp.wait_ge(rope_done, n + 1) if n < 5 else sp.wait_ge(proj_evac, 36)
                        for name, c, w in stores[n]:
                            p_out, s_out = t["p_" + name], t["s_" + name]
                            store(sp, p_out.rearrange("a (t p) h d -> p (a t) (h d)", p=P), raw[n % 2][:, 0:2, c:c + w], n)
                            dst = s_out.rearrange("a b h d -> (a b) (h d)") if name not in ("k_w", "v_w") else None
                            if name in ("k_w", "v_w"):
                                dst = s_out[:, SEQ, :, :].rearrange("a h d -> a (h d)")
                            store(sp, dst, raw[n % 2][0:DB, 2, c:c + w], n)
                for name, src in (("s_k_w", "cache_nsa_win_k"), ("s_v_w", "cache_nsa_win_v")):
                    store(sp, t[name][:, 0:SEQ].rearrange("b s h d -> b (s h d)"), t[src].rearrange("b s h d -> b (s h d)"), "windows")

            @block.tensor
            def _(pe):
                def project(n):
                    w = BLOCK_W[n]
                    weights = ring[:, n % RING, 0:KC * w].rearrange("p (c n) -> p c n", c=KC)
                    pe.wait_ge(ring_in[n % RING], landed[n])
                    if n >= 2:
                        pe.wait_ge(proj_evac, 6 * (n - 1))
                    for i in range(2):
                        for c in range(KC):
                            mm = nc.tensor.matmul(banks[:, 2 * (n % 2) + i, 0:w], xnT[:, c, P * i:P * i + P], weights[:, c, :],
                                                  start=(c == 0), stop=(c == KC - 1))
                        mm.then_inc(proj_done, 1)
                    q = w // 4
                    for c in range(KC):
                        for j in range(4):
                            mm = nc.tensor.matmul(banks[32 * j:32 * j + DB, 4 + n % 2, 0:q], xnT[:, c, SEQ:TOK],
                                                  weights[:, c, q * j:q * j + q], start=(c == 0), stop=(c == KC - 1),
                                                  tile_position=(0, 32 * j))
                    mm.then_inc(proj_done, 1)

                def turn(n):
                    pe.wait_ge(rope_done, n + 1)
                    for k, (_, c0) in enumerate(turns[n]):
                        job = turns_before[n] + k
                        if job >= 2:
                            pe.wait_ge(p_copied, job - 1)
                        for i in range(NT):
                            r = ROWS[i]
                            mm = nc.tensor.transpose(banks[:, 6 + job % 2, P * i:P * i + r], raw[n % 2][0:r, i, c0:c0 + P], ident[0:r, 0:r])
                        mm.then_inc(p_turned, 1)

                for n in range(6):
                    project(n)
                    if n >= 1:
                        turn(n - 1)

            @block.scalar
            def _(act):
                def evacuate(n):
                    w = BLOCK_W[n]
                    q = w // 4
                    if n >= 2:
                        act.wait_ge(p_turned, turns_before[n - 1])
                        act.wait_ge(v_copied, [0, 0, 0, 1, 3, 3][n])
                        if n - 2 in stores:
                            act.wait_ge(stored[n - 2], 32 * len(stores[n - 2]))
                    for i in range(2):
                        act.wait_ge(proj_done, 3 * n + i + 1)
                        nc.scalar.copy(raw[n % 2][:, i, 0:w], banks[:, 2 * (n % 2) + i, 0:w]).then_inc(proj_evac, 1)
                    act.wait_ge(proj_done, 3 * n + 3)
                    for j in range(4):
                        nc.scalar.copy(raw[n % 2][0:DB, 2, q * j:q * j + q], banks[32 * j:32 * j + DB, 4 + n % 2, 0:q]).then_inc(proj_evac, 1)

                def roots(s):
                    nh = segs[s][2]
                    act.wait_ge(ms_done, s + 1)
                    nc.scalar.activation(head_ss[:, 0:NT * nh], head_ss[:, 0:NT * nh], ACT.Sqrt).then_inc(root_done, 1)

                def copies(n):
                    for k, (dst, _) in enumerate(turns[n]):
                        job = turns_before[n] + k
                        act.wait_ge(p_turned, job + 1)
                        nc.scalar.copy(dst, banks[:, 6 + job % 2, 0:TOK]).then_inc(p_copied, 1)

                act.wait_ge(rows_cleared, 2)
                evacuate(0)
                roots(0)
                evacuate(1)
                for n in range(1, 6):
                    for s, seg in enumerate(segs):
                        if seg[0] == n:
                            roots(s)
                    copies(n - 1)
                    if n + 1 < 6:
                        evacuate(n + 1)

            @block.gpsimd
            def _(pool):
                for n in range(6):
                    pool.wait_ge(proj_evac, 6 * (n + 1))
                    for s, (blk, c0, nh, _) in enumerate(segs):
                        if blk != n:
                            continue
                        if s >= 1:
                            pool.wait_ge(ss_done, s)
                        x = raw[n % 2][:, :, c0:c0 + nh * HD]
                        nc.gpsimd.tensor_tensor(squares[:, 0:NT * nh * HD].rearrange("p (t c) -> p t c", t=NT), x, x, ALU.mult).then_inc(sq_done, 1)
                    if n == 1:
                        nc.gpsimd.tensor_copy(v_sel, raw[1][:, :, 384:512]).then_inc(v_copied, 1)
                    if n == 2:
                        nc.gpsimd.tensor_copy(v_win, raw[0][:, :, 128:256]).then_inc(v_copied, 1)
                        nc.gpsimd.tensor_copy(g_nsa, raw[0][:, :, 256:280]).then_inc(v_copied, 1)
                    if n == 5:
                        nc.gpsimd.tensor_copy(v_moba, raw[1]).then_inc(v_copied, 1)

            @block.vector
            def _(dve):
                for i in range(2):
                    nc.vector.memset(raw[i][:, 2, :], 0.0).then_inc(rows_cleared, 1)
                for s, (n, c0, nh, gi) in enumerate(segs):
                    x = raw[n % 2][:, :, c0:c0 + nh * HD].rearrange("p t (h d) -> p t h d", d=HD)
                    full = [P, NT, nh, HD]
                    view = lambda a: a[:, 0:NT * nh * HD].rearrange("p (t h d) -> p t h d", t=NT, h=nh)
                    ss = head_ss[:, 0:NT * nh].rearrange("p (t h) -> p t h", t=NT)
                    dve.wait_ge(sq_done, s + 1)
                    nc.vector.tensor_reduce(ss, view(squares), X, ALU.add).then_inc(ss_done, 1)
                    dve.wait_ge(ss_done, s + 1)
                    nc.vector.tensor_scalar(ss, ss, 1.0 / HD, EPS, ALU.mult, ALU.add).then_inc(ms_done, 1)
                    dve.wait_ge(root_done, s + 1)
                    settle(nc.vector.reciprocal(ss, ss))
                    settle(nc.vector.tensor_tensor(x, x, ss.unsqueeze(3).broadcast_to(full), ALU.mult))
                    settle(nc.vector.tensor_tensor(x, x, head_gain[:, gi, :].unsqueeze(1).unsqueeze(1).broadcast_to(full), ALU.mult))
                    nc.vector.tensor_tensor(view(xcos), x, cos.unsqueeze(2).broadcast_to(full), ALU.mult)
                    lo = [P, NT, nh, HALF]
                    nc.vector.tensor_tensor(view(xsin)[:, :, :, 0:HALF], x[:, :, :, HALF:HD], sin[:, :, 0:HALF].unsqueeze(2).broadcast_to(lo), ALU.mult)
                    settle(nc.vector.tensor_tensor(view(xsin)[:, :, :, HALF:HD], x[:, :, :, 0:HALF], sin[:, :, HALF:HD].unsqueeze(2).broadcast_to(lo), ALU.mult))
                    if s == 0:
                        pairs = x.rearrange("p t (j g) d -> p t j g d", g=NSA_G)
                        for g in range(NSA_G):
                            last = nc.vector.tensor_tensor(pairs[:, :, :, g, :], view(xcos)[:, :, GRP * g:GRP * g + GRP, :],
                                                           view(xsin)[:, :, GRP * g:GRP * g + GRP, :], ALU.add)
                    else:
                        last = nc.vector.tensor_tensor(x, view(xcos), view(xsin), ALU.add)
                    if s == len(segs) - 1 or segs[s + 1][0] != n:
                        last.then_inc(rope_done, 1)
                        dve.wait_ge(rope_done, n + 1)
                    else:
                        settle(last)
        c_turned, c_out = sem("c_turned"), [sem("c_copied_act"), sem("c_copied_dve")]
        hid_done, h_chain, bent, h_ready = sem("hid_done"), sem("h_chain"), sem("bent"), sem("h_ready")
        packed_done, rows_out, c_ms, c_root, c_normed = sem("packed_done"), sem("rows_out"), sem("c_ms"), sem("c_root"), sem("c_normed")
        c_final, c_kept, c_zero, small_in, prompt_in = sem("c_final"), sem("c_kept"), sem("c_zero"), sem("small_in"), sem("prompt_in")
        rT = [at(k_at + 2432 * i, 19, P) for i in range(2)]
        hidden = [at(d_at + 4608 + 540 * i, 2, NSA_G, 9 * NC) for i in range(2)]
        w2 = [at(blk_at + 128 * i, 2, HD) for i in range(2)]
        pos_rows = [at(blk_at + 256 + P * i, P) for i in range(2)]
        pre, cube, bend = ([at(blk_at + 512 + 1080 * a + 270 * i, 270) for i in range(4)] for a in range(3))
        kc_rows = at(blk_at + 3752, 2, P)
        kc_sq, kc_ss = at(blk_at + 4008, 2 * P), at(blk_at + 4264, 4)
        vcZ, vc_rows = at(k_at + 4096, 4, P), at(k_at + 4608, 2, P)
        pieces = [(0, NC, 0), (1, 120, 9 - 8)]
        GELU_C = float(np.sqrt(2.0 / np.pi))
        with nc.Block() as block:
            @block.sync
            def _(sp):
                for n in stores:
                    sp.wait_ge(stored[n], 32 * len(stores[n]))
                for i, kv in enumerate("kv"):
                    sp.dma_start(pos_rows[i][0:CST_R, :], t["cmp_pos_" + kv].rearrange("(p two) d -> p (two d)", two=2)).then_inc(small_in, 16)
                    sp.dma_start(w2[i], t["cmp_w2_" + kv].rearrange("(m p) d -> p m d", p=P)).then_inc(small_in, 16)
                for i, name in enumerate(("p_k_c", "p_v_c")):
                    for g in range(NSA_G):
                        sp.dma_start(cmp_rows[i][:, 0, g], t[name].rearrange("a (p two) g d -> (a p) g two d", two=2)[:, g]).then_inc(prompt_in, 16)
                for i in range(2):
                    sp.wait_ge(hid_done, 2 * (i + 1))
                    load_item(sp, 6 + i + RING)

            @block.tensor
            def _(pe):
                pe.wait_ge(small_in, 64)
                pe.wait_ge(prompt_in, 64)
                pe.wait_ge(cache_in, 16 * 64)
                for job in range(20):
                    if job >= 4:
                        pe.wait_ge(c_out[job % 2], job // 2 - 1)
                    if job < 2:
                        mm = nc.tensor.transpose(banks[:, job % 4, 0:CST_R], pos_rows[job][0:CST_R, :], ident[0:CST_R, 0:CST_R])
                    else:
                        i, q = divmod(job - 2, 9)
                        for g in range(NSA_G):
                            mm = nc.tensor.transpose(banks[:, job % 4, P * g:P * g + P], cmp_rows[i][:, q, g].rearrange("p two d -> p (two d)"), ident)
                    mm.then_inc(c_turned, 1)
                for i in range(2):
                    w1 = slot(6 + i, 16)
                    pe.wait_ge(ring_in[(6 + i) % RING], landed[6 + i])
                    for e in range(2):
                        pe.wait_ge(c_out[e], [6, 10][i])
                    for m in range(2):
                        for r in range(CST_R):
                            mm = nc.tensor.matmul(banks[:, 4 + 2 * i + m, 0:19 * NC].rearrange("p (s c) -> p s c", c=NC), w1[:, r, P * m:P * m + P],
                                                  rT[i][:, :, r:r + 113:8], start=(r == 0), stop=(r == CST_R - 1))
                        mm.then_inc(hid_done, 1)
                for i in range(2):
                    pe.wait_ge(h_ready, 4 * (i + 1))
                    for part, rows, s0 in pieces:
                        n = rows // NC
                        for g in range(NSA_G):
                            for m in range(2):
                                mm = nc.tensor.matmul(banks[0:rows, i, P * part + HD * g:P * part + HD * g + HD],
                                                      hidden[i][:, m, g, NC * s0:NC * (s0 + n)], w2[i][:, m, :], start=(m == 0), stop=(m == 1))
                    mm.then_inc(packed_done, 1)
                pe.wait_ge(rows_out, 4)
                for j in range(4):
                    mm = nc.tensor.matmul(banks[:, 3, P * j:P * j + P], const("spread")[0:NC, j, :], vc_rows[0:NC, 0, :], start=True, stop=True)
                mm.then_inc(c_final, 1)
                pe.wait_ge(c_normed, 1)
                for part, rows, _ in pieces:
                    mm = nc.tensor.transpose(banks[:, 2, NC * part:NC * part + rows], kc_rows[0:rows, part, :], ident[0:rows, 0:rows])
                mm.then_inc(c_final, 1)

            def copies(eng, copy, e):
                for job in range(e, 20, 2):
                    eng.wait_ge(c_turned, job + 1)
                    if job < 2:
                        eng.wait_ge(c_zero, 1)
                        copy(rT[job][:, 18, 0:CST_R], banks[:, job % 4, 0:CST_R]).then_inc(c_out[e], 1)
                    else:
                        i, q = divmod(job - 2, 9)
                        copy(rT[i][:, 2 * q:2 * q + 2, :].rearrange("p a b -> p (a b)"), banks[:, job % 4, 0:2 * P]).then_inc(c_out[e], 1)

            @block.scalar
            def _(act):
                copies(act, nc.scalar.copy, 0)
                for k in range(4):
                    act.wait_ge(bent, k + 1)
                    nc.scalar.activation(bend[k], cube[k], ACT.Tanh, scale=GELU_C).then_inc(h_chain, 1)
                act.wait_ge(c_ms, 1)
                nc.scalar.activation(kc_ss, kc_ss, ACT.Sqrt).then_inc(c_root, 1)
                act.wait_ge(c_final, 2)
                nc.scalar.copy(kcT, banks[:, 2, 0:NC + 120]).then_inc(c_kept, 1)

            @block.gpsimd
            def _(pool):
                for i in range(2):
                    nc.gpsimd.memset(rT[i][:, 18, :], 0.0)
                nc.gpsimd.memset(kc_rows, 0.0).then_inc(c_zero, 1)

            @block.vector
            def _(dve):
                copies(dve, nc.vector.tensor_copy, 1)
                for k in range(4):
                    dve.wait_ge(hid_done, k + 1)
                    bank = banks[:, 4 + k, :]
                    settle(nc.vector.tensor_scalar(pre[k], bank[:, 0:270], bank[:, 270:271], None, ALU.add))
                    settle(nc.vector.tensor_tensor(cube[k], pre[k], pre[k], ALU.mult))
                    settle(nc.vector.tensor_scalar(cube[k], cube[k], 0.044715, 1.0, ALU.mult, ALU.add))
                    nc.vector.tensor_tensor(cube[k], cube[k], pre[k], ALU.mult).then_inc(bent, 1)
                for k in range(4):
                    dve.wait_ge(h_chain, k + 1)
                    view = lambda a, g: a.rearrange("p (s g c) -> p s g c", s=9, g=NSA_G)[:, :, g, :]
                    for g in range(NSA_G):
                        nc.vector.scalar_tensor_tensor(hidden[k // 2][:, k % 2, g, :].rearrange("p (s c) -> p s c", c=NC), view(bend[k], g), 1.0,
                                                       view(pre[k], g), ALU.add, ALU.mult).then_inc(h_ready, 1)
                for i, dst in enumerate((kc_rows, vc_rows)):
                    dve.wait_ge(packed_done, i + 1)
                    for part, rows, _ in pieces:
                        nc.vector.tensor_scalar(dst[0:rows, part, :], banks[0:rows, i, P * part:P * part + P], 0.5, None, ALU.mult).then_inc(rows_out, 1)
                dve.wait_ge(rows_out, 4)
                x = kc_rows.rearrange("p a (g d) -> p (a g) d", d=HD)
                sq = kc_sq.rearrange("p (a d) -> p a d", d=HD)
                settle(nc.vector.tensor_tensor(sq, x, x, ALU.mult))
                settle(nc.vector.tensor_reduce(kc_ss, sq, X, ALU.add))
                nc.vector.tensor_scalar(kc_ss, kc_ss, 1.0 / HD, EPS, ALU.mult, ALU.add).then_inc(c_ms, 1)
                dve.wait_ge(c_root, 1)
                settle(nc.vector.reciprocal(kc_ss, kc_ss))
                settle(nc.vector.tensor_tensor(x, x, kc_ss.unsqueeze(2).broadcast_to([P, 4, HD]), ALU.mult))
                nc.vector.tensor_tensor(x, x, head_gain[:, 6, :].unsqueeze(1).broadcast_to([P, 4, HD]), ALU.mult).then_inc(c_normed, 1)
                dve.wait_ge(c_final, 1)
                nc.vector.tensor_copy(vcZ.rearrange("p a b -> p (a b)"), banks[:, 3, :]).then_inc(c_kept, 1)

        oaT, obT = at(out_at, 4, TOK), at(out_at + 4 * TOK, 4, TOK)
        q_nsa, q_cmp, q_moba = at(d_at, 576), at(d_at + 576, 64), at(d_at + 640, 4, 272)
        p_nsa, p_moba, p_cmp = at(d_at + 1728, 257), at(d_at + 1988, 257), at(d_at + 2248, 120)
        pT_nsa, pT_new, pT_moba = at(d_at + 2368, 2, 152), at(d_at + 2672, 152), at(d_at + 2824, 2, 88)
        pT_mnew, pT_cmp = at(d_at + 3000, 88), at(d_at + 3088, 88)
        own_new = at(d_at + 3176, 2, 8)
        soft = at(d_at + 3192, 24)
        o_nsa, o_moba = at(d_at + 3216, 2, P), at(d_at + 3472, 2, 512)
        sig_nsa = g_nsa
        cache = [at(blk_at + 1536 * i, 1536) for i in range(3)]
        kT = [at(k_at + 1536 * i, 1536) for i in range(2)]
        slot_in = [sem(f"cache_slot{i}") for i in range(3)]
        q_spread, k_turned, k_out, qk_done = sem("q_spread"), sem("k_turned"), [sem("k_out_act"), sem("k_out_dve")], sem("qk_done")
        gate_e, gate_done, gate_rows, d_min, d_exp = (sem("d_" + x) for x in ("ge", "gd", "gr", "min", "exp"))
        d_prob, d_turned, d_kept, pv_done, o_out, o_turned, o_kept = (sem("d_" + x) for x in ("prob", "turned", "kept", "pv", "oout", "oturned", "okept"))
        K_NAMES = ("cache_nsa_sel_k", "cache_nsa_win_k", "cache_moba_k")
        V_NAMES = ("cache_nsa_sel_v", "cache_nsa_win_v", "cache_moba_v")
        with nc.Block() as block:
            @block.sync
            def _(sp):
                pages = at(k_at + 3100, 16).bitcast(I32)
                sp.dma_start(pages[0:1, :], t["page_table"].rearrange("a b -> (a b)").unsqueeze(0)).then_inc(pages_in, 16)
                sp.wait_ge(pages_in, 32)
                for q in range(2 * DB):
                    b, names = q % DB, (K_NAMES if q < DB else V_NAMES)
                    if q >= 3:
                        if q - 3 < DB:
                            sp.wait_ge(k_turned, 3 * (q - 3) + 3)
                        else:
                            sp.wait_ge(pv_done, q - 3 - DB + 1)
                    dst, arrived = cache[q % 3], slot_in[q % 3]
                    for g in range(N_PAGES):
                        page = sp.value_load(pages[0:1, 2 * b + g:2 * b + g + 1], min_val=0, max_val=t["cache_moba_k"].shape[0] - 1)
                        sp.dma_start(dst[:, P * g:P * g + P], t[names[0]][page].rearrange("p h d -> p (h d)")).then_inc(arrived, 16)
                        sp.dma_start(dst[:, 512 + 512 * g:1024 + 512 * g], t[names[2]][page].rearrange("p h d -> p (h d)")).then_inc(arrived, 16)
                    sp.dma_start(dst[:, 256:512].rearrange("p (t n) -> p t n", t=2),
                                 t[names[1]][b].rearrange("(t p) h d -> p t (h d)", p=P)).then_inc(arrived, 16)

            @block.gpsimd
            def _(pool):
                nc.gpsimd.memset(at(d_at, 1728), 0.0).then_inc(q_spread, 1)
                nc.gpsimd.memset(at(d_at + 2368, 808), 0.0).then_inc(q_spread, 1)

            @block.tensor
            def _(pe):
                def turn_keys(b):
                    pe.wait_ge(slot_in[b % 3], 80 * (b // 3 + 1))
                    for k in range(3):
                        job = 3 * b + k
                        if job >= 4:
                            pe.wait_ge(k_out[job % 2], job // 2 - 1)
                        for i in range(4):
                            c = [P * i, 512 + 512 * (i % 2) + P * (i // 2), 512 + 512 * (i % 2) + P * (2 + i // 2)][k]
                            mm = nc.tensor.transpose(banks[:, job % 4, P * i:P * i + P], cache[b % 3][:, c:c + P], ident)
                        mm.then_inc(k_turned, 1)

                def scores(b):
                    for e in range(2):
                        pe.wait_ge(k_out[e], (3 * b + 3 + 1 - e) // 2)
                    keys = kT[b % 2]
                    for c0, c1, new in ((0, 256, False), (256, 257, True)):
                        for br in range(2):
                            rhs = (ksT, kwT)[br][:, SEQ + b:SEQ + b + 1] if new else keys[:, 256 * br:256 * br + 256]
                            nc.tensor.matmul(banks[64 * br:64 * br + 64, 4, c0:c1], q_nsa[:, 64 * b:64 * b + 64], rhs,
                                             start=(b == 0 and not new), stop=(b == DB - 1), skip_group_check=True)
                        for j in range(4):
                            rhs = kbT[:, j, SEQ + b:SEQ + b + 1] if new else keys[:, 512 + 256 * j:768 + 256 * j]
                            mm = nc.tensor.matmul(banks[32 * j:32 * j + 32, 5, c0:c1], q_moba[:, j, 32 * b:32 * b + 32], rhs,
                                                  start=(b == 0 and not new), stop=(b == DB - 1), skip_group_check=True, tile_position=(0, 32 * j))
                    mm.then_inc(qk_done, 1)

                turn_keys(0)
                pe.wait_ge(q_spread, 3)
                nc.tensor.matmul(banks[0:64, 6, 0:120], q_cmp, kcT[:, NC:NC + 120], start=True, stop=True)
                pe.wait_ge(gate_done, 1)
                nc.tensor.matmul(banks[:, 7, 0:24], const("req_rows")[0:DB, :], sig_nsa[0:DB, 2, :], start=True, stop=True).then_inc(gate_rows, 1)
                for b in range(DB):
                    if b + 1 < DB:
                        turn_keys(b + 1)
                    scores(b)
                for e in range(2):
                    pe.wait_ge(k_out[e], 12)
                for i, (src, new) in enumerate(((p_nsa, own_new[:, 0, :]), (p_moba, own_new[:, 1, :]))):
                    pe.wait_ge(d_prob, i + 1)
                    for k in range(2):
                        nc.tensor.transpose(banks[:, i, P * k:P * k + P], src[:, P * k:P * k + P], ident)
                    nc.tensor.transpose(banks[0:8, i, 256:384], new, ident).then_inc(d_turned, 1)
                pe.wait_ge(d_prob, 3)
                nc.tensor.transpose(banks[0:120, 2, 0:64], p_cmp[0:64, :], ident[0:64, 0:64]).then_inc(d_turned, 1)
                pe.wait_ge(d_kept, 7)
                for b in range(DB):
                    q = DB + b
                    pe.wait_ge(slot_in[q % 3], 80 * (q // 3 + 1))
                    v, row, w = cache[q % 3], 32 * (b % 4), 8 * b
                    out = banks[row:row + 32, 6, P * (b // 4):P * (b // 4) + P]
                    terms = []
                    for br, v_new in enumerate((v_sel, v_win)):
                        terms.append((pT_new[0:DB, 64 * br + w:64 * br + w + 32], v_new[0:DB, 2, :]))
                        for k in range(2):
                            terms.append((pT_nsa[:, k, 64 * br + w:64 * br + w + 32], v[:, 256 * br + P * k:256 * br + P * k + P]))
                    terms.append((pT_cmp[0:120, w:w + 32], vc_rows[0:120, 1, :]))
                    for n, (lhsT, rhs) in enumerate(terms):
                        nc.tensor.matmul(out, lhsT, rhs, start=(n == 0), stop=(n == len(terms) - 1), tile_position=(0, row))
                    out = banks[row:row + 32, 4 + b // 4, :]
                    nc.tensor.matmul(out, pT_mnew[0:DB, w:w + 32], v_moba[0:DB, 2, :], start=True, stop=False, tile_position=(0, row))
                    for k in range(2):
                        mm = nc.tensor.matmul(out, pT_moba[:, k, w:w + 32], v[:, 512 + 512 * k:1024 + 512 * k], start=False, stop=(k == 1), tile_position=(0, row))
                    mm.then_inc(pv_done, 1)
                pe.wait_ge(o_out, 3)
                for n in range(2):
                    nc.tensor.transpose(banks[:, 0, P * n:P * n + P], o_nsa[:, n, :], ident)
                for n in range(2):
                    for j in range(4):
                        mm = nc.tensor.transpose(banks[:, 1 + n, P * j:P * j + P], o_moba[:, n, P * j:P * j + P], ident)
                mm.then_inc(o_turned, 1)

            def copy_keys(eng, copy, e):
                for job in range(e, 3 * DB, 2):
                    b, k = divmod(job, 3)
                    eng.wait_ge(k_turned, job + 1)
                    if b >= 2:
                        eng.wait_ge(qk_done, b - 1)
                    copy(kT[b % 2][:, 512 * k:512 * k + 512], banks[:, job % 4, :]).then_inc(k_out[e], 1)

            @block.scalar
            def _(act):
                nc.scalar.activation(sig_nsa, sig_nsa, ACT.Exp, scale=-1.0).then_inc(gate_e, 1)
                copy_keys(act, nc.scalar.copy, 0)
                for i, (dst, src, rows) in enumerate(((p_nsa, banks[:, 4, 0:257], P), (p_moba, banks[:, 5, 0:257], P), (p_cmp[0:64, :], p_cmp[0:64, :], 64))):
                    act.wait_ge(d_min, i + 1)
                    nc.scalar.activation(dst, src, ACT.Exp, scale=-1.0, bias=soft[0:rows, i:i + 1], accum_out=soft[0:rows, 4 + i:5 + i]).then_inc(d_exp, 1)
                act.wait_ge(d_turned, 2)
                for k in range(2):
                    src = banks[:, 1, P * k:P * k + P].rearrange("p (j q) -> p j q", q=32)[:, :, 0:16].rearrange("p j (b h) -> p j b h", h=2)
                    dst = pT_moba[:, k, 0:64].rearrange("p (b j h) -> p j b h", b=8, j=4)
                    nc.scalar.copy(dst, src).then_inc(d_kept, 1)
                src = banks[0:8, 1, 256:384].rearrange("p (j q) -> p j q", q=32)[:, :, 0:16].rearrange("p j (b h) -> p j b h", h=2)
                nc.scalar.copy(pT_mnew[0:8, 0:64].rearrange("p (b j h) -> p j b h", b=8, j=4), src).then_inc(d_kept, 1)
                act.wait_ge(d_turned, 3)
                nc.scalar.copy(pT_cmp[0:120, 0:64], banks[0:120, 2, 0:64]).then_inc(d_kept, 1)
                for n in range(2):
                    act.wait_ge(pv_done, 4 * n + 4)
                    nc.scalar.copy(o_moba[:, n, :], banks[:, 4 + n, :]).then_inc(o_out, 1)
                act.wait_ge(o_turned, 1)
                for j in range(4):
                    for h in range(2):
                        half = slice(64 * h, 64 * h + 64)
                        src = banks[half, 1:3, P * j + 2 * j + h:P * j + 2 * j + h + 97:32]
                        last = nc.scalar.copy(obT[half, j, SEQ:TOK].rearrange("p (n b) -> p n b", n=2), src)
                last.then_inc(o_kept, 1)

            @block.vector
            def _(dve):
                dve.wait_ge(q_spread, 2)
                for g in range(2):
                    half = slice(64 * g, 64 * g + 64)
                    src = qaT[half, :, SEQ:TOK].rearrange("p j b -> p b j")
                    nc.vector.tensor_copy(q_nsa[half, :].rearrange("p (b x) -> p b x", x=72)[:, :, 4 * g:4 * g + 4], src)
                    nc.vector.tensor_copy(q_cmp[half, :].rearrange("p (b x) -> p b x", x=8)[:, :, 4 * g:4 * g + 4], src)
                    last = nc.vector.tensor_copy(q_moba[half].rearrange("p j (b x) -> p j b x", x=34)[:, :, :, g], qbT[half, :, SEQ:TOK])
                last.then_inc(q_spread, 1)
                dve.wait_ge(gate_e, 1)
                flat = sig_nsa.rearrange("p a b -> p (a b)")
                settle(nc.vector.tensor_scalar(flat, flat, 1.0, None, ALU.add))
                nc.vector.reciprocal(flat, flat).then_inc(gate_done, 1)
                copy_keys(dve, nc.vector.tensor_copy, 1)
                dve.wait_ge(qk_done, DB)
                for i in range(2):
                    nc.vector.tensor_reduce(soft[:, i:i + 1], banks[:, 4 + i, 0:257], X, ALU.min).then_inc(d_min, 1)
                nc.vector.tensor_tensor_reduce(p_cmp[0:64, :], banks[0:64, 6, 0:120], const("dec_cmp")[0:64, :], 1.0, 3e38,
                                               ALU.add, ALU.min, soft[0:64, 2:3]).then_inc(d_min, 1)
                dve.wait_ge(gate_rows, 1)
                nc.vector.tensor_tensor_reduce(o_nsa[:, 0, 0:24], banks[:, 7, 0:24], const("gate_sel"), 1.0, 0.0, ALU.mult, ALU.add, soft[:, 8:9])
                settle(nc.vector.tensor_tensor_reduce(o_nsa[0:64, 1, 0:24], banks[0:64, 7, 0:24], const("gate_cmp")[0:64, :], 1.0, 0.0, ALU.mult, ALU.add, soft[0:64, 10:11]))
                for i, (p, rows, cols) in enumerate(((p_nsa, P, 257), (p_moba, P, 257), (p_cmp, 64, 120))):
                    dve.wait_ge(d_exp, i + 1)
                    weight = soft[0:rows, 4 + i:5 + i]
                    settle(nc.vector.reciprocal(weight, weight))
                    if i != 1:
                        settle(nc.vector.tensor_tensor(weight, weight, soft[0:rows, 8 + i:9 + i], ALU.mult))
                    scaled = nc.vector.tensor_scalar(p[0:rows, :], p[0:rows, :], weight, None, ALU.mult)
                    if i < 2:
                        settle(scaled)
                        scaled = nc.vector.tensor_scalar(own_new[:, i, :], const(("own_nsa", "own_moba")[i]), p[:, 256:257], None, ALU.mult)
                    scaled.then_inc(d_prob, 1)
                dve.wait_ge(d_turned, 1)
                for k in range(2):
                    nc.vector.tensor_copy(pT_nsa[:, k, 0:P], banks[:, 0, P * k:P * k + P]).then_inc(d_kept, 1)
                nc.vector.tensor_copy(pT_new[0:8, 0:P], banks[0:8, 0, 256:384]).then_inc(d_kept, 1)
                dve.wait_ge(pv_done, DB)
                nc.vector.tensor_copy(o_nsa.rearrange("p a b -> p (a b)"), banks[:, 6, 0:256]).then_inc(o_out, 1)
                dve.wait_ge(o_turned, 1)
                for g in range(2):
                    half = slice(64 * g, 64 * g + 64)
                    src = banks[half, 0, 0:256].rearrange("p (b x) -> p b x", x=32)[:, :, 4 * g:4 * g + 4]
                    nc.vector.tensor_copy(oaT[half, :, SEQ:TOK].rearrange("p j b -> p b j"), src).then_inc(o_kept, 1)

        units = [("moba", j, 0) for j in range(4)] + [("nsa", j, i) for j in range(4) for i in range(2)]

        def blocks_of(unit):
            kind, j, i = unit
            if kind == "moba":
                return [(0, kbT[:, j, :], P, 0), (1, kbT[:, j, :], 2 * P, P)]
            n = P * (i + 1)
            return [(i, ksT, n, 0), (i, kwT, n, n)]

        prob = [[at(k_at + 1024 * a + 512 * x, 512) for x in range(2)] for a in range(2)]
        probT = [[at(k_at + 2048 + 1024 * a + 512 * x, 512) for x in range(2)] for a in range(2)]
        cmp_s, cmp_p, cmp_pT = at(d_at, 2, 2, 60), at(d_at + 240, 2, 2, P), at(d_at + 752, 4, P)
        cmp_min, cmp_sum = at(d_at + 1264, 4, 4), at(d_at + 1280, 4, 4)
        mins = [at(d_at + 1300 + 4 * a, 4) for a in range(2)]
        sums = [at(d_at + 1310 + 4 * a, 4) for a in range(2)]
        s_done, a_min, a_exp, a_weight, a_scaled, a_turned = (sem("a_" + x) for x in ("s", "min", "exp", "weight", "scaled", "turned"))
        a_kept, a_pv, a_out, cmp_sem, cmp_exp = [sem("a_kept_act"), sem("a_kept_dve")], sem("a_pv"), sem("a_out"), sem("cmp_sem"), sem("cmp_exp")
        cmp_read, cmp_ready, cmp_T, cmp_kept = sem("cmp_read"), sem("cmp_ready"), sem("cmp_T"), sem("cmp_kept")
        with nc.Block() as block:
            @block.tensor
            def _(pe):
                for g in range(2):
                    half = slice(64 * g, 64 * g + 64)
                    for i in range(2):
                        for j in range(4):
                            c = 60 * i + NC * j
                            mm = nc.tensor.matmul(banks[:, 4 + g, c:c + NC], qaT[half, j, P * i:P * i + P], kcT[half, 0:NC], start=True, stop=True)
                mm.then_inc(cmp_sem, 1)
                for step in range(len(units) + 2):
                    if step < len(units):
                        u = step
                        if u >= 2:
                            pe.wait_ge(a_min, 4 * (u - 1))
                        q = (qbT if units[u][0] == "moba" else qaT)[:, units[u][1], :]
                        for i, keys, n, c in blocks_of(units[u]):
                            for x in range(2):
                                half = slice(64 * x, 64 * x + 64)
                                mm = nc.tensor.matmul(banks[:, 2 * (u % 2) + x, c:c + n], q[half, P * i:P * i + P], keys[half, 0:n], start=True, stop=True)
                        mm.then_inc(s_done, 1)
                    if 1 <= step <= len(units):
                        u = step - 1
                        pe.wait_ge(a_scaled, 4 * (u + 1))
                        if u == 0:
                            pe.wait_ge(cmp_read, 4)
                        for x in range(2):
                            if u >= 1:
                                pe.wait_ge(a_kept[x], u)
                            tile = 0
                            for i, _, n, c in blocks_of(units[u]):
                                for k in range(n // P):
                                    mm = nc.tensor.transpose(banks[:, 4 + x, P * tile:P * tile + P], prob[u % 2][x][:, c + P * k:c + P * k + P], ident)
                                    tile += 1
                            mm.then_inc(a_turned, 1)
                    if step == 1:
                        pe.wait_ge(cmp_ready, 1)
                        for n in range(4):
                            mm = nc.tensor.transpose(banks[:, 7, P * n:P * n + P], cmp_p[:, n // 2, n % 2, :], ident)
                        mm.then_inc(cmp_T, 1)
                    if step >= 2:
                        u = step - 2
                        kind, j, i = units[u]
                        out_job = j if kind == "moba" else 4 + j
                        for x in range(2):
                            pe.wait_ge(a_kept[x], u + 1)
                        if out_job >= 2:
                            pe.wait_ge(a_out, out_job - 1)
                        if u == 1:
                            pe.wait_ge(cmp_kept, 1)
                        for x in range(2):
                            rows, tile = slice(64 * x, 64 * x + 64), 0
                            bank = banks[rows, 6 + out_job % 2, :]
                            if kind == "moba":
                                v = v_moba[:, :, P * j + 64 * x:P * j + 64 * x + 64]
                                for i, _, n, _ in blocks_of(units[u]):
                                    for k in range(n // P):
                                        mm = nc.tensor.matmul(bank[:, P * i:P * i + P], v[:, k, :], probT[u % 2][x][:, P * tile:P * tile + P],
                                                              start=(k == 0), stop=(k == n // P - 1))
                                        tile += 1
                            else:
                                for br, v in enumerate((v_sel, v_win)):
                                    for k in range(i + 1):
                                        nc.tensor.matmul(bank[:, P * i:P * i + P], v[:, k, 64 * x:64 * x + 64], probT[u % 2][x][:, P * tile:P * tile + P],
                                                         start=(tile == 0), stop=False)
                                        tile += 1
                                mm = nc.tensor.matmul(bank[:, P * i:P * i + P], vcZ[:, j, 64 * x:64 * x + 64], cmp_pT[:, 2 * x + i, :], start=False, stop=True)
                        mm.then_inc(a_pv, 1)

            def keep(eng, copy, x, u):
                eng.wait_ge(a_turned, 2 * u + x + 1)
                if u >= 2:
                    eng.wait_ge(a_pv, u - 1)
                n = sum(b[2] for b in blocks_of(units[u]))
                copy(probT[u % 2][x][:, 0:n], banks[:, 4 + x, 0:n]).then_inc(a_kept[x], 1)

            @block.scalar
            def _(act):
                for step in range(len(units) + 1):
                    if step < len(units):
                        u = step
                        for x in range(2):
                            for k, (i, _, n, c) in enumerate(blocks_of(units[u])):
                                act.wait_ge(a_min, 4 * u + 2 * x + k + 1)
                                s = prob[u % 2][x][:, c:c + n]
                                nc.scalar.activation(s, s, ACT.Exp, scale=-1.0, bias=mins[u % 2][:, 2 * x + k:2 * x + k + 1],
                                                     accum_out=sums[u % 2][:, 2 * x + k:2 * x + k + 1]).then_inc(a_exp, 1)
                    if step == 0:
                        act.wait_ge(cmp_exp, 1)
                        flat = cmp_s.rearrange("p a b c -> p (a b c)")
                        nc.scalar.activation(flat, flat, ACT.Exp, scale=-1.0).then_inc(cmp_exp, 1)
                    if step >= 1:
                        keep(act, nc.scalar.copy, 0, step - 1)

            @block.gpsimd
            def _(pool):
                nc.gpsimd.memset(cmp_p, 0.0).then_inc(cmp_exp, 1)
                for u in range(len(units)):
                    pool.wait_ge(a_weight, u + 1)
                    for x in range(2):
                        for k, (i, _, n, c) in enumerate(blocks_of(units[u])):
                            s = prob[u % 2][x][:, c:c + n]
                            nc.gpsimd.tensor_scalar(s, s, sums[u % 2][:, 2 * x + k:2 * x + k + 1], None, ALU.mult).then_inc(a_scaled, 1)

            @block.vector
            def _(dve):
                def compressed():
                    dve.wait_ge(cmp_sem, 1)
                    for g in range(2):
                        for i in range(2):
                            nc.vector.tensor_tensor(cmp_s[:, g, i, :].rearrange("p (j c) -> p j c", c=NC), banks[:, 4 + g, 60 * i:60 * i + 60].rearrange("p (j c) -> p j c", c=NC),
                                                    const("cmp_out")[:, i, :].unsqueeze(1).broadcast_to([P, 4, NC]), ALU.add).then_inc(cmp_read, 1)
                    dve.wait_ge(cmp_read, 4)
                    s = cmp_s.rearrange("p a b (j c) -> p (a b) j c", c=NC)
                    settle(nc.vector.tensor_reduce(cmp_min, s, X, ALU.min))
                    nc.vector.tensor_tensor(s, s, cmp_min.unsqueeze(3).broadcast_to([P, 4, 4, NC]), ALU.subtract).then_inc(cmp_exp, 1)

                def compressed_rest():
                    s = cmp_s.rearrange("p a b (j c) -> p (a b) j c", c=NC)
                    dve.wait_ge(cmp_exp, 3)
                    for i in range(2):
                        v = cmp_s[:, :, i, :].rearrange("p g (j c) -> p g j c", c=NC)
                        last = nc.vector.tensor_tensor(v, v, const("cmp_in")[:, i, :].unsqueeze(1).unsqueeze(1).broadcast_to([P, 2, 4, NC]), ALU.mult)
                    settle(last)
                    settle(nc.vector.tensor_reduce(cmp_sum, s, X, ALU.add))
                    flat = cmp_sum.rearrange("p a b -> p (a b)")
                    settle(nc.vector.tensor_scalar(flat, flat, 1e-30, None, ALU.max))
                    settle(nc.vector.reciprocal(flat, flat))
                    gates = sig_nsa.rearrange("p t (g j c) -> p t g j c", g=2, j=4)
                    for g in range(2):
                        last = nc.vector.tensor_tensor(cmp_sum[:, 2 * g:2 * g + 2, :], cmp_sum[:, 2 * g:2 * g + 2, :], gates[:, 0:2, g, :, 0], ALU.mult)
                    settle(last)
                    for g in range(2):
                        for i in range(2):
                            last = nc.vector.tensor_tensor(cmp_p[:, g, i, :].rearrange("p (j c) -> p j c", c=32)[:, :, 0:NC], cmp_s[:, g, i, :].rearrange("p (j c) -> p j c", c=NC),
                                                           cmp_sum[:, 2 * g + i, :].unsqueeze(2).broadcast_to([P, 4, NC]), ALU.mult)
                    last.then_inc(cmp_ready, 1)
                    dve.wait_ge(cmp_T, 1)
                    nc.vector.tensor_copy(cmp_pT.rearrange("p a b -> p (a b)"), banks[:, 7, :]).then_inc(cmp_kept, 1)

                compressed()
                for step in range(len(units) + 2):
                    if step < len(units):
                        u = step
                        dve.wait_ge(s_done, u + 1)
                        if u >= 2:
                            dve.wait_ge(a_turned, 2 * (u - 1))
                        for x in range(2):
                            for k, (i, _, n, c) in enumerate(blocks_of(units[u])):
                                nc.vector.tensor_tensor_reduce(prob[u % 2][x][:, c:c + n], banks[:, 2 * (u % 2) + x, c:c + n], causal[:, 2 * P - n:2 * P],
                                                               1.0, 3e38, ALU.add, ALU.min, mins[u % 2][:, 2 * x + k:2 * x + k + 1]).then_inc(a_min, 1)
                    if step >= 1 and step <= len(units):
                        keep(dve, nc.vector.tensor_copy, 1, step - 1)
                    if step >= 2:
                        kind, j, i = units[step - 2]
                        if kind == "moba" or i == 1:
                            out_job = j if kind == "moba" else 4 + j
                            dve.wait_ge(a_pv, step - 1)
                            nc.vector.tensor_copy((obT if kind == "moba" else oaT)[:, j, 0:SEQ], banks[:, 6 + out_job % 2, 0:SEQ]).then_inc(a_out, 1)
                    if step < len(units):
                        u = step
                        dve.wait_ge(a_exp, 4 * (u + 1))
                        kind, j, i = units[u]
                        if kind == "moba":
                            nc.vector.reciprocal(sums[u % 2], sums[u % 2]).then_inc(a_weight, 1)
                        else:
                            settle(nc.vector.reciprocal(sums[u % 2], sums[u % 2]))
                            w = sums[u % 2].rearrange("p (g k) -> p g k", g=2)
                            gates = sig_nsa[:, i, :].rearrange("p (g j c) -> p g j c", g=2, j=4)[:, :, j, 1:3]
                            nc.vector.tensor_tensor(w, w, gates, ALU.mult).then_inc(a_weight, 1)
                    if step == 0:
                        compressed_rest()
        g_done, g_sig, up_done, up_scaled, merged, out_done, out_added, x_in = (sem("m_" + x) for x in ("g", "sig", "up", "scaled", "merged", "out", "added", "x"))
        sig = at(d_at, 16, TOK)
        h = at(blk_at, NT, D)
        EXPERT0 = N_DENSE

        def expert_slot(s):
            return (EXPERT0 + s) % RING

        def load_expert_slot(eng, e, s):
            if s < 4:
                src = t["w_gu"][e].rearrange("(c p) n -> p c n", p=P)[:, 2 * s:2 * s + 2, :]
                dst = ring[:, expert_slot(s), :].rearrange("p (c n) -> p c n", c=2)
            else:
                src = t["w_down"][e].rearrange("(c p) n -> p c n", p=P)[:, 4 * (s - 4):4 * (s - 4) + 4, :]
                dst = ring[:, expert_slot(s), :].rearrange("p (c n) -> p c n", c=4)
            eng.dma_start(dst, src).then_inc(ring_in[expert_slot(s)], 16)

        with nc.Block() as block:
            @block.sync
            def _(sp):
                sp.dma_start(h[:, 0:2, :], t["x_prompt"].rearrange("a (t p) d -> p (a t) d", p=P)).then_inc(x_in, 16)
                sp.dma_start(h[0:DB, 2, :], t["x_sample"].rearrange("a b d -> (a b) d")).then_inc(x_in, 16)
                for n in range(8, N_DENSE):
                    if n < 12:
                        sp.wait_ge(g_done, 4 * (n - 7))
                    elif n < 14:
                        sp.wait_ge(up_done, 16)
                    else:
                        sp.wait_ge(out_done, n - 13)
                    if n + RING < N_DENSE:
                        load_item(sp, n + RING)
                    else:
                        load_expert_slot(sp, 0, n + RING - N_DENSE)

            @block.tensor
            def _(pe):
                for f in range(16):
                    if f % 4 == 0:
                        pe.wait_ge(ring_in[(8 + f // 4) % RING], landed[8 + f // 4])
                    if f >= 4:
                        pe.wait_ge(g_sig, f - 3)
                    w = slot(8 + f // 4, KC)
                    for c in range(KC):
                        mm = nc.tensor.matmul(banks[:, f % 4, 0:TOK], w[:, c, P * (f % 4):P * (f % 4) + P], xnT[:, c, :], start=(c == 0), stop=(c == KC - 1))
                    mm.then_inc(g_done, 1)
                for m in range(KC):
                    for x, o in enumerate((oaT, obT)):
                        if m == 0:
                            pe.wait_ge(ring_in[(12 + x) % RING], landed[12 + x])
                        if m >= 2:
                            pe.wait_ge(up_scaled, 2 * (m - 2) + x + 1)
                        w = slot(12 + x, 4)
                        for j in range(4):
                            mm = nc.tensor.matmul(banks[:, 4 + 2 * (m % 2) + x, 0:TOK], w[:, j, P * m:P * m + P], o[:, j, :], start=(j == 0), stop=(j == 3))
                        mm.then_inc(up_done, 1)
                pe.wait_ge(up_scaled, 16)
                for c in range(KC):
                    if c % 4 == 0:
                        pe.wait_ge(ring_in[(14 + c // 4) % RING], landed[14 + c // 4])
                    pe.wait_ge(merged, c + 1)
                    w = slot(14 + c // 4, 4)
                    for i in range(2):
                        for n in range(2):
                            nc.tensor.matmul(banks[:, 2 * i + n, :], sig[:, c, P * i:P * i + P], w[:, c % 4, 512 * n:512 * n + 512], start=(c == 0), stop=(c == KC - 1))
                    for j in range(4):
                        mm = nc.tensor.matmul(banks[32 * j:32 * j + DB, 4, 0:256], sig[:, c, SEQ:TOK], w[:, c % 4, 256 * j:256 * j + 256],
                                              start=(c == 0), stop=(c == KC - 1), tile_position=(0, 32 * j))
                    if c % 4 == 3:
                        mm.then_inc(out_done, 1)

            @block.scalar
            def _(act):
                for f in range(16):
                    act.wait_ge(g_done, f + 1)
                    nc.scalar.activation(sig[:, f, :], banks[:, f % 4, 0:TOK], ACT.Sigmoid).then_inc(g_sig, 1)

            @block.gpsimd
            def _(pool):
                for m in range(KC):
                    pool.wait_ge(up_scaled, 2 * m + 2)
                    nc.gpsimd.tensor_tensor(sig[:, m, :], sig[:, m, :], sig[:, 8 + m, :], ALU.add).then_inc(merged, 1)

            @block.vector
            def _(dve):
                dve.wait_ge(g_sig, 16)
                for m in range(KC):
                    for x in range(2):
                        dve.wait_ge(up_done, 2 * m + x + 1)
                        s = sig[:, 8 * x + m, :]
                        nc.vector.tensor_tensor(s, banks[:, 4 + 2 * (m % 2) + x, 0:TOK], s, ALU.mult).then_inc(up_scaled, 1)
                dve.wait_ge(x_in, 32)
                dve.wait_ge(out_done, 2)
                for i in range(2):
                    for n in range(2):
                        v = h[:, i, 512 * n:512 * n + 512]
                        nc.vector.tensor_tensor(v, banks[:, 2 * i + n, :], v, ALU.add).then_inc(out_added, 1)
                for j in range(4):
                    nc.vector.tensor_copy(at(k_at, D)[0:DB, 256 * j:256 * j + 256], banks[32 * j:32 * j + DB, 4, 0:256]).then_inc(out_added, 1)
                dve.wait_ge(out_added, 8)
                nc.vector.tensor_tensor(h[0:DB, 2, :], h[0:DB, 2, :], at(k_at, D)[0:DB, :], ALU.add).then_inc(out_added, 1)

        m_at = blk_at + 3 * 1536
        xn2 = at(m_at, NT, D)
        norm_phase("n2_", h, xn2, at(k_at, D), at(k_at + D, D), False)

        e_at = [m_at + 3072]

        def etake(*dims):
            if e_at[0] < out_at and e_at[0] + int(np.prod(dims)) > out_at - 64:
                e_at[0] = out_at
            v = at(e_at[0], *dims)
            e_at[0] += int(np.prod(dims))
            return v

        w_router, b_router = etake(KC, NEXP), etake(NEXP)
        logits, top8, top_f, gate4 = etake(NT, NEXP), etake(NT, 8), etake(NT, 8), etake(NT, 8)
        top_i = etake(NT, 8).bitcast(U32)
        chosen, weight, rank = etake(NT, NEXP), etake(NT, NEXP), etake(NT, NEXP)
        hits = etake(2, TOPK, NEXP)
        many = etake(NT, P)
        over, over_hot, over_i, over_base = etake(4), etake(16), etake(36).bitcast(I32), etake(16)
        b_gu, b_down = etake(2 * D), etake(D)
        acc = etake(KC, TOK)
        r_in, r_done, r_exp, r_counted, r_ready, r_listed, r_max = (sem("r_" + x) for x in ("in", "done", "exp", "counted", "ready", "listed", "max"))
        with nc.Block() as block:
            @block.sync
            def _(sp):
                sp.dma_start(w_router, t["w_router"].rearrange("(c p) n -> p c n", p=P)).then_inc(r_in, 16)
                sp.dma_start(b_router[0:1, :], t["b_router"].unsqueeze(0)).then_inc(r_in, 16)
                sp.dma_start(b_gu[0:NEXP, :], t["b_gu"]).then_inc(r_in, 16)
                sp.dma_start(b_down[0:NEXP, :], t["b_down"]).then_inc(r_in, 16)

            @block.tensor
            def _(pe):
                pe.wait_ge(r_in, 64)
                for i in range(NT):
                    r = ROWS[i]
                    for c in range(KC):
                        nc.tensor.matmul(banks[0:r, 5 + i, 0:NEXP], xnT[:, c, P * i:P * i + r], w_router[:, c, :], start=(c == 0), stop=False)
                    nc.tensor.matmul(banks[0:r, 5 + i, 0:NEXP], ones[0:1, 0:r], b_router[0:1, :], start=False, stop=True).then_inc(r_done, 1)
                pe.wait_ge(r_counted, 1)
                for i in range(NT):
                    for k in range(i + 1):
                        mm = nc.tensor.matmul(banks[:, 1, NEXP * i:NEXP * i + NEXP], const("before") if k == i else ones, chosen[:, k, :], start=(k == 0), stop=(k == i))
                for i in range(NT):
                    mm = nc.tensor.matmul(banks[:, 2, 0:1], many[:, i, :], ones[:, 0:1], start=(i == 0), stop=(i == NT - 1))
                mm.then_inc(r_done, 1)
                pe.wait_ge(r_ready, 1)
                nc.tensor.matmul(banks[:, 3, 0:1], const("before"), over[:, 0:1], start=True, stop=True).then_inc(r_done, 1)
                pe.wait_ge(r_ready, 2)
                nc.tensor.matmul(banks[0:1, 4, 0:16], const("over_expert"), over_hot, start=True, stop=True)
                nc.tensor.matmul(banks[0:1, 4, 16:17], over[:, 0:1], ones[:, 0:1], start=True, stop=True)
                nc.tensor.matmul(banks[:, 5, 0:16], const("over_base"), over_hot, start=True, stop=True).then_inc(r_done, 1)

            @block.scalar
            def _(act):
                for i in range(NT):
                    r = ROWS[i]
                    act.wait_ge(r_max, i + 1)
                    nc.scalar.activation(gate4[0:r, i, 0:4], top8[0:r, i, 0:4], ACT.Exp, bias=gate4[0:r, i, 4:5], accum_out=gate4[0:r, i, 5:6]).then_inc(r_exp, 1)

            @block.vector
            def _(dve):
                nc.vector.memset(acc, 0.0)
                nc.vector.memset(chosen, 0.0)
                settle(nc.vector.memset(weight, 0.0))
                for i in range(NT):
                    r = ROWS[i]
                    dve.wait_ge(r_done, i + 1)
                    settle(nc.vector.tensor_copy(logits[0:r, i, :], banks[0:r, 5 + i, 0:NEXP]))
                    settle(nc.vector.max(top8[0:r, i, :], logits[0:r, i, :]))
                    nc.vector.tensor_scalar(gate4[0:r, i, 4:5], top8[0:r, i, 0:1], -1.0, None, ALU.mult).then_inc(r_max, 1)
                    settle(nc.vector.max_index(top_i[0:r, i, :], top8[0:r, i, :], logits[0:r, i, :]))
                    settle(nc.vector.tensor_copy(top_f[0:r, i, :], top_i[0:r, i, :]))
                    dve.wait_ge(r_exp, i + 1)
                    settle(nc.vector.reciprocal(gate4[0:r, i, 5:6], gate4[0:r, i, 5:6]))
                    settle(nc.vector.tensor_scalar(gate4[0:r, i, 0:4], gate4[0:r, i, 0:4], gate4[0:r, i, 5:6], None, ALU.mult))
                    for k in range(TOPK):
                        iota = const("iota")[0:r, 0:NEXP]
                        nc.vector.tensor_scalar(hits[0:r, 0, k, :], iota, top_f[0:r, i, k:k + 1], None, ALU.is_equal)
                        last = nc.vector.tensor_scalar(hits[0:r, 1, k, :], iota, top_f[0:r, i, k:k + 1], gate4[0:r, i, k:k + 1], ALU.is_equal, ALU.mult)
                    settle(last)
                    nc.vector.tensor_reduce(chosen[0:r, i, :], hits[0:r, 0].rearrange("p k e -> p e k"), X, ALU.add)
                    settle(nc.vector.tensor_reduce(weight[0:r, i, :], hits[0:r, 1].rearrange("p k e -> p e k"), X, ALU.add))
                for i in range(NT):
                    last = nc.vector.tensor_copy(many[:, i, :].rearrange("p (k e) -> p k e", k=4), chosen[:, i, :].unsqueeze(1).broadcast_to([P, 4, NEXP]))
                last.then_inc(r_counted, 1)
                dve.wait_ge(r_done, 4)
                flat = rank.rearrange("p a b -> p (a b)")
                settle(nc.vector.scalar_tensor_tensor(flat, banks[:, 1, 0:NT * NEXP], 1.0, chosen.rearrange("p a b -> p (a b)"), ALU.add, ALU.mult))
                nc.vector.tensor_scalar(flat, flat, -1.0, None, ALU.add)
                nc.vector.tensor_scalar(over[:, 0:1], banks[:, 2, 0:1], const("over_past")[:, 0:1], None, ALU.is_gt).then_inc(r_ready, 1)
                dve.wait_ge(r_done, 5)
                settle(nc.vector.tensor_copy(over[:, 1:2], banks[:, 3, 0:1]))
                nc.vector.tensor_scalar(over_hot, const("iota")[:, 0:16], over[:, 1:2], over[:, 0:1], ALU.is_equal, ALU.mult).then_inc(r_ready, 1)
                dve.wait_ge(r_done, 6)
                nc.vector.tensor_copy(over_i[0:1, 0:17], banks[0:1, 4, 0:17])
                nc.vector.tensor_copy(over_base, banks[:, 5, 0:16]).then_inc(r_listed, 1)

        sel, sel_g, selT = etake(NT, CAP), etake(NT, P), etake(TOK)
        pick, xg, xgT = etake(CAP), etake(512), etake(4, P)
        gate, up, sgm, act_in, aT, y = etake(512), etake(512), etake(512), etake(512), etake(4, P), etake(512)
        past = etake(4)
        half0, half1 = slice(0, 64), slice(64, 128)
        BG, BU, BX, BT, BA, BY, BS = 0, 1, 2, 3, 4, 5, 6

        def expert_sems(tag):
            names = ("sel", "selg", "pick", "gathered", "xkept", "xturned", "xtkept", "gu", "clip", "sigm", "prod", "aturned",
                     "atkept", "ydone", "ykept", "sturned", "stkept", "scat", "added", "used")
            return {n: sem(tag + n) for n in names}

        def wait_past_zero(eng, s, value):
            if not (isinstance(value, int) and value == 0):
                eng.wait_ge(s, value)

        def pe_steps(pe, S, base):
            def gather(e):
                pe.wait_ge(S["sel"], e + 1)
                for x in range(2):
                    for i in range(NT):
                        r = ROWS[i]
                        mm = nc.tensor.matmul(banks[64 * x:64 * x + 64, BX, :], sel[0:r, i, :], xn2[0:r, i, 512 * x:512 * x + 512],
                                              start=(i == 0), stop=(i == NT - 1), tile_position=(0, 64 * x))
                mm.then_inc(S["gathered"], 1)

            def turn_rows(e):
                pe.wait_ge(S["xkept"], e + 1)
                for k in range(4):
                    mm = nc.tensor.transpose(banks[:, BT, P * k:P * k + P], xg[:, P * k:P * k + P], ident)
                mm.then_inc(S["xturned"], 1)

            def scatter(e, k):
                if k == 0:
                    pe.wait_ge(S["ykept"], e + 1)
                    pe.wait_ge(S["stkept"], e + 1)
                wait_past_zero(pe, S["added"], 4 * e + k)
                for x in range(2):
                    rows = slice(64 * x, 64 * x + 64)
                    mm = nc.tensor.matmul(banks[:, BS + x, 0:TOK], y[rows, P * k:P * k + P], selT[rows, :], start=True, stop=True)
                mm.then_inc(S["scat"], 1)

            def gate_up(e, scatter_last):
                pe.wait_ge(S["xtkept"], e + 1)
                pe.wait_ge(S["pick"], e + 1)
                wait_past_zero(pe, S["clip"], 3 * e)
                for b in range(2):
                    for x in range(2):
                        nc.tensor.matmul(banks[64 * x:64 * x + 64, BG + b, :], pick[0:NEXP, :], b_gu[0:NEXP, D * b + 512 * x:D * b + 512 * x + 512],
                                         start=True, stop=False, tile_position=(0, 64 * x))
                for c in range(KC):
                    s = expert_slot(c // 2)
                    if c % 2 == 0:
                        pe.wait_ge(ring_in[s], base(c // 2) + 16 * e + 16)
                    w = ring[:, s, :].rearrange("p (c n) -> p c n", c=2)[:, c % 2, :]
                    for b in range(2):
                        for x in range(2):
                            mm = nc.tensor.matmul(banks[64 * x:64 * x + 64, BG + b, :], xgT[:, c % 4, 64 * (c // 4):64 * (c // 4) + 64],
                                                  w[:, D * b + 512 * x:D * b + 512 * x + 512], start=False, stop=(c == KC - 1), tile_position=(0, 64 * x))
                    if c % 2:
                        mm.then_inc(S["used"] if c < KC - 1 else S["gu"], 1)
                    if scatter_last and c < 4:
                        scatter(e - 1, c)

            def turn_selection(e):
                pe.wait_ge(S["selg"], e + 1)
                for i in range(NT):
                    r = ROWS[i]
                    mm = nc.tensor.transpose(banks[:, BT, P * i:P * i + r], sel_g[0:r, i, :], ident[0:r, 0:r])
                mm.then_inc(S["sturned"], 1)

            def turn_product(e):
                pe.wait_ge(S["prod"], e + 1)
                for k in range(4):
                    mm = nc.tensor.transpose(banks[:, BA, P * k:P * k + P], act_in[:, P * k:P * k + P], ident)
                mm.then_inc(S["aturned"], 1)

            def down(e):
                pe.wait_ge(S["atkept"], e + 1)
                for x in range(2):
                    nc.tensor.matmul(banks[64 * x:64 * x + 64, BY, :], pick[0:NEXP, :], b_down[0:NEXP, 512 * x:512 * x + 512],
                                     start=True, stop=False, tile_position=(0, 64 * x))
                for c in range(KC):
                    s = expert_slot(4 + c // 4)
                    if c % 4 == 0:
                        pe.wait_ge(ring_in[s], base(4 + c // 4) + 16 * e + 16)
                    w = ring[:, s, :].rearrange("p (c n) -> p c n", c=4)[:, c % 4, :]
                    for x in range(2):
                        mm = nc.tensor.matmul(banks[64 * x:64 * x + 64, BY, :], aT[:, c % 4, 64 * (c // 4):64 * (c // 4) + 64],
                                              w[:, 512 * x:512 * x + 512], start=False, stop=(c == KC - 1), tile_position=(0, 64 * x))
                    if c == 3:
                        mm.then_inc(S["used"], 1)
                mm.then_inc(S["ydone"], 1)

            return gather, turn_rows, scatter, gate_up, turn_selection, turn_product, down

        def sp_expert(sp, S, e, done):
            for s in range(6):
                if s == 3:
                    sp.wait_ge(S["gu"], done)
                elif s == 5:
                    sp.wait_ge(S["ydone"], done)
                else:
                    sp.wait_ge(S["used"], 4 * done - 4 + (s + 1 if s < 3 else 4))
                load_expert_slot(sp, e, s)

        def act_rows(act, S, e):
            act.wait_ge(S["gathered"], e + 1)
            nc.scalar.copy(xg, banks[:, BX, :]).then_inc(S["xkept"], 1)

        def act_rowsT(act, S, e):
            act.wait_ge(S["xturned"], e + 1)
            nc.scalar.copy(xgT.rearrange("p a b -> p (a b)"), banks[:, BT, :]).then_inc(S["xtkept"], 1)

        def act_sigmoid(act, S, e):
            act.wait_ge(S["clip"], 3 * e + 1)
            nc.scalar.activation(sgm, gate, ACT.Sigmoid, scale=ALPHA).then_inc(S["sigm"], 1)

        def act_productT(act, S, e):
            act.wait_ge(S["aturned"], e + 1)
            nc.scalar.copy(aT.rearrange("p a b -> p (a b)"), banks[:, BA, :]).then_inc(S["atkept"], 1)

        def act_out(act, S, e):
            act.wait_ge(S["ydone"], e + 1)
            wait_past_zero(act, S["scat"], 4 * e)
            nc.scalar.copy(y, banks[:, BY, :]).then_inc(S["ykept"], 1)

        def dve_select(dve, S, e, position):
            for i in range(NT):
                last = nc.vector.tensor_scalar(sel[:, i, :], const("iota")[:, 0:CAP], position(i), None, ALU.is_equal)
            last.then_inc(S["sel"], 1)

        def dve_gates(dve, S, e, position, share, which):
            for i in range(NT):
                last = nc.vector.tensor_scalar(sel_g[:, i, :], const("slots"), position(i), share(i), ALU.is_equal, ALU.mult)
            last.then_inc(S["selg"], 1)

        def dve_pick(dve, S, e, which):
            nc.vector.tensor_copy(pick[0:NEXP, :], which.broadcast_to([NEXP, CAP])).then_inc(S["pick"], 1)

        def dve_product(dve, S, e):
            dve.wait_ge(S["gu"], e + 1)
            nc.vector.tensor_scalar(gate, banks[:, BG, :], LIMIT, None, ALU.min).then_inc(S["clip"], 1)
            nc.vector.tensor_scalar(up, banks[:, BU, :], LIMIT, -LIMIT, ALU.min, ALU.max).then_inc(S["clip"], 1)
            dve.wait_ge(S["clip"], 3 * e + 2)
            nc.vector.scalar_tensor_tensor(up, up, 1.0, gate, ALU.add, ALU.mult).then_inc(S["clip"], 1)

        def dve_product_end(dve, S, e):
            dve.wait_ge(S["sigm"], e + 1)
            dve.wait_ge(S["clip"], 3 * e + 3)
            nc.vector.tensor_tensor(act_in, up, sgm, ALU.mult).then_inc(S["prod"], 1)

        def dve_selT(dve, S, e):
            dve.wait_ge(S["sturned"], e + 1)
            nc.vector.tensor_copy(selT, banks[:, BT, 0:TOK]).then_inc(S["stkept"], 1)

        def dve_add(dve, S, e, k):
            dve.wait_ge(S["scat"], 4 * e + k + 1)
            v = acc[:, k:k + 5:4, :]
            nc.vector.tensor_tensor(v, banks[:, BS:BS + 2, 0:TOK], v, ALU.add).then_inc(S["added"], 1)

        S = expert_sems("e_")
        first_base = lambda s: dense_count[expert_slot(s)]
        with nc.Block() as block:
            @block.sync
            def _(sp):
                with sp.Fori(1, NEXP) as e:
                    sp_expert(sp, S, e, e)

            @block.tensor
            def _(pe):
                gather, turn_rows, scatter, gate_up, turn_selection, turn_product, down = pe_steps(pe, S, first_base)

                def expert(e, first=False, last=False):
                    gate_up(e, not first)
                    turn_selection(e)
                    if not last:
                        gather(e + 1)
                    turn_product(e)
                    if not last:
                        pe.wait_ge(S["stkept"], e + 1)
                        turn_rows(e + 1)
                    down(e)

                gather(0)
                turn_rows(0)
                expert(0, first=True)
                expert(1)
                with pe.Fori(2, NEXP - 1) as e:
                    expert(e)
                expert(NEXP - 1, last=True)
                for k in range(4):
                    scatter(NEXP - 1, k)

            @block.scalar
            def _(act):
                def expert(e, last=False):
                    if not last:
                        act_rows(act, S, e + 1)
                    act_sigmoid(act, S, e)
                    act_productT(act, S, e)
                    if not last:
                        act_rowsT(act, S, e + 1)
                    act_out(act, S, e)

                act_rows(act, S, 0)
                act_rowsT(act, S, 0)
                expert(0)
                with act.Fori(1, NEXP - 1) as e:
                    expert(e)
                expert(NEXP - 1, last=True)

            @block.vector
            def _(dve):
                position = lambda e: (lambda i: rank[:, i, bass.ds(e, 1)])
                share = lambda e: (lambda i: weight[:, i, bass.ds(e, 1)])

                def expert(e, first=False, last=False):
                    if not first:
                        for k in range(4):
                            dve_add(dve, S, e - 1, k)
                    if not first:
                        dve.wait_ge(S["sturned"], e)
                    dve_gates(dve, S, e, position(e), share(e), None)
                    if not last:
                        dve.wait_ge(S["gathered"], e + 1)
                        dve_select(dve, S, e + 1, position(e + 1))
                    dve_product(dve, S, e)
                    dve_selT(dve, S, e)
                    dve_product_end(dve, S, e)
                    if not last:
                        dve.wait_ge(S["ydone"], e + 1)
                        dve_pick(dve, S, e + 1, ident[0:NEXP, bass.ds(e + 1, 1)])

                dve_select(dve, S, 0, position(0))
                dve_pick(dve, S, 0, ident[0:NEXP, 0:1])
                expert(0, first=True)
                with dve.Fori(1, NEXP - 1) as e:
                    expert(e)
                expert(NEXP - 1, last=True)
                for k in range(4):
                    dve_add(dve, S, NEXP - 1, k)

        MAX_OVER = TOK * TOPK // CAP
        O = expert_sems("o_")
        o_past = sem("o_past")

        def listed(eng):
            return eng.value_load(over_i[0:1, 16:17], min_val=0, max_val=MAX_OVER)

        def listed_expert(eng, k):
            return eng.value_load(over_i[0:1, bass.ds(k, 1)], min_val=0, max_val=NEXP - 1)

        with nc.Block() as block:
            @block.sync
            def _(sp):
                n = listed(sp)

                def item(k):
                    with sp.If(n > k):
                        e = listed_expert(sp, k)
                        wait_past_zero(sp, O["ydone"], k)
                        for s in range(6):
                            if s < 4:
                                src = t["w_gu"][e].rearrange("(c p) n -> p c n", p=P)[:, 2 * s:2 * s + 2, :]
                                dst = ring[:, expert_slot(s), :].rearrange("p (c n) -> p c n", c=2)
                            else:
                                src = t["w_down"][e].rearrange("(c p) n -> p c n", p=P)[:, 4 * (s - 4):4 * (s - 4) + 4, :]
                                dst = ring[:, expert_slot(s), :].rearrange("p (c n) -> p c n", c=4)
                            sp.dma_start(dst, src).then_inc(ring_in[expert_slot(s)], 16)

                item(0)
                with sp.Fori(1, MAX_OVER) as k:
                    item(k)

            @block.tensor
            def _(pe):
                gather, turn_rows, scatter, gate_up, turn_selection, turn_product, down = pe_steps(pe, O, lambda s: first_base(s) + 16 * NEXP)
                n = listed(pe)

                def item(k):
                    with pe.If(n > k):
                        gather(k)
                        turn_rows(k)
                        gate_up(k, False)
                        pe.wait_ge(O["xtkept"], k + 1)
                        turn_selection(k)
                        turn_product(k)
                        down(k)
                        for c in range(4):
                            scatter(k, c)

                item(0)
                with pe.Fori(1, MAX_OVER) as k:
                    item(k)

            @block.scalar
            def _(act):
                n = listed(act)

                def item(k):
                    with act.If(n > k):
                        act_rows(act, O, k)
                        act_rowsT(act, O, k)
                        act_sigmoid(act, O, k)
                        act_productT(act, O, k)
                        act_out(act, O, k)

                item(0)
                with act.Fori(1, MAX_OVER) as k:
                    item(k)

            @block.vector
            def _(dve):
                n = listed(dve)

                def item(k):
                    with dve.If(n > k):
                        e = listed_expert(dve, k)
                        for i in range(NT):
                            last = nc.vector.tensor_scalar(past[:, i:i + 1], rank[:, i, bass.ds(e, 1)], over_base[:, bass.ds(k, 1)], None, ALU.subtract)
                        last.then_inc(o_past, 1)
                        dve.wait_ge(o_past, k + 1)
                        position = lambda i: past[:, i:i + 1]
                        dve_select(dve, O, k, position)
                        dve_pick(dve, O, k, ident[0:NEXP, bass.ds(e, 1)])
                        dve_gates(dve, O, k, position, lambda i: weight[:, i, bass.ds(e, 1)], None)
                        dve_product(dve, O, k)
                        dve_selT(dve, O, k)
                        dve_product_end(dve, O, k)
                        for c in range(4):
                            dve_add(dve, O, k, c)

                item(0)
                with dve.Fori(1, MAX_OVER) as k:
                    item(k)

        f_turned, f_added = sem("f_turned"), sem("f_added")
        with nc.Block() as block:
            @block.tensor
            def _(pe):
                for i in range(NT):
                    r = ROWS[i]
                    for n in range(2):
                        for c in range(4):
                            mm = nc.tensor.transpose(banks[0:r, 2 * i + n, P * c:P * c + P], acc[:, 4 * n + c, P * i:P * i + r], ident)
                        mm.then_inc(f_turned, 1)

            @block.vector
            def _(dve):
                for i in range(NT):
                    r = ROWS[i]
                    for n in range(2):
                        dve.wait_ge(f_turned, 2 * i + n + 1)
                        v = h[0:r, i, 512 * n:512 * n + 512]
                        nc.vector.tensor_tensor(v, banks[0:r, 2 * i + n, :], v, ALU.add).then_inc(f_added, 1)

            @block.sync
            def _(sp):
                for i in range(2):
                    sp.wait_ge(f_added, 2 * i + 2)
                    store(sp, t["y_prompt"][0, P * i:P * i + P, :], h[:, i, :], "y")
                sp.wait_ge(f_added, 6)
                store(sp, t["y_sample"].rearrange("a b d -> (a b) d"), h[0:DB, 2, :], "y")
                for group, s in stored.items():
                    sp.wait_ge(s, store_count[group])


_INPUTS = ["x_prompt", "x_sample", "cache_nsa_cmp_k", "cache_nsa_cmp_v", "cache_nsa_sel_k", "cache_nsa_sel_v",
           "cache_nsa_win_k", "cache_nsa_win_v", "cache_moba_k", "cache_moba_v", "page_table", "norm_attn", "w_in",
           "g_qa", "g_ka", "g_kc", "cmp_pos_k", "cmp_w1_k", "cmp_w2_k", "cmp_pos_v", "cmp_w1_v", "cmp_w2_v", "g_qb",
           "g_kb", "w_up_a", "w_up_b", "w_out", "norm_ffn", "w_router", "b_router", "w_gu", "b_gu", "w_down", "b_down"]
_KV, _KVB = (NSA_G, HD), (MOBA_H, HD)
_OUTPUTS = [("y_prompt", (1, SEQ, D)), ("y_sample", (DB, 1, D))]
for _side, _lead, _win in (("p_", (1, SEQ), (1, SEQ)), ("s_", (DB, 1), (DB, SEQ + 1))):
    _OUTPUTS += [(_side + n, _lead + _KV) for n in ("k_c", "v_c", "k_s", "v_s")]
    _OUTPUTS += [(_side + n, _win + _KV) for n in ("k_w", "v_w")]
    _OUTPUTS += [(_side + n, _lead + _KVB) for n in ("k_b", "v_b")]


def kernel(**inputs):
    import concourse.bacc as _bacc
    from concourse.bass_utils import run_bass_kernel_spmd as _run

    const_at, packed = constants()
    nc = _bacc.Bacc("TRN2", target_bir_lowering=False, num_devices=1)
    arrays, t = {"const": packed}, {}
    for name in _INPUTS:
        arrays[name] = np.ascontiguousarray(inputs[name])
    for name, a in arrays.items():
        t[name] = nc.dram_tensor(name, a.shape, mybir.dt.from_np(a.dtype), kind="ExternalInput").ap()
    for name, shape in _OUTPUTS:
        t[name] = nc.dram_tensor(name, shape, F32, kind="ExternalOutput").ap()
    build(nc, t, const_at, packed.shape[1])
    r = _run(nc, [arrays], core_ids=[0])
    return tuple(r.results[0][name] for name, _ in _OUTPUTS)
```

```python
from contextlib import ExitStack

import numpy as np

import concourse.bass as bass
from concourse import mybir

F32 = mybir.dt.float32
I32 = mybir.dt.int32
BF16 = mybir.dt.bfloat16
U32 = mybir.dt.uint32
ALU = mybir.AluOpType
ACT = mybir.ActivationFunctionType
X = mybir.AxisListType.X

P = 128
D = 1024
KC = D // P
SEQ = 256
DB = 8
TOK = SEQ + DB
NT = 3
ROWS = [P, P, DB]
PAGE = 128
N_PAGES = 2
HD = 64
HALF = HD // 2
NSA_H, NSA_G, GRP = 8, 2, 4
MOBA_H = 8
KVA = NSA_G * HD
NC = 15
CST_R = 16
HID = 256
NEXP, TOPK = 32, 4
CAP = 64
ROUNDS = -(-TOK // CAP)
EPS = 1e-6
BIG = 1e30
LIMIT, ALPHA = 7.0, 1.702
QSCALE = -(HD ** -0.5)
SLOT = 4096
RING = 6
BLOCK_AT = [0, 512, 1024, 1304, 1816, 2328]
BLOCK_W = [512, 512, 280, 512, 512, 512]
GATES_AT = 2840


def constants():
    p = np.arange(P)
    parts = {}
    parts["ident"] = np.eye(P)
    pos = np.zeros((P, NT))
    pos[:, 0], pos[:, 1], pos[:, 2] = p, p + P, SEQ
    half = HD // 2
    inv = (np.float32(10000.0) ** (-np.arange(half, dtype=np.float32) / np.float32(half))).astype(np.float32)
    ang = pos.astype(np.float32)[:, :, None] * inv
    cos, sin = np.cos(ang.astype(np.float32)), np.sin(ang.astype(np.float32))
    parts["cos"] = np.concatenate([cos, cos], -1)
    parts["sin"] = np.concatenate([-sin, sin], -1)
    parts["causal"] = np.concatenate([np.zeros((P, P)), np.where(p[None, :] > p[:, None], BIG, 0.0)], 1)
    valid = (np.arange(NC) * 16 + 31)[None, None, :] <= pos[:, :2, None]
    parts["cmp_out"] = np.where(valid, 0.0, BIG)
    parts["cmp_in"] = np.where(valid, 1.0, 0.0)
    r = p % 64
    b, h, br = r // 8, r % 8, p // 64
    parts["dec_cmp"] = np.where((np.arange(120) // NC)[None, :] == b[:, None], 0.0, BIG)
    hc = np.arange(24)
    parts["gate_sel"] = (hc // 3 == h[:, None]) & (hc % 3 == 1 + br[:, None])
    parts["gate_cmp"] = (hc // 3 == h[:, None]) & (hc % 3 == 0)
    parts["own_nsa"] = np.arange(8)[None, :] == b[:, None]
    q = p % 32
    parts["own_moba"] = (np.arange(8)[None, :] == (q // 2)[:, None]) & (q < 16)[:, None]
    parts["req_rows"] = p[:, None] == b[None, :]
    rz = np.zeros((P, 4, P))
    for j in range(4):
        rz[np.arange(NC), j, 32 * j + np.arange(NC)] = 1.0
    parts["spread"] = rz
    parts["over_expert"] = (p % NEXP)[:, None]
    parts["over_base"] = np.broadcast_to((CAP * (p // NEXP + 1))[:, None], (P, P))
    parts["over_past"] = (CAP * (p // NEXP + 1))[:, None]
    parts["slot"] = (p % CAP)[:, None]
    parts["expert_of"] = (p % NEXP)[:, None] == np.arange(NEXP)[None, :]
    parts["less_first"] = -1.0 * (p >= 32)[:, None]
    parts["less_second"] = -1.0 * (p >= 64)[:, None]
    parts["before"] = p[:, None] < p[None, :]
    parts["ones"] = np.ones((P, P))
    parts["iota"] = np.broadcast_to(np.arange(P)[None, :], (P, P))
    at, cols = {}, 0
    for name, a in parts.items():
        n = int(np.prod(a.shape[1:]))
        at[name] = (cols, a.shape[1:])
        cols += n
    packed = np.concatenate([np.asarray(a, np.float32).reshape(P, -1) for a in parts.values()], 1)
    return at, np.ascontiguousarray(packed, dtype=np.float32)


def build(nc, t, const_at, const_w):
    ctx = ExitStack()
    with ctx:
        total = 53200
        arena = ctx.enter_context(nc.sbuf_tensor("arena", [P, total], F32))
        banks = ctx.enter_context(nc.psum_tensor("banks", [P, 8, 512], F32))

        def sem(name):
            return ctx.enter_context(nc.semaphore(name))

        dve_chain, chained = sem("dve_chain"), [0]

        def settle(ins):
            ins.then_inc(dve_chain, 1)
            chained[0] += 1
            nc.vector.wait_ge(dve_chain, chained[0])

        taken = [0]

        def at(offset, *dims):
            n = int(np.prod(dims))
            assert offset + n <= total, (offset, n)
            v = arena[:, offset:offset + n]
            if len(dims) == 1:
                return v
            names = "abcd"[:len(dims)]
            return v.rearrange(f"p ({' '.join(names)}) -> p {' '.join(names)}",
                               **{k: d for k, d in zip(names[1:], dims[1:])})

        def take(*dims):
            offset = taken[0]
            taken[0] += int(np.prod(dims))
            return at(offset, *dims)

        def region(n):
            offset = taken[0]
            taken[0] += n
            return offset

        ring = take(RING, SLOT)
        cst = take(const_w)
        moe_at = taken[0]
        xnT = take(KC, TOK)
        blk_at = region(2 * 1536 + 1536)
        v_sel, v_win = take(NT, KVA), take(NT, KVA)
        v_moba = take(NT, 512)
        g_nsa = take(NT, 24)
        qaT, qbT, kbT = take(4, TOK), take(4, TOK), take(4, TOK)
        ksT, kwT = take(TOK), take(TOK)
        kcT = take(NC + 120)
        small = take(64)
        out_at = region(2 * 4 * TOK)
        k_at = region(19 * P * 2)
        d_at = region(2 * 9 * 256 + 2 * 540)
        assert taken[0] <= total, taken[0]

        def const(name):
            c, shape = const_at[name]
            v = cst[:, c:c + int(np.prod(shape))]
            if len(shape) == 2:
                v = v.rearrange("p (a b) -> p a b", b=shape[1])
            return v

        ident, cos, sin = const("ident"), const("cos"), const("sin")
        causal, ones = const("causal"), const("ones")

        w_in = t["w_in"].rearrange("(c p) n -> p c n", p=P)

        def proj_item(a, w):
            return lambda s: (ring[:, s, 0:KC * w].rearrange("p (c n) -> p c n", c=KC), w_in[:, :, a:a + w])

        def rows_item(src, chunks, width):
            view = src.rearrange("(c p) n -> p c n", p=P)
            return lambda s: (ring[:, s, 0:chunks * width].rearrange("p (c n) -> p c n", c=chunks), view)

        items = [proj_item(a, w) for a, w in zip(BLOCK_AT, BLOCK_W)]
        items += [rows_item(t["cmp_w1_k"], 16, HID), rows_item(t["cmp_w1_v"], 16, HID)]
        items += [proj_item(GATES_AT + 512 * i, 512) for i in range(4)]
        up_a = t["w_up_a"].rearrange("(g j d) n -> g d j n", g=NSA_G, j=GRP)
        items += ["up_a", rows_item(t["w_up_b"], 4, D)]
        items += [rows_item(t["w_out"][512 * i:512 * i + 512], 4, D) for i in range(2)]
        N_DENSE = len(items)
        ring_in = [sem(f"ring_in{s}") for s in range(RING)]
        ring_count = [0] * RING
        landed = {}

        def load_item(eng, n):
            s = n % RING
            if items[n] == "up_a":
                for g in range(NSA_G):
                    dst = ring[64 * g:64 * g + 64, s, :].rearrange("p (c n) -> p c n", c=4)
                    eng.dma_start(dst, up_a[g]).then_inc(ring_in[s], 16)
                ring_count[s] += 32
            else:
                dst, src = items[n](s)
                eng.dma_start(dst, src).then_inc(ring_in[s], 16)
                ring_count[s] += 16
            landed[n] = ring_count[s]

        def slot(n, chunks):
            width = SLOT // chunks
            return ring[:, n % RING, 0:chunks * width].rearrange("p (c n) -> p c n", c=chunks)

        def promise():
            count = [0] * RING
            for n, item in enumerate(items):
                count[n % RING] += 32 if item == "up_a" else 16
                landed[n] = count[n % RING]
            return count
        dense_count = promise()

        const_in, rows_in, vec_in = sem("const_in"), sem("rows_in"), sem("vec_in")
        pages_in, ffn_gain_in = sem("pages_in"), sem("ffn_gain_in")
        stored, store_count = {}, {}

        def store(eng, dst, src, group):
            if group not in stored:
                stored[group], store_count[group] = sem(f"stored_{group}"), 0
            eng.dma_start(dst, src).then_inc(stored[group], 16)
            store_count[group] += 16

        def norm_phase(tag, src, dst, gain, scratch, first):
            sq_done, mean_done, root_done = sem(tag + "sq"), sem(tag + "mean"), sem(tag + "root")
            scaled = sem(tag + "scaled")
            turned, copied = sem(tag + "turned"), sem(tag + "copied")
            sumsq, rstd = small[:, 0:3], small[:, 4:7]
            cleared = sem(tag + "cleared") if first else None
            with nc.Block() as block:
                @block.sync
                def _(sp):
                    if not first:
                        sp.dma_start(gain, t["norm_ffn"].partition_broadcast(P)).then_inc(ffn_gain_in, 16)
                    if first:
                        sp.wait_ge(cleared, 1)
                        sp.dma_start(src[:, 0:2, :], t["x_prompt"].rearrange("a (t p) d -> p (a t) d", p=P)).then_inc(rows_in, 16)
                        sp.dma_start(src[0:DB, 2, :], t["x_sample"].rearrange("a b d -> (a b) d")).then_inc(rows_in, 16)
                        sp.dma_start(gain, t["norm_attn"].partition_broadcast(P)).then_inc(vec_in, 16)
                        sp.dma_start(cst, t["const"]).then_inc(const_in, 16)
                        for i, v in enumerate([t["g_qa"], t["g_ka"][0], t["g_ka"][1], t["g_ka"][2], t["g_qb"], t["g_kb"], t["g_kc"]]):
                            sp.dma_start(head_gain[:, i, :], v.partition_broadcast(P)).then_inc(vec_in, 16)
                        for n in range(RING):
                            load_item(sp, n)

                @block.scalar
                def _(act):
                    if first:
                        act.wait_ge(rows_in, 32)
                    for i in range(NT):
                        nc.scalar.activation(scratch, src[:, i, :], ACT.Square, accum_out=sumsq[:, i:i + 1]).then_inc(sq_done, 1)
                        act.wait_ge(sq_done, i + 1)
                    act.wait_ge(mean_done, 1)
                    nc.scalar.activation(rstd, rstd, ACT.Sqrt).then_inc(root_done, 1)
                    for c in range(1, KC, 2):
                        act.wait_ge(turned, c + 1)
                        nc.scalar.copy(xnT[:, c, :], banks[:, c, 0:TOK]).then_inc(copied, 1)

                @block.vector
                def _(dve):
                    if first:
                        nc.vector.memset(src[:, 2, :], 0.0).then_inc(cleared, 1)
                        dve.wait_ge(vec_in, 16 * 8)
                    else:
                        dve.wait_ge(ffn_gain_in, 16)
                    dve.wait_ge(sq_done, NT)
                    nc.vector.tensor_scalar(rstd, sumsq, 1.0 / D, EPS, ALU.mult, ALU.add).then_inc(mean_done, 1)
                    dve.wait_ge(root_done, 1)
                    settle(nc.vector.reciprocal(rstd, rstd))
                    if not first:
                        settle(nc.vector.memset(dst[:, 2, :], 0.0))
                    for i in range(NT):
                        r = P if first else ROWS[i]
                        nc.vector.scalar_tensor_tensor(dst[0:r, i, :], src[0:r, i, :], rstd[0:r, i:i + 1], gain[0:r, :], ALU.mult, ALU.mult).then_inc(scaled, 1)
                    if first:
                        for i in (0, 4):
                            settle(nc.vector.tensor_scalar(head_gain[:, i, :], head_gain[:, i, :], QSCALE, None, ALU.mult))
                    for c in range(0, KC, 2):
                        dve.wait_ge(turned, c + 1)
                        nc.vector.tensor_copy(xnT[:, c, :], banks[:, c, 0:TOK]).then_inc(copied, 1)

                @block.tensor
                def _(pe):
                    if first:
                        pe.wait_ge(const_in, 16)
                    pe.wait_ge(scaled, NT)
                    for c in range(KC):
                        for i in range(NT):
                            r = ROWS[i]
                            mm = nc.tensor.transpose(banks[:, c, P * i:P * i + r], dst[0:r, i, P * c:P * c + P], ident[0:r, 0:r])
                        mm.then_inc(turned, 1)

        head_gain = at(out_at, 7, HD)
        x_at = k_at
        norm_phase("n1_", at(x_at, NT, D), at(x_at, NT, D), at(d_at, D), at(d_at + D, D), True)

        proj_done, proj_evac, sq_done, ss_done = sem("proj_done"), sem("proj_evac"), sem("p_sq"), sem("p_ss")
        ms_done, root_done, rope_done, v_copied = sem("p_ms"), sem("p_root"), sem("p_rope"), sem("p_vcopied")
        p_turned, p_copied = sem("p_turned"), sem("p_copied")
        cache_in, rows_cleared = sem("cache_in"), sem("rows_cleared")
        raw = [at(blk_at + 1536 * i, NT, 512) for i in range(2)]
        squares, xcos, xsin = at(blk_at + 3072, 1536), at(k_at, 1536), at(k_at + 1536, 1536)
        head_ss = at(k_at + 3072, 24)
        segs = [(0, 0, 8, 0), (1, 0, 2, 1), (1, 256, 2, 2), (2, 0, 2, 3), (3, 0, 8, 4), (4, 0, 8, 5)]
        turns = {
            0: [(qaT[:, j, :], P * j) for j in range(4)],
            1: [(ksT, 256)],
            2: [(kwT, 0)],
            3: [(qbT[:, j, :], P * j) for j in range(4)],
            4: [(kbT[:, j, :], P * j) for j in range(4)],
        }
        turns_before = [0, 4, 5, 6, 10, 14]
        stores = {1: [("k_c", 0, KVA), ("v_c", 128, KVA), ("k_s", 256, KVA), ("v_s", 384, KVA)],
                  2: [("k_w", 0, KVA), ("v_w", 128, KVA)],
                  4: [("k_b", 0, 512)], 5: [("v_b", 0, 512)]}
        for n in stores:
            stored[n], store_count[n] = sem(f"stored_{n}"), 0
        cmp_rows = [at(d_at + 2304 * i, 9, NSA_G, 2 * HD).rearrange("p s g (two d) -> p s g two d", two=2) for i in range(2)]

        with nc.Block() as block:
            @block.sync
            def _(sp):
                pages = at(k_at + 3100, 16).bitcast(I32)
                sp.dma_start(pages[0:1, :], t["page_table"].rearrange("a b -> (a b)").unsqueeze(0)).then_inc(pages_in, 16)
                sp.wait_ge(pages_in, 16)
                for b in range(DB):
                    for g in range(N_PAGES):
                        page = sp.value_load(pages[0:1, 2 * b + g:2 * b + g + 1], min_val=0, max_val=t["cache_nsa_cmp_k"].shape[0] - 1)
                        for kv, name in enumerate(("cache_nsa_cmp_k", "cache_nsa_cmp_v")):
                            for group in range(NSA_G):
                                sp.dma_start(cmp_rows[kv][64 * g:64 * g + 64, 1 + b, group],
                                             t[name][page].rearrange("(p two) g d -> p g two d", two=2)[:, group]).then_inc(cache_in, 16)
                for n in range(6):
                    sp.wait_ge(proj_done, 3 * (n + 1))
                    load_item(sp, n + RING)
                    if n in stores:
                        sp.wait_ge(rope_done, n + 1) if n < 5 else sp.wait_ge(proj_evac, 36)
                        for name, c, w in stores[n]:
                            p_out, s_out = t["p_" + name], t["s_" + name]
                            store(sp, p_out.rearrange("a (t p) h d -> p (a t) (h d)", p=P), raw[n % 2][:, 0:2, c:c + w], n)
                            dst = s_out.rearrange("a b h d -> (a b) (h d)") if name not in ("k_w", "v_w") else None
                            if name in ("k_w", "v_w"):
                                dst = s_out[:, SEQ, :, :].rearrange("a h d -> a (h d)")
                            store(sp, dst, raw[n % 2][0:DB, 2, c:c + w], n)
                for name, src in (("s_k_w", "cache_nsa_win_k"), ("s_v_w", "cache_nsa_win_v")):
                    store(sp, t[name][:, 0:SEQ].rearrange("b s h d -> b (s h d)"), t[src].rearrange("b s h d -> b (s h d)"), "windows")

            @block.tensor
            def _(pe):
                def project(n):
                    w = BLOCK_W[n]
                    weights = ring[:, n % RING, 0:KC * w].rearrange("p (c n) -> p c n", c=KC)
                    pe.wait_ge(ring_in[n % RING], landed[n])
                    if n >= 2:
                        pe.wait_ge(proj_evac, 6 * (n - 1))
                    for i in range(2):
                        for c in range(KC):
                            mm = nc.tensor.matmul(banks[:, 2 * (n % 2) + i, 0:w], xnT[:, c, P * i:P * i + P], weights[:, c, :],
                                                  start=(c == 0), stop=(c == KC - 1))
                        mm.then_inc(proj_done, 1)
                    q = w // 4
                    for c in range(KC):
                        for j in range(4):
                            mm = nc.tensor.matmul(banks[32 * j:32 * j + DB, 4 + n % 2, 0:q], xnT[:, c, SEQ:TOK],
                                                  weights[:, c, q * j:q * j + q], start=(c == 0), stop=(c == KC - 1),
                                                  tile_position=(0, 32 * j))
                    mm.then_inc(proj_done, 1)

                def turn(n):
                    pe.wait_ge(rope_done, n + 1)
                    for k, (_, c0) in enumerate(turns[n]):
                        job = turns_before[n] + k
                        if job >= 2:
                            pe.wait_ge(p_copied, job - 1)
                        for i in range(NT):
                            r = ROWS[i]
                            mm = nc.tensor.transpose(banks[:, 6 + job % 2, P * i:P * i + r], raw[n % 2][0:r, i, c0:c0 + P], ident[0:r, 0:r])
                        mm.then_inc(p_turned, 1)

                for n in range(6):
                    project(n)
                    if n >= 1:
                        turn(n - 1)

            @block.scalar
            def _(act):
                def evacuate(n):
                    w = BLOCK_W[n]
                    q = w // 4
                    if n >= 2:
                        act.wait_ge(p_turned, turns_before[n - 1])
                        act.wait_ge(v_copied, [0, 0, 0, 1, 3, 3][n])
                        if n - 2 in stores:
                            act.wait_ge(stored[n - 2], 32 * len(stores[n - 2]))
                    for i in range(2):
                        act.wait_ge(proj_done, 3 * n + i + 1)
                        nc.scalar.copy(raw[n % 2][:, i, 0:w], banks[:, 2 * (n % 2) + i, 0:w]).then_inc(proj_evac, 1)
                    act.wait_ge(proj_done, 3 * n + 3)
                    for j in range(4):
                        nc.scalar.copy(raw[n % 2][0:DB, 2, q * j:q * j + q], banks[32 * j:32 * j + DB, 4 + n % 2, 0:q]).then_inc(proj_evac, 1)

                def roots(s):
                    nh = segs[s][2]
                    act.wait_ge(ms_done, s + 1)
                    nc.scalar.activation(head_ss[:, 0:NT * nh], head_ss[:, 0:NT * nh], ACT.Sqrt).then_inc(root_done, 1)

                def copies(n):
                    for k, (dst, _) in enumerate(turns[n]):
                        job = turns_before[n] + k
                        act.wait_ge(p_turned, job + 1)
                        nc.scalar.copy(dst, banks[:, 6 + job % 2, 0:TOK]).then_inc(p_copied, 1)

                act.wait_ge(rows_cleared, 2)
                evacuate(0)
                roots(0)
                evacuate(1)
                for n in range(1, 6):
                    for s, seg in enumerate(segs):
                        if seg[0] == n:
                            roots(s)
                    copies(n - 1)
                    if n + 1 < 6:
                        evacuate(n + 1)

            @block.gpsimd
            def _(pool):
                for n in range(6):
                    pool.wait_ge(proj_evac, 6 * (n + 1))
                    for s, (blk, c0, nh, _) in enumerate(segs):
                        if blk != n:
                            continue
                        if s >= 1:
                            pool.wait_ge(ss_done, s)
                        x = raw[n % 2][:, :, c0:c0 + nh * HD]
                        nc.gpsimd.tensor_tensor(squares[:, 0:NT * nh * HD].rearrange("p (t c) -> p t c", t=NT), x, x, ALU.mult).then_inc(sq_done, 1)
                    if n == 1:
                        nc.gpsimd.tensor_copy(v_sel, raw[1][:, :, 384:512]).then_inc(v_copied, 1)
                    if n == 2:
                        nc.gpsimd.tensor_copy(v_win, raw[0][:, :, 128:256]).then_inc(v_copied, 1)
                        nc.gpsimd.tensor_copy(g_nsa, raw[0][:, :, 256:280]).then_inc(v_copied, 1)
                    if n == 5:
                        nc.gpsimd.tensor_copy(v_moba, raw[1]).then_inc(v_copied, 1)

            @block.vector
            def _(dve):
                for i in range(2):
                    nc.vector.memset(raw[i][:, 2, :], 0.0).then_inc(rows_cleared, 1)
                for s, (n, c0, nh, gi) in enumerate(segs):
                    x = raw[n % 2][:, :, c0:c0 + nh * HD].rearrange("p t (h d) -> p t h d", d=HD)
                    full = [P, NT, nh, HD]
                    view = lambda a: a[:, 0:NT * nh * HD].rearrange("p (t h d) -> p t h d", t=NT, h=nh)
                    ss = head_ss[:, 0:NT * nh].rearrange("p (t h) -> p t h", t=NT)
                    dve.wait_ge(sq_done, s + 1)
                    nc.vector.tensor_reduce(ss, view(squares), X, ALU.add).then_inc(ss_done, 1)
                    dve.wait_ge(ss_done, s + 1)
                    nc.vector.tensor_scalar(ss, ss, 1.0 / HD, EPS, ALU.mult, ALU.add).then_inc(ms_done, 1)
                    dve.wait_ge(root_done, s + 1)
                    settle(nc.vector.reciprocal(ss, ss))
                    settle(nc.vector.tensor_tensor(x, x, ss.unsqueeze(3).broadcast_to(full), ALU.mult))
                    settle(nc.vector.tensor_tensor(x, x, head_gain[:, gi, :].unsqueeze(1).unsqueeze(1).broadcast_to(full), ALU.mult))
                    nc.vector.tensor_tensor(view(xcos), x, cos.unsqueeze(2).broadcast_to(full), ALU.mult)
                    lo = [P, NT, nh, HALF]
                    nc.vector.tensor_tensor(view(xsin)[:, :, :, 0:HALF], x[:, :, :, HALF:HD], sin[:, :, 0:HALF].unsqueeze(2).broadcast_to(lo), ALU.mult)
                    settle(nc.vector.tensor_tensor(view(xsin)[:, :, :, HALF:HD], x[:, :, :, 0:HALF], sin[:, :, HALF:HD].unsqueeze(2).broadcast_to(lo), ALU.mult))
                    if s == 0:
                        pairs = x.rearrange("p t (j g) d -> p t j g d", g=NSA_G)
                        for g in range(NSA_G):
                            last = nc.vector.tensor_tensor(pairs[:, :, :, g, :], view(xcos)[:, :, GRP * g:GRP * g + GRP, :],
                                                           view(xsin)[:, :, GRP * g:GRP * g + GRP, :], ALU.add)
                    else:
                        last = nc.vector.tensor_tensor(x, view(xcos), view(xsin), ALU.add)
                    if s == len(segs) - 1 or segs[s + 1][0] != n:
                        last.then_inc(rope_done, 1)
                        dve.wait_ge(rope_done, n + 1)
                    else:
                        settle(last)
        c_turned, c_out = sem("c_turned"), [sem("c_copied_act"), sem("c_copied_dve")]
        hid_done, h_chain, bent, h_ready = sem("hid_done"), sem("h_chain"), sem("bent"), sem("h_ready")
        packed_done, rows_out, c_ms, c_root, c_normed = sem("packed_done"), sem("rows_out"), sem("c_ms"), sem("c_root"), sem("c_normed")
        c_final, c_kept, c_zero, small_in, prompt_in = sem("c_final"), sem("c_kept"), sem("c_zero"), sem("small_in"), sem("prompt_in")
        rT = [at(k_at + 2432 * i, 19, P) for i in range(2)]
        hidden = [at(d_at + 4608 + 540 * i, 2, NSA_G, 9 * NC) for i in range(2)]
        w2 = [at(blk_at + 128 * i, 2, HD) for i in range(2)]
        pos_rows = [at(blk_at + 256 + P * i, P) for i in range(2)]
        pre, cube, bend = ([at(blk_at + 512 + 1080 * a + 270 * i, 270) for i in range(4)] for a in range(3))
        kc_rows = at(blk_at + 3752, 2, P)
        kc_sq, kc_ss = at(blk_at + 4008, 2 * P), at(blk_at + 4264, 4)
        vcZ, vc_rows = at(k_at + 4096, 4, P), at(k_at + 4608, 2, P)
        pieces = [(0, NC, 0), (1, 120, 9 - 8)]
        GELU_C = float(np.sqrt(2.0 / np.pi))
        with nc.Block() as block:
            @block.sync
            def _(sp):
                for n in stores:
                    sp.wait_ge(stored[n], 32 * len(stores[n]))
                for i, kv in enumerate("kv"):
                    sp.dma_start(pos_rows[i][0:CST_R, :], t["cmp_pos_" + kv].rearrange("(p two) d -> p (two d)", two=2)).then_inc(small_in, 16)
                    sp.dma_start(w2[i], t["cmp_w2_" + kv].rearrange("(m p) d -> p m d", p=P)).then_inc(small_in, 16)
                for i, name in enumerate(("p_k_c", "p_v_c")):
                    for g in range(NSA_G):
                        sp.dma_start(cmp_rows[i][:, 0, g], t[name].rearrange("a (p two) g d -> (a p) g two d", two=2)[:, g]).then_inc(prompt_in, 16)
                for i in range(2):
                    sp.wait_ge(hid_done, 2 * (i + 1))
                    load_item(sp, 6 + i + RING)

            @block.tensor
            def _(pe):
                pe.wait_ge(small_in, 64)
                pe.wait_ge(prompt_in, 64)
                pe.wait_ge(cache_in, 16 * 64)
                for job in range(20):
                    if job >= 4:
                        pe.wait_ge(c_out[job % 2], job // 2 - 1)
                    if job < 2:
                        mm = nc.tensor.transpose(banks[:, job % 4, 0:CST_R], pos_rows[job][0:CST_R, :], ident[0:CST_R, 0:CST_R])
                    else:
                        i, q = divmod(job - 2, 9)
                        for g in range(NSA_G):
                            mm = nc.tensor.transpose(banks[:, job % 4, P * g:P * g + P], cmp_rows[i][:, q, g].rearrange("p two d -> p (two d)"), ident)
                    mm.then_inc(c_turned, 1)
                for i in range(2):
                    w1 = slot(6 + i, 16)
                    pe.wait_ge(ring_in[(6 + i) % RING], landed[6 + i])
                    for e in range(2):
                        pe.wait_ge(c_out[e], [6, 10][i])
                    for m in range(2):
                        for r in range(CST_R):
                            mm = nc.tensor.matmul(banks[:, 4 + 2 * i + m, 0:19 * NC].rearrange("p (s c) -> p s c", c=NC), w1[:, r, P * m:P * m + P],
                                                  rT[i][:, :, r:r + 113:8], start=(r == 0), stop=(r == CST_R - 1))
                        mm.then_inc(hid_done, 1)
                for i in range(2):
                    pe.wait_ge(h_ready, 4 * (i + 1))
                    for part, rows, s0 in pieces:
                        n = rows // NC
                        for g in range(NSA_G):
                            for m in range(2):
                                mm = nc.tensor.matmul(banks[0:rows, i, P * part + HD * g:P * part + HD * g + HD],
                                                      hidden[i][:, m, g, NC * s0:NC * (s0 + n)], w2[i][:, m, :], start=(m == 0), stop=(m == 1))
                    mm.then_inc(packed_done, 1)
                pe.wait_ge(rows_out, 4)
                for j in range(4):
                    mm = nc.tensor.matmul(banks[:, 3, P * j:P * j + P], const("spread")[0:NC, j, :], vc_rows[0:NC, 0, :], start=True, stop=True)
                mm.then_inc(c_final, 1)
                pe.wait_ge(c_normed, 1)
                for part, rows, _ in pieces:
                    mm = nc.tensor.transpose(banks[:, 2, NC * part:NC * part + rows], kc_rows[0:rows, part, :], ident[0:rows, 0:rows])
                mm.then_inc(c_final, 1)

            def copies(eng, copy, e):
                for job in range(e, 20, 2):
                    eng.wait_ge(c_turned, job + 1)
                    if job < 2:
                        eng.wait_ge(c_zero, 1)
                        copy(rT[job][:, 18, 0:CST_R], banks[:, job % 4, 0:CST_R]).then_inc(c_out[e], 1)
                    else:
                        i, q = divmod(job - 2, 9)
                        copy(rT[i][:, 2 * q:2 * q + 2, :].rearrange("p a b -> p (a b)"), banks[:, job % 4, 0:2 * P]).then_inc(c_out[e], 1)

            @block.scalar
            def _(act):
                copies(act, nc.scalar.copy, 0)
                for k in range(4):
                    act.wait_ge(bent, k + 1)
                    nc.scalar.activation(bend[k], cube[k], ACT.Tanh, scale=GELU_C).then_inc(h_chain, 1)
                act.wait_ge(c_ms, 1)
                nc.scalar.activation(kc_ss, kc_ss, ACT.Sqrt).then_inc(c_root, 1)
                act.wait_ge(c_final, 2)
                nc.scalar.copy(kcT, banks[:, 2, 0:NC + 120]).then_inc(c_kept, 1)

            @block.gpsimd
            def _(pool):
                for i in range(2):
                    nc.gpsimd.memset(rT[i][:, 18, :], 0.0)
                nc.gpsimd.memset(kc_rows, 0.0).then_inc(c_zero, 1)

            @block.vector
            def _(dve):
                copies(dve, nc.vector.tensor_copy, 1)
                for k in range(4):
                    dve.wait_ge(hid_done, k + 1)
                    bank = banks[:, 4 + k, :]
                    settle(nc.vector.tensor_scalar(pre[k], bank[:, 0:270], bank[:, 270:271], None, ALU.add))
                    settle(nc.vector.tensor_tensor(cube[k], pre[k], pre[k], ALU.mult))
                    settle(nc.vector.tensor_scalar(cube[k], cube[k], 0.044715, 1.0, ALU.mult, ALU.add))
                    nc.vector.tensor_tensor(cube[k], cube[k], pre[k], ALU.mult).then_inc(bent, 1)
                for k in range(4):
                    dve.wait_ge(h_chain, k + 1)
                    view = lambda a, g: a.rearrange("p (s g c) -> p s g c", s=9, g=NSA_G)[:, :, g, :]
                    for g in range(NSA_G):
                        nc.vector.scalar_tensor_tensor(hidden[k // 2][:, k % 2, g, :].rearrange("p (s c) -> p s c", c=NC), view(bend[k], g), 1.0,
                                                       view(pre[k], g), ALU.add, ALU.mult).then_inc(h_ready, 1)
                for i, dst in enumerate((kc_rows, vc_rows)):
                    dve.wait_ge(packed_done, i + 1)
                    for part, rows, _ in pieces:
                        nc.vector.tensor_scalar(dst[0:rows, part, :], banks[0:rows, i, P * part:P * part + P], 0.5, None, ALU.mult).then_inc(rows_out, 1)
                dve.wait_ge(rows_out, 4)
                x = kc_rows.rearrange("p a (g d) -> p (a g) d", d=HD)
                sq = kc_sq.rearrange("p (a d) -> p a d", d=HD)
                settle(nc.vector.tensor_tensor(sq, x, x, ALU.mult))
                settle(nc.vector.tensor_reduce(kc_ss, sq, X, ALU.add))
                nc.vector.tensor_scalar(kc_ss, kc_ss, 1.0 / HD, EPS, ALU.mult, ALU.add).then_inc(c_ms, 1)
                dve.wait_ge(c_root, 1)
                settle(nc.vector.reciprocal(kc_ss, kc_ss))
                settle(nc.vector.tensor_tensor(x, x, kc_ss.unsqueeze(2).broadcast_to([P, 4, HD]), ALU.mult))
                nc.vector.tensor_tensor(x, x, head_gain[:, 6, :].unsqueeze(1).broadcast_to([P, 4, HD]), ALU.mult).then_inc(c_normed, 1)
                dve.wait_ge(c_final, 1)
                nc.vector.tensor_copy(vcZ.rearrange("p a b -> p (a b)"), banks[:, 3, :]).then_inc(c_kept, 1)

        oaT, obT = at(out_at, 4, TOK), at(out_at + 4 * TOK, 4, TOK)
        q_nsa, q_cmp, q_moba = at(d_at, 576), at(d_at + 576, 64), at(d_at + 640, 4, 272)
        p_nsa, p_moba, p_cmp = at(d_at + 1728, 257), at(d_at + 1988, 257), at(d_at + 2248, 120)
        pT_nsa, pT_new, pT_moba = at(d_at + 2368, 2, 152), at(d_at + 2672, 152), at(d_at + 2824, 2, 88)
        pT_mnew, pT_cmp = at(d_at + 3000, 88), at(d_at + 3088, 88)
        own_new = at(d_at + 3176, 2, 8)
        soft = at(d_at + 3192, 24)
        o_nsa, o_moba = at(d_at + 3216, 2, P), at(d_at + 3472, 2, 512)
        sig_nsa = g_nsa
        cache = [at(blk_at + 1536 * i, 1536) for i in range(3)]
        kT = [at(k_at + 1536 * i, 1536) for i in range(2)]
        slot_in = [sem(f"cache_slot{i}") for i in range(3)]
        q_spread, k_turned, k_out, qk_done = sem("q_spread"), sem("k_turned"), [sem("k_out_act"), sem("k_out_dve")], sem("qk_done")
        gate_e, gate_done, gate_rows, d_min, d_exp = (sem("d_" + x) for x in ("ge", "gd", "gr", "min", "exp"))
        d_prob, d_turned, d_kept, pv_done, o_out, o_turned, o_kept = (sem("d_" + x) for x in ("prob", "turned", "kept", "pv", "oout", "oturned", "okept"))
        K_NAMES = ("cache_nsa_sel_k", "cache_nsa_win_k", "cache_moba_k")
        V_NAMES = ("cache_nsa_sel_v", "cache_nsa_win_v", "cache_moba_v")
        with nc.Block() as block:
            @block.sync
            def _(sp):
                pages = at(k_at + 3100, 16).bitcast(I32)
                sp.dma_start(pages[0:1, :], t["page_table"].rearrange("a b -> (a b)").unsqueeze(0)).then_inc(pages_in, 16)
                sp.wait_ge(pages_in, 32)
                for q in range(2 * DB):
                    b, names = q % DB, (K_NAMES if q < DB else V_NAMES)
                    if q >= 3:
                        if q - 3 < DB:
                            sp.wait_ge(k_turned, 3 * (q - 3) + 3)
                        else:
                            sp.wait_ge(pv_done, q - 3 - DB + 1)
                    dst, arrived = cache[q % 3], slot_in[q % 3]
                    for g in range(N_PAGES):
                        page = sp.value_load(pages[0:1, 2 * b + g:2 * b + g + 1], min_val=0, max_val=t["cache_moba_k"].shape[0] - 1)
                        sp.dma_start(dst[:, P * g:P * g + P], t[names[0]][page].rearrange("p h d -> p (h d)")).then_inc(arrived, 16)
                        sp.dma_start(dst[:, 512 + 512 * g:1024 + 512 * g], t[names[2]][page].rearrange("p h d -> p (h d)")).then_inc(arrived, 16)
                    sp.dma_start(dst[:, 256:512].rearrange("p (t n) -> p t n", t=2),
                                 t[names[1]][b].rearrange("(t p) h d -> p t (h d)", p=P)).then_inc(arrived, 16)

            @block.gpsimd
            def _(pool):
                nc.gpsimd.memset(at(d_at, 1728), 0.0).then_inc(q_spread, 1)
                nc.gpsimd.memset(at(d_at + 2368, 808), 0.0).then_inc(q_spread, 1)

            @block.tensor
            def _(pe):
                def turn_keys(b):
                    pe.wait_ge(slot_in[b % 3], 80 * (b // 3 + 1))
                    for k in range(3):
                        job = 3 * b + k
                        if job >= 4:
                            pe.wait_ge(k_out[job % 2], job // 2 - 1)
                        for i in range(4):
                            c = [P * i, 512 + 512 * (i % 2) + P * (i // 2), 512 + 512 * (i % 2) + P * (2 + i // 2)][k]
                            mm = nc.tensor.transpose(banks[:, job % 4, P * i:P * i + P], cache[b % 3][:, c:c + P], ident)
                        mm.then_inc(k_turned, 1)

                def scores(b):
                    for e in range(2):
                        pe.wait_ge(k_out[e], (3 * b + 3 + 1 - e) // 2)
                    keys = kT[b % 2]
                    for c0, c1, new in ((0, 256, False), (256, 257, True)):
                        for br in range(2):
                            rhs = (ksT, kwT)[br][:, SEQ + b:SEQ + b + 1] if new else keys[:, 256 * br:256 * br + 256]
                            nc.tensor.matmul(banks[64 * br:64 * br + 64, 4, c0:c1], q_nsa[:, 64 * b:64 * b + 64], rhs,
                                             start=(b == 0 and not new), stop=(b == DB - 1), skip_group_check=True)
                        for j in range(4):
                            rhs = kbT[:, j, SEQ + b:SEQ + b + 1] if new else keys[:, 512 + 256 * j:768 + 256 * j]
                            mm = nc.tensor.matmul(banks[32 * j:32 * j + 32, 5, c0:c1], q_moba[:, j, 32 * b:32 * b + 32], rhs,
                                                  start=(b == 0 and not new), stop=(b == DB - 1), skip_group_check=True, tile_position=(0, 32 * j))
                    mm.then_inc(qk_done, 1)

                turn_keys(0)
                pe.wait_ge(q_spread, 3)
                nc.tensor.matmul(banks[0:64, 6, 0:120], q_cmp, kcT[:, NC:NC + 120], start=True, stop=True)
                pe.wait_ge(gate_done, 1)
                nc.tensor.matmul(banks[:, 7, 0:24], const("req_rows")[0:DB, :], sig_nsa[0:DB, 2, :], start=True, stop=True).then_inc(gate_rows, 1)
                for b in range(DB):
                    if b + 1 < DB:
                        turn_keys(b + 1)
                    scores(b)
                for e in range(2):
                    pe.wait_ge(k_out[e], 12)
                for i, (src, new) in enumerate(((p_nsa, own_new[:, 0, :]), (p_moba, own_new[:, 1, :]))):
                    pe.wait_ge(d_prob, i + 1)
                    for k in range(2):
                        nc.tensor.transpose(banks[:, i, P * k:P * k + P], src[:, P * k:P * k + P], ident)
                    nc.tensor.transpose(banks[0:8, i, 256:384], new, ident).then_inc(d_turned, 1)
                pe.wait_ge(d_prob, 3)
                nc.tensor.transpose(banks[0:120, 2, 0:64], p_cmp[0:64, :], ident[0:64, 0:64]).then_inc(d_turned, 1)
                pe.wait_ge(d_kept, 7)
                for b in range(DB):
                    q = DB + b
                    pe.wait_ge(slot_in[q % 3], 80 * (q // 3 + 1))
                    v, row, w = cache[q % 3], 32 * (b % 4), 8 * b
                    out = banks[row:row + 32, 6, P * (b // 4):P * (b // 4) + P]
                    terms = []
                    for br, v_new in enumerate((v_sel, v_win)):
                        terms.append((pT_new[0:DB, 64 * br + w:64 * br + w + 32], v_new[0:DB, 2, :]))
                        for k in range(2):
                            terms.append((pT_nsa[:, k, 64 * br + w:64 * br + w + 32], v[:, 256 * br + P * k:256 * br + P * k + P]))
                    terms.append((pT_cmp[0:120, w:w + 32], vc_rows[0:120, 1, :]))
                    for n, (lhsT, rhs) in enumerate(terms):
                        nc.tensor.matmul(out, lhsT, rhs, start=(n == 0), stop=(n == len(terms) - 1), tile_position=(0, row))
                    out = banks[row:row + 32, 4 + b // 4, :]
                    nc.tensor.matmul(out, pT_mnew[0:DB, w:w + 32], v_moba[0:DB, 2, :], start=True, stop=False, tile_position=(0, row))
                    for k in range(2):
                        mm = nc.tensor.matmul(out, pT_moba[:, k, w:w + 32], v[:, 512 + 512 * k:1024 + 512 * k], start=False, stop=(k == 1), tile_position=(0, row))
                    mm.then_inc(pv_done, 1)
                pe.wait_ge(o_out, 3)
                for n in range(2):
                    nc.tensor.transpose(banks[:, 0, P * n:P * n + P], o_nsa[:, n, :], ident)
                for n in range(2):
                    for j in range(4):
                        mm = nc.tensor.transpose(banks[:, 1 + n, P * j:P * j + P], o_moba[:, n, P * j:P * j + P], ident)
                mm.then_inc(o_turned, 1)

            def copy_keys(eng, copy, e):
                for job in range(e, 3 * DB, 2):
                    b, k = divmod(job, 3)
                    eng.wait_ge(k_turned, job + 1)
                    if b >= 2:
                        eng.wait_ge(qk_done, b - 1)
                    copy(kT[b % 2][:, 512 * k:512 * k + 512], banks[:, job % 4, :]).then_inc(k_out[e], 1)

            @block.scalar
            def _(act):
                nc.scalar.activation(sig_nsa, sig_nsa, ACT.Exp, scale=-1.0).then_inc(gate_e, 1)
                copy_keys(act, nc.scalar.copy, 0)
                for i, (dst, src, rows) in enumerate(((p_nsa, banks[:, 4, 0:257], P), (p_moba, banks[:, 5, 0:257], P), (p_cmp[0:64, :], p_cmp[0:64, :], 64))):
                    act.wait_ge(d_min, i + 1)
                    nc.scalar.activation(dst, src, ACT.Exp, scale=-1.0, bias=soft[0:rows, i:i + 1], accum_out=soft[0:rows, 4 + i:5 + i]).then_inc(d_exp, 1)
                act.wait_ge(d_turned, 2)
                for k in range(2):
                    src = banks[:, 1, P * k:P * k + P].rearrange("p (j q) -> p j q", q=32)[:, :, 0:16].rearrange("p j (b h) -> p j b h", h=2)
                    dst = pT_moba[:, k, 0:64].rearrange("p (b j h) -> p j b h", b=8, j=4)
                    nc.scalar.copy(dst, src).then_inc(d_kept, 1)
                src = banks[0:8, 1, 256:384].rearrange("p (j q) -> p j q", q=32)[:, :, 0:16].rearrange("p j (b h) -> p j b h", h=2)
                nc.scalar.copy(pT_mnew[0:8, 0:64].rearrange("p (b j h) -> p j b h", b=8, j=4), src).then_inc(d_kept, 1)
                act.wait_ge(d_turned, 3)
                nc.scalar.copy(pT_cmp[0:120, 0:64], banks[0:120, 2, 0:64]).then_inc(d_kept, 1)
                for n in range(2):
                    act.wait_ge(pv_done, 4 * n + 4)
                    nc.scalar.copy(o_moba[:, n, :], banks[:, 4 + n, :]).then_inc(o_out, 1)
                act.wait_ge(o_turned, 1)
                for j in range(4):
                    for h in range(2):
                        half = slice(64 * h, 64 * h + 64)
                        src = banks[half, 1:3, P * j + 2 * j + h:P * j + 2 * j + h + 97:32]
                        last = nc.scalar.copy(obT[half, j, SEQ:TOK].rearrange("p (n b) -> p n b", n=2), src)
                last.then_inc(o_kept, 1)

            @block.vector
            def _(dve):
                dve.wait_ge(q_spread, 2)
                for g in range(2):
                    half = slice(64 * g, 64 * g + 64)
                    src = qaT[half, :, SEQ:TOK].rearrange("p j b -> p b j")
                    nc.vector.tensor_copy(q_nsa[half, :].rearrange("p (b x) -> p b x", x=72)[:, :, 4 * g:4 * g + 4], src)
                    nc.vector.tensor_copy(q_cmp[half, :].rearrange("p (b x) -> p b x", x=8)[:, :, 4 * g:4 * g + 4], src)
                    last = nc.vector.tensor_copy(q_moba[half].rearrange("p j (b x) -> p j b x", x=34)[:, :, :, g], qbT[half, :, SEQ:TOK])
                last.then_inc(q_spread, 1)
                dve.wait_ge(gate_e, 1)
                flat = sig_nsa.rearrange("p a b -> p (a b)")
                settle(nc.vector.tensor_scalar(flat, flat, 1.0, None, ALU.add))
                nc.vector.reciprocal(flat, flat).then_inc(gate_done, 1)
                copy_keys(dve, nc.vector.tensor_copy, 1)
                dve.wait_ge(qk_done, DB)
                for i in range(2):
                    nc.vector.tensor_reduce(soft[:, i:i + 1], banks[:, 4 + i, 0:257], X, ALU.min).then_inc(d_min, 1)
                nc.vector.tensor_tensor_reduce(p_cmp[0:64, :], banks[0:64, 6, 0:120], const("dec_cmp")[0:64, :], 1.0, 3e38,
                                               ALU.add, ALU.min, soft[0:64, 2:3]).then_inc(d_min, 1)
                dve.wait_ge(gate_rows, 1)
                nc.vector.tensor_tensor_reduce(o_nsa[:, 0, 0:24], banks[:, 7, 0:24], const("gate_sel"), 1.0, 0.0, ALU.mult, ALU.add, soft[:, 8:9])
                settle(nc.vector.tensor_tensor_reduce(o_nsa[0:64, 1, 0:24], banks[0:64, 7, 0:24], const("gate_cmp")[0:64, :], 1.0, 0.0, ALU.mult, ALU.add, soft[0:64, 10:11]))
                for i, (p, rows, cols) in enumerate(((p_nsa, P, 257), (p_moba, P, 257), (p_cmp, 64, 120))):
                    dve.wait_ge(d_exp, i + 1)
                    weight = soft[0:rows, 4 + i:5 + i]
                    settle(nc.vector.reciprocal(weight, weight))
                    if i != 1:
                        settle(nc.vector.tensor_tensor(weight, weight, soft[0:rows, 8 + i:9 + i], ALU.mult))
                    scaled = nc.vector.tensor_scalar(p[0:rows, :], p[0:rows, :], weight, None, ALU.mult)
                    if i < 2:
                        settle(scaled)
                        scaled = nc.vector.tensor_scalar(own_new[:, i, :], const(("own_nsa", "own_moba")[i]), p[:, 256:257], None, ALU.mult)
                    scaled.then_inc(d_prob, 1)
                dve.wait_ge(d_turned, 1)
                for k in range(2):
                    nc.vector.tensor_copy(pT_nsa[:, k, 0:P], banks[:, 0, P * k:P * k + P]).then_inc(d_kept, 1)
                nc.vector.tensor_copy(pT_new[0:8, 0:P], banks[0:8, 0, 256:384]).then_inc(d_kept, 1)
                dve.wait_ge(pv_done, DB)
                nc.vector.tensor_copy(o_nsa.rearrange("p a b -> p (a b)"), banks[:, 6, 0:256]).then_inc(o_out, 1)
                dve.wait_ge(o_turned, 1)
                for g in range(2):
                    half = slice(64 * g, 64 * g + 64)
                    src = banks[half, 0, 0:256].rearrange("p (b x) -> p b x", x=32)[:, :, 4 * g:4 * g + 4]
                    nc.vector.tensor_copy(oaT[half, :, SEQ:TOK].rearrange("p j b -> p b j"), src).then_inc(o_kept, 1)

        units = [("moba", j, 0) for j in range(4)] + [("nsa", j, i) for j in range(4) for i in range(2)]

        def blocks_of(unit):
            kind, j, i = unit
            if kind == "moba":
                return [(0, kbT[:, j, :], P, 0), (1, kbT[:, j, :], 2 * P, P)]
            n = P * (i + 1)
            return [(i, ksT, n, 0), (i, kwT, n, n)]

        prob = [[at(k_at + 1024 * a + 512 * x, 512) for x in range(2)] for a in range(2)]
        probT = [[at(k_at + 2048 + 1024 * a + 512 * x, 512) for x in range(2)] for a in range(2)]
        cmp_s, cmp_p, cmp_pT = at(d_at, 2, 2, 60), at(d_at + 240, 2, 2, P), at(d_at + 752, 4, P)
        cmp_min, cmp_sum = at(d_at + 1264, 4, 4), at(d_at + 1280, 4, 4)
        mins = [at(d_at + 1300 + 4 * a, 4) for a in range(2)]
        sums = [at(d_at + 1310 + 4 * a, 4) for a in range(2)]
        s_done, a_min, a_exp, a_weight, a_scaled, a_turned = (sem("a_" + x) for x in ("s", "min", "exp", "weight", "scaled", "turned"))
        a_kept, a_pv, a_out, cmp_sem, cmp_exp = [sem("a_kept_act"), sem("a_kept_dve")], sem("a_pv"), sem("a_out"), sem("cmp_sem"), sem("cmp_exp")
        cmp_read, cmp_ready, cmp_T, cmp_kept = sem("cmp_read"), sem("cmp_ready"), sem("cmp_T"), sem("cmp_kept")
        with nc.Block() as block:
            @block.tensor
            def _(pe):
                for g in range(2):
                    half = slice(64 * g, 64 * g + 64)
                    for i in range(2):
                        for j in range(4):
                            c = 60 * i + NC * j
                            mm = nc.tensor.matmul(banks[:, 4 + g, c:c + NC], qaT[half, j, P * i:P * i + P], kcT[half, 0:NC], start=True, stop=True)
                mm.then_inc(cmp_sem, 1)
                for step in range(len(units) + 2):
                    if step < len(units):
                        u = step
                        if u >= 2:
                            pe.wait_ge(a_min, 4 * (u - 1))
                        q = (qbT if units[u][0] == "moba" else qaT)[:, units[u][1], :]
                        for i, keys, n, c in blocks_of(units[u]):
                            for x in range(2):
                                half = slice(64 * x, 64 * x + 64)
                                mm = nc.tensor.matmul(banks[:, 2 * (u % 2) + x, c:c + n], q[half, P * i:P * i + P], keys[half, 0:n], start=True, stop=True)
                        mm.then_inc(s_done, 1)
                    if 1 <= step <= len(units):
                        u = step - 1
                        pe.wait_ge(a_scaled, 4 * (u + 1))
                        if u == 0:
                            pe.wait_ge(cmp_read, 4)
                        for x in range(2):
                            if u >= 1:
                                pe.wait_ge(a_kept[x], u)
                            tile = 0
                            for i, _, n, c in blocks_of(units[u]):
                                for k in range(n // P):
                                    mm = nc.tensor.transpose(banks[:, 4 + x, P * tile:P * tile + P], prob[u % 2][x][:, c + P * k:c + P * k + P], ident)
                                    tile += 1
                            mm.then_inc(a_turned, 1)
                    if step == 1:
                        pe.wait_ge(cmp_ready, 1)
                        for n in range(4):
                            mm = nc.tensor.transpose(banks[:, 7, P * n:P * n + P], cmp_p[:, n // 2, n % 2, :], ident)
                        mm.then_inc(cmp_T, 1)
                    if step >= 2:
                        u = step - 2
                        kind, j, i = units[u]
                        out_job = j if kind == "moba" else 4 + j
                        for x in range(2):
                            pe.wait_ge(a_kept[x], u + 1)
                        if out_job >= 2:
                            pe.wait_ge(a_out, out_job - 1)
                        if u == 1:
                            pe.wait_ge(cmp_kept, 1)
                        for x in range(2):
                            rows, tile = slice(64 * x, 64 * x + 64), 0
                            bank = banks[rows, 6 + out_job % 2, :]
                            if kind == "moba":
                                v = v_moba[:, :, P * j + 64 * x:P * j + 64 * x + 64]
                                for i, _, n, _ in blocks_of(units[u]):
                                    for k in range(n // P):
                                        mm = nc.tensor.matmul(bank[:, P * i:P * i + P], v[:, k, :], probT[u % 2][x][:, P * tile:P * tile + P],
                                                              start=(k == 0), stop=(k == n // P - 1))
                                        tile += 1
                            else:
                                for br, v in enumerate((v_sel, v_win)):
                                    for k in range(i + 1):
                                        nc.tensor.matmul(bank[:, P * i:P * i + P], v[:, k, 64 * x:64 * x + 64], probT[u % 2][x][:, P * tile:P * tile + P],
                                                         start=(tile == 0), stop=False)
                                        tile += 1
                                mm = nc.tensor.matmul(bank[:, P * i:P * i + P], vcZ[:, j, 64 * x:64 * x + 64], cmp_pT[:, 2 * x + i, :], start=False, stop=True)
                        mm.then_inc(a_pv, 1)

            def keep(eng, copy, x, u):
                eng.wait_ge(a_turned, 2 * u + x + 1)
                if u >= 2:
                    eng.wait_ge(a_pv, u - 1)
                n = sum(b[2] for b in blocks_of(units[u]))
                copy(probT[u % 2][x][:, 0:n], banks[:, 4 + x, 0:n]).then_inc(a_kept[x], 1)

            @block.scalar
            def _(act):
                for step in range(len(units) + 1):
                    if step < len(units):
                        u = step
                        for x in range(2):
                            for k, (i, _, n, c) in enumerate(blocks_of(units[u])):
                                act.wait_ge(a_min, 4 * u + 2 * x + k + 1)
                                s = prob[u % 2][x][:, c:c + n]
                                nc.scalar.activation(s, s, ACT.Exp, scale=-1.0, bias=mins[u % 2][:, 2 * x + k:2 * x + k + 1],
                                                     accum_out=sums[u % 2][:, 2 * x + k:2 * x + k + 1]).then_inc(a_exp, 1)
                    if step == 0:
                        act.wait_ge(cmp_exp, 1)
                        flat = cmp_s.rearrange("p a b c -> p (a b c)")
                        nc.scalar.activation(flat, flat, ACT.Exp, scale=-1.0).then_inc(cmp_exp, 1)
                    if step >= 1:
                        keep(act, nc.scalar.copy, 0, step - 1)

            @block.gpsimd
            def _(pool):
                nc.gpsimd.memset(cmp_p, 0.0).then_inc(cmp_exp, 1)
                for u in range(len(units)):
                    pool.wait_ge(a_weight, u + 1)
                    for x in range(2):
                        for k, (i, _, n, c) in enumerate(blocks_of(units[u])):
                            s = prob[u % 2][x][:, c:c + n]
                            nc.gpsimd.tensor_scalar(s, s, sums[u % 2][:, 2 * x + k:2 * x + k + 1], None, ALU.mult).then_inc(a_scaled, 1)

            @block.vector
            def _(dve):
                def compressed():
                    dve.wait_ge(cmp_sem, 1)
                    for g in range(2):
                        for i in range(2):
                            nc.vector.tensor_tensor(cmp_s[:, g, i, :].rearrange("p (j c) -> p j c", c=NC), banks[:, 4 + g, 60 * i:60 * i + 60].rearrange("p (j c) -> p j c", c=NC),
                                                    const("cmp_out")[:, i, :].unsqueeze(1).broadcast_to([P, 4, NC]), ALU.add).then_inc(cmp_read, 1)
                    dve.wait_ge(cmp_read, 4)
                    s = cmp_s.rearrange("p a b (j c) -> p (a b) j c", c=NC)
                    settle(nc.vector.tensor_reduce(cmp_min, s, X, ALU.min))
                    nc.vector.tensor_tensor(s, s, cmp_min.unsqueeze(3).broadcast_to([P, 4, 4, NC]), ALU.subtract).then_inc(cmp_exp, 1)

                def compressed_rest():
                    s = cmp_s.rearrange("p a b (j c) -> p (a b) j c", c=NC)
                    dve.wait_ge(cmp_exp, 3)
                    for i in range(2):
                        v = cmp_s[:, :, i, :].rearrange("p g (j c) -> p g j c", c=NC)
                        last = nc.vector.tensor_tensor(v, v, const("cmp_in")[:, i, :].unsqueeze(1).unsqueeze(1).broadcast_to([P, 2, 4, NC]), ALU.mult)
                    settle(last)
                    settle(nc.vector.tensor_reduce(cmp_sum, s, X, ALU.add))
                    flat = cmp_sum.rearrange("p a b -> p (a b)")
                    settle(nc.vector.tensor_scalar(flat, flat, 1e-30, None, ALU.max))
                    settle(nc.vector.reciprocal(flat, flat))
                    gates = sig_nsa.rearrange("p t (g j c) -> p t g j c", g=2, j=4)
                    for g in range(2):
                        last = nc.vector.tensor_tensor(cmp_sum[:, 2 * g:2 * g + 2, :], cmp_sum[:, 2 * g:2 * g + 2, :], gates[:, 0:2, g, :, 0], ALU.mult)
                    settle(last)
                    for g in range(2):
                        for i in range(2):
                            last = nc.vector.tensor_tensor(cmp_p[:, g, i, :].rearrange("p (j c) -> p j c", c=32)[:, :, 0:NC], cmp_s[:, g, i, :].rearrange("p (j c) -> p j c", c=NC),
                                                           cmp_sum[:, 2 * g + i, :].unsqueeze(2).broadcast_to([P, 4, NC]), ALU.mult)
                    last.then_inc(cmp_ready, 1)
                    dve.wait_ge(cmp_T, 1)
                    nc.vector.tensor_copy(cmp_pT.rearrange("p a b -> p (a b)"), banks[:, 7, :]).then_inc(cmp_kept, 1)

                compressed()
                for step in range(len(units) + 2):
                    if step < len(units):
                        u = step
                        dve.wait_ge(s_done, u + 1)
                        if u >= 2:
                            dve.wait_ge(a_turned, 2 * (u - 1))
                        for x in range(2):
                            for k, (i, _, n, c) in enumerate(blocks_of(units[u])):
                                nc.vector.tensor_tensor_reduce(prob[u % 2][x][:, c:c + n], banks[:, 2 * (u % 2) + x, c:c + n], causal[:, 2 * P - n:2 * P],
                                                               1.0, 3e38, ALU.add, ALU.min, mins[u % 2][:, 2 * x + k:2 * x + k + 1]).then_inc(a_min, 1)
                    if step >= 1 and step <= len(units):
                        keep(dve, nc.vector.tensor_copy, 1, step - 1)
                    if step >= 2:
                        kind, j, i = units[step - 2]
                        if kind == "moba" or i == 1:
                            out_job = j if kind == "moba" else 4 + j
                            dve.wait_ge(a_pv, step - 1)
                            nc.vector.tensor_copy((obT if kind == "moba" else oaT)[:, j, 0:SEQ], banks[:, 6 + out_job % 2, 0:SEQ]).then_inc(a_out, 1)
                    if step < len(units):
                        u = step
                        dve.wait_ge(a_exp, 4 * (u + 1))
                        kind, j, i = units[u]
                        if kind == "moba":
                            nc.vector.reciprocal(sums[u % 2], sums[u % 2]).then_inc(a_weight, 1)
                        else:
                            settle(nc.vector.reciprocal(sums[u % 2], sums[u % 2]))
                            w = sums[u % 2].rearrange("p (g k) -> p g k", g=2)
                            gates = sig_nsa[:, i, :].rearrange("p (g j c) -> p g j c", g=2, j=4)[:, :, j, 1:3]
                            nc.vector.tensor_tensor(w, w, gates, ALU.mult).then_inc(a_weight, 1)
                    if step == 0:
                        compressed_rest()
        g_done, g_sig, up_done, up_scaled, merged, out_done, out_added, x_in = (sem("m_" + x) for x in ("g", "sig", "up", "scaled", "merged", "out", "added", "x"))
        sig = at(d_at, 16, TOK)
        h = at(blk_at, NT, D)
        EXPERT0 = N_DENSE

        def expert_slot(s):
            return (EXPERT0 + s) % RING

        def load_expert_slot(eng, e, s):
            if s < 4:
                src = t["w_gu"][e].rearrange("(c p) n -> p c n", p=P)[:, 2 * s:2 * s + 2, :]
                dst = ring[:, expert_slot(s), :].rearrange("p (c n) -> p c n", c=2)
            else:
                src = t["w_down"][e].rearrange("(c p) n -> p c n", p=P)[:, 4 * (s - 4):4 * (s - 4) + 4, :]
                dst = ring[:, expert_slot(s), :].rearrange("p (c n) -> p c n", c=4)
            eng.dma_start(dst, src).then_inc(ring_in[expert_slot(s)], 16)

        m_at = blk_at + 3 * 1536
        bias_in, bias_split, bias_left = sem("bias_in"), sem("bias_split"), sem("bias_left")
        bias = at(m_at, 3 * D)
        bias_parts = at(m_at + 3 * D, 3 * D // 2).bitcast(BF16)
        SPLIT = 3 * NEXP
        with nc.Block() as block:
            @block.sync
            def _(sp):
                for q in range(3):
                    rows = slice(NEXP * q, NEXP * q + NEXP)
                    sp.dma_start(bias[rows, 0:2 * D], t["b_gu"]).then_inc(bias_in, 16)
                    sp.dma_start(bias[rows, 2 * D:3 * D], t["b_down"]).then_inc(bias_in, 16)
                sp.dma_start(h[:, 0:2, :], t["x_prompt"].rearrange("a (t p) d -> p (a t) d", p=P)).then_inc(x_in, 16)
                sp.dma_start(h[0:DB, 2, :], t["x_sample"].rearrange("a b d -> (a b) d")).then_inc(x_in, 16)
                for n in range(8, N_DENSE):
                    if n < 12:
                        sp.wait_ge(g_done, 4 * (n - 7))
                    elif n < 14:
                        sp.wait_ge(up_done, 16)
                    else:
                        sp.wait_ge(out_done, n - 13)
                    if n + RING < N_DENSE:
                        load_item(sp, n + RING)
                    else:
                        load_expert_slot(sp, 0, n + RING - N_DENSE)

            @block.tensor
            def _(pe):
                for f in range(16):
                    if f % 4 == 0:
                        pe.wait_ge(ring_in[(8 + f // 4) % RING], landed[8 + f // 4])
                    if f >= 4:
                        pe.wait_ge(g_sig, f - 3)
                    w = slot(8 + f // 4, KC)
                    for c in range(KC):
                        mm = nc.tensor.matmul(banks[:, f % 4, 0:TOK], w[:, c, P * (f % 4):P * (f % 4) + P], xnT[:, c, :], start=(c == 0), stop=(c == KC - 1))
                    mm.then_inc(g_done, 1)
                for m in range(KC):
                    for x, o in enumerate((oaT, obT)):
                        if m == 0:
                            pe.wait_ge(ring_in[(12 + x) % RING], landed[12 + x])
                        if m >= 2:
                            pe.wait_ge(up_scaled, 2 * (m - 2) + x + 1)
                        w = slot(12 + x, 4)
                        for j in range(4):
                            mm = nc.tensor.matmul(banks[:, 4 + 2 * (m % 2) + x, 0:TOK], w[:, j, P * m:P * m + P], o[:, j, :], start=(j == 0), stop=(j == 3))
                        mm.then_inc(up_done, 1)
                pe.wait_ge(up_scaled, 16)
                for c in range(KC):
                    if c % 4 == 0:
                        pe.wait_ge(ring_in[(14 + c // 4) % RING], landed[14 + c // 4])
                    pe.wait_ge(merged, c + 1)
                    w = slot(14 + c // 4, 4)
                    for i in range(2):
                        for n in range(2):
                            nc.tensor.matmul(banks[:, 2 * i + n, :], sig[:, c, P * i:P * i + P], w[:, c % 4, 512 * n:512 * n + 512], start=(c == 0), stop=(c == KC - 1))
                    for j in range(4):
                        mm = nc.tensor.matmul(banks[32 * j:32 * j + DB, 4, 0:256], sig[:, c, SEQ:TOK], w[:, c % 4, 256 * j:256 * j + 256],
                                              start=(c == 0), stop=(c == KC - 1), tile_position=(0, 32 * j))
                    if c % 4 == 3:
                        mm.then_inc(out_done, 1)

            @block.scalar
            def _(act):
                for f in range(16):
                    act.wait_ge(g_done, f + 1)
                    nc.scalar.activation(sig[:, f, :], banks[:, f % 4, 0:TOK], ACT.Sigmoid).then_inc(g_sig, 1)

            @block.gpsimd
            def _(pool):
                pool.wait_ge(bias_in, 16 * 6)
                for step, less in enumerate(("less_first", "less_second", None)):
                    nc.gpsimd.tensor_copy(bias_parts[0:SPLIT, :], bias[0:SPLIT, :]).then_inc(bias_split, 1)
                    if less:
                        pool.wait_ge(bias_left, step + 1)
                for m in range(KC):
                    pool.wait_ge(up_scaled, 2 * m + 2)
                    nc.gpsimd.tensor_tensor(sig[:, m, :], sig[:, m, :], sig[:, 8 + m, :], ALU.add).then_inc(merged, 1)

            @block.vector
            def _(dve):
                for step, less in enumerate(("less_first", "less_second")):
                    dve.wait_ge(bias_split, step + 1)
                    nc.vector.scalar_tensor_tensor(bias[0:SPLIT, :], bias_parts[0:SPLIT, :], const(less)[0:SPLIT, 0:1], bias[0:SPLIT, :], ALU.mult, ALU.add).then_inc(bias_left, 1)
                dve.wait_ge(g_sig, 16)
                for m in range(KC):
                    for x in range(2):
                        dve.wait_ge(up_done, 2 * m + x + 1)
                        s = sig[:, 8 * x + m, :]
                        nc.vector.tensor_tensor(s, banks[:, 4 + 2 * (m % 2) + x, 0:TOK], s, ALU.mult).then_inc(up_scaled, 1)
                dve.wait_ge(x_in, 32)
                dve.wait_ge(out_done, 2)
                for i in range(2):
                    for n in range(2):
                        v = h[:, i, 512 * n:512 * n + 512]
                        nc.vector.tensor_tensor(v, banks[:, 2 * i + n, :], v, ALU.add).then_inc(out_added, 1)
                for j in range(4):
                    nc.vector.tensor_copy(at(k_at, D)[0:DB, 256 * j:256 * j + 256], banks[32 * j:32 * j + DB, 4, 0:256]).then_inc(out_added, 1)
                dve.wait_ge(out_added, 8)
                nc.vector.tensor_tensor(h[0:DB, 2, :], h[0:DB, 2, :], at(k_at, D)[0:DB, :], ALU.add).then_inc(out_added, 1)

        free = [(d_at + 3 * D, total), (m_at, m_at + 3 * D), (m_at + 3 * D + 3 * D // 2, out_at - 64), (blk_at + 3 * D, m_at), (out_at, k_at - 16)]

        def etake(*dims):
            n = int(np.prod(dims))
            k = next(k for k, (a, b) in enumerate(free) if b - a >= n)
            a, b = free[k]
            free[k] = (a + n, b)
            return at(a, *dims)

        def etake_bf16(rows, *dims):
            n = int(np.prod(dims))
            names = "abcd"[:len(dims)]
            return etake(-(-n // 2)).bitcast(BF16)[0:rows, 0:n].rearrange(
                f"p ({' '.join(names)}) -> p {' '.join(names)}", **{k: d for k, d in zip(names[1:], dims[1:])})

        xn2 = at(d_at, NT, D)
        norm_phase("n2_", h, xn2, at(k_at, D), at(k_at + D, D), False)
        free.append((k_at, d_at))

        x_parts = etake_bf16(P, 2, 3, D)
        tail_parts = etake_bf16(P, D)
        acc = etake(KC, TOK)
        TAIL = 64 + DB
        tail_rows = xn2[:, 2, :]
        w_router, b_router = etake(KC, NEXP), etake(NEXP)
        logits, top8, top_f, gate4 = etake(NT, NEXP), etake(NT, 8), etake(NT, 8), etake(NT, 8)
        top_i = etake(NT, 8).bitcast(U32)
        chosen, weight, rank = etake(NT, NEXP), etake(NT, NEXP), etake(NT, NEXP)
        hits = etake(2, TOPK, NEXP)
        many = etake(NT, P)
        triple = etake(2, NT, 3 * NEXP)
        by_expert = etake(2, TOK)
        by_expert_parts = etake_bf16(P, 2 * TOK)
        over, over_hot, over_i, over_base, over_slot = etake(4), etake(16), etake(36).bitcast(I32), etake(16), etake(16)
        r_in, r_done, r_exp, r_counted, r_ready, r_listed, r_max = (sem("r_" + x) for x in ("in", "done", "exp", "counted", "ready", "listed", "max"))
        r_cast, r_left, r_tail_left, r_copied = sem("r_cast"), sem("r_left"), sem("r_tail_left"), sem("r_copied")
        with nc.Block() as block:
            @block.sync
            def _(sp):
                sp.dma_start(w_router, t["w_router"].rearrange("(c p) n -> p c n", p=P)).then_inc(r_in, 16)
                sp.dma_start(b_router[0:1, :], t["b_router"].unsqueeze(0)).then_inc(r_in, 16)

            @block.tensor
            def _(pe):
                pe.wait_ge(r_in, 32)
                for i in range(NT):
                    r = ROWS[i]
                    for c in range(KC):
                        nc.tensor.matmul(banks[0:r, 5 + i, 0:NEXP], xnT[:, c, P * i:P * i + r], w_router[:, c, :], start=(c == 0), stop=False)
                    nc.tensor.matmul(banks[0:r, 5 + i, 0:NEXP], ones[0:1, 0:r], b_router[0:1, :], start=False, stop=True).then_inc(r_done, 1)
                pe.wait_ge(r_counted, 1)
                for i in range(NT):
                    for k in range(i + 1):
                        nc.tensor.matmul(banks[:, 1, NEXP * i:NEXP * i + NEXP], const("before") if k == i else ones, chosen[:, k, :], start=(k == 0), stop=(k == i))
                for i in range(NT):
                    mm = nc.tensor.matmul(banks[:, 2, 0:1], many[:, i, :], ones[:, 0:1], start=(i == 0), stop=(i == NT - 1))
                mm.then_inc(r_done, 1)
                pe.wait_ge(r_ready, 1)
                for x in range(2):
                    for i in range(NT):
                        r = ROWS[i]
                        mm = nc.tensor.transpose(banks[0:3 * NEXP, 5 + x, P * i:P * i + r], triple[0:r, x, i, :], ident[0:r, 0:r])
                mm.then_inc(r_done, 1)
                pe.wait_ge(r_ready, 2)
                nc.tensor.matmul(banks[:, 3, 0:1], const("before"), over[:, 0:1], start=True, stop=True).then_inc(r_done, 1)
                pe.wait_ge(r_ready, 3)
                nc.tensor.matmul(banks[0:1, 4, 0:16], const("over_expert"), over_hot, start=True, stop=True)
                nc.tensor.matmul(banks[0:1, 4, 16:17], over[:, 0:1], ones[:, 0:1], start=True, stop=True)
                nc.tensor.matmul(banks[:, 0, 0:16], const("over_base"), over_hot, start=True, stop=True).then_inc(r_done, 1)

            @block.scalar
            def _(act):
                nc.scalar.copy(xn2[32:32 + DB, 2, :], xn2[0:DB, 2, :]).then_inc(r_copied, 1)
                nc.scalar.copy(xn2[64:64 + DB, 2, :], xn2[0:DB, 2, :]).then_inc(r_copied, 1)
                nc.scalar.copy(x_parts[:, 0, 0, :], xn2[:, 0, :]).then_inc(r_cast, 1)
                act.wait_ge(r_copied, 2)
                nc.scalar.copy(tail_parts[0:TAIL, :], tail_rows[0:TAIL, :]).then_inc(r_cast, 1)
                for i in range(NT):
                    r = ROWS[i]
                    act.wait_ge(r_max, i + 1)
                    nc.scalar.activation(gate4[0:r, i, 0:4], top8[0:r, i, 0:4], ACT.Exp, bias=gate4[0:r, i, 4:5], accum_out=gate4[0:r, i, 5:6]).then_inc(r_exp, 1)
                nc.scalar.copy(x_parts[:, 1, 0, :], xn2[:, 1, :]).then_inc(r_cast, 1)
                for q in (1, 2):
                    act.wait_ge(r_left, 2 * q - 1)
                    nc.scalar.copy(x_parts[:, 0, q, :], xn2[:, 0, :]).then_inc(r_cast, 1)
                    act.wait_ge(r_tail_left, q)
                    nc.scalar.copy(tail_parts[0:TAIL, :], tail_rows[0:TAIL, :]).then_inc(r_cast, 1)
                    act.wait_ge(r_left, 2 * q)
                    nc.scalar.copy(x_parts[:, 1, q, :], xn2[:, 1, :]).then_inc(r_cast, 1)

            @block.gpsimd
            def _(pool):
                for q in range(2):
                    pool.wait_ge(r_cast, 3 * q + 1)
                    nc.gpsimd.tensor_tensor(xn2[:, 0, :], xn2[:, 0, :], x_parts[:, 0, q, :], ALU.subtract).then_inc(r_left, 1)
                    pool.wait_ge(r_cast, 3 * q + 3)
                    nc.gpsimd.tensor_tensor(xn2[:, 1, :], xn2[:, 1, :], x_parts[:, 1, q, :], ALU.subtract).then_inc(r_left, 1)

            @block.vector
            def _(dve):
                nc.vector.memset(chosen, 0.0)
                settle(nc.vector.memset(weight, 0.0))
                for i in range(NT):
                    r = ROWS[i]
                    dve.wait_ge(r_done, i + 1)
                    settle(nc.vector.tensor_copy(logits[0:r, i, :], banks[0:r, 5 + i, 0:NEXP]))
                    settle(nc.vector.max(top8[0:r, i, :], logits[0:r, i, :]))
                    nc.vector.tensor_scalar(gate4[0:r, i, 4:5], top8[0:r, i, 0:1], -1.0, None, ALU.mult).then_inc(r_max, 1)
                    settle(nc.vector.max_index(top_i[0:r, i, :], top8[0:r, i, :], logits[0:r, i, :]))
                    settle(nc.vector.tensor_copy(top_f[0:r, i, :], top_i[0:r, i, :]))
                    dve.wait_ge(r_exp, i + 1)
                    settle(nc.vector.reciprocal(gate4[0:r, i, 5:6], gate4[0:r, i, 5:6]))
                    settle(nc.vector.tensor_scalar(gate4[0:r, i, 0:4], gate4[0:r, i, 0:4], gate4[0:r, i, 5:6], None, ALU.mult))
                    for k in range(TOPK):
                        iota = const("iota")[0:r, 0:NEXP]
                        nc.vector.tensor_scalar(hits[0:r, 0, k, :], iota, top_f[0:r, i, k:k + 1], None, ALU.is_equal)
                        last = nc.vector.tensor_scalar(hits[0:r, 1, k, :], iota, top_f[0:r, i, k:k + 1], gate4[0:r, i, k:k + 1], ALU.is_equal, ALU.mult)
                    settle(last)
                    nc.vector.tensor_reduce(chosen[0:r, i, :], hits[0:r, 0].rearrange("p k e -> p e k"), X, ALU.add)
                    settle(nc.vector.tensor_reduce(weight[0:r, i, :], hits[0:r, 1].rearrange("p k e -> p e k"), X, ALU.add))
                for i in range(NT):
                    last = nc.vector.tensor_copy(many[:, i, :].rearrange("p (k e) -> p k e", k=4), chosen[:, i, :].unsqueeze(1).broadcast_to([P, 4, NEXP]))
                last.then_inc(r_counted, 1)
                for q, less in enumerate(("less_first", "less_second")):
                    dve.wait_ge(r_cast, 3 * q + 2)
                    nc.vector.scalar_tensor_tensor(tail_rows[0:TAIL, :], tail_parts[0:TAIL, :], const(less)[0:TAIL, 0:1], tail_rows[0:TAIL, :], ALU.mult, ALU.add).then_inc(r_tail_left, 1)
                dve.wait_ge(r_done, 4)
                flat = rank.rearrange("p a b -> p (a b)")
                settle(nc.vector.scalar_tensor_tensor(flat, banks[:, 1, 0:NT * NEXP], 1.0, chosen.rearrange("p a b -> p (a b)"), ALU.add, ALU.mult))
                settle(nc.vector.tensor_scalar(flat, flat, -1.0, None, ALU.add))
                for x, table in enumerate((rank, weight)):
                    for i in range(NT):
                        last = nc.vector.tensor_copy(triple[:, x, i, :].rearrange("p (k e) -> p k e", k=3), table[:, i, :].unsqueeze(1).broadcast_to([P, 3, NEXP]))
                last.then_inc(r_ready, 1)
                nc.vector.tensor_scalar(over[:, 0:1], banks[:, 2, 0:1], const("over_past")[:, 0:1], None, ALU.is_gt).then_inc(r_ready, 1)
                dve.wait_ge(r_ready, 2)
                for q in (1, 2):
                    nc.vector.tensor_copy(rank[32 * q:32 * q + DB, 2, :], rank[0:DB, 2, :])
                dve.wait_ge(r_done, 6)
                settle(nc.vector.tensor_copy(over[:, 1:2], banks[:, 3, 0:1]))
                nc.vector.tensor_scalar(over_hot, const("iota")[:, 0:16], over[:, 1:2], over[:, 0:1], ALU.is_equal, ALU.mult).then_inc(r_ready, 1)
                for x in range(2):
                    last = nc.vector.tensor_copy(by_expert[0:SPLIT, x, :], banks[0:SPLIT, 5 + x, 0:TOK])
                settle(last)
                whole, parts = by_expert[0:SPLIT].rearrange("p a b -> p (a b)"), by_expert_parts[0:SPLIT, :]
                for less in ("less_first", "less_second", None):
                    settle(nc.vector.tensor_copy(parts, whole))
                    if less:
                        settle(nc.vector.scalar_tensor_tensor(whole, parts, const(less)[0:SPLIT, 0:1], whole, ALU.mult, ALU.add))
                dve.wait_ge(r_done, 7)
                nc.vector.tensor_copy(over_i[0:1, 0:17], banks[0:1, 4, 0:17])
                settle(nc.vector.tensor_copy(over_base, banks[:, 0, 0:16]))
                nc.vector.tensor_scalar(over_slot, over_base, const("slot")[:, 0:1], None, ALU.add).then_inc(r_listed, 1)

        sel, sel_tail, selT = etake_bf16(P, 2, CAP), etake_bf16(P, CAP), etake(TOK)
        pick, pick_down = etake_bf16(P, P), etake_bf16(P, P)
        xg, xgT = etake(512), etake(4, P)
        gate, up, sgm, act_in, aT, y = etake(512), etake(512), etake(512), etake(512), etake(4, P), etake(512)
        past = etake(4)
        BG, BU, BX, BT, BA, BY, BS = 0, 1, 2, 3, 4, 5, 6
        names = ("sel", "pick", "gathered", "xkept", "xturned", "xtkept", "used", "gu", "clip", "sigm", "prod", "aturned",
                 "atkept", "pick_down", "half_down", "ydone", "ykept", "spread", "stkept", "scat", "added")
        S = {n: sem("e_" + n) for n in names}

        def unless_first(eng, s, value):
            if not (isinstance(value, int) and value == 0):
                eng.wait_ge(s, value)

        def ring_value(s, e):
            return 16 * e + 16 + dense_count[expert_slot(s)]

        def gather(pe, e):
            pe.wait_ge(S["sel"], e + 1)
            for i in range(2):
                for q in range(3):
                    for x in range(2):
                        nc.tensor.matmul(banks[64 * x:64 * x + 64, BX, :], sel[:, i, :], x_parts[:, i, q, 512 * x:512 * x + 512],
                                         start=(i == 0 and q == 0), stop=False, tile_position=(0, 64 * x))
            for x in range(2):
                mm = nc.tensor.matmul(banks[64 * x:64 * x + 64, BX, :], sel_tail[0:TAIL, :], tail_parts[0:TAIL, 512 * x:512 * x + 512],
                                      start=False, stop=True, tile_position=(0, 64 * x))
            mm.then_inc(S["gathered"], 1)

        def turn_rows(pe, e):
            pe.wait_ge(S["xkept"], e + 1)
            for k in range(4):
                mm = nc.tensor.transpose(banks[:, BT, P * k:P * k + P], xg[:, P * k:P * k + P], ident)
            mm.then_inc(S["xturned"], 1)

        def scatter(pe, e, k):
            if k == 0:
                pe.wait_ge(S["ykept"], e + 1)
                pe.wait_ge(S["stkept"], 2 * e + 2)
            pe.wait_ge(S["added"], 4 * e + k + 1)
            for x in range(2):
                rows = slice(64 * x, 64 * x + 64)
                mm = nc.tensor.matmul(banks[:, BS + x, 0:TOK], y[rows, P * k:P * k + P], selT[rows, :], start=True, stop=True)
            mm.then_inc(S["scat"], 1)

        def gate_up(pe, e, scattered):
            pe.wait_ge(S["xtkept"], e + 1)
            pe.wait_ge(S["pick"], e + 1)
            unless_first(pe, S["clip"], 3 * e)
            for b in range(2):
                for x in range(2):
                    nc.tensor.matmul(banks[64 * x:64 * x + 64, BG + b, :], pick[0:SPLIT, 0:CAP], bias_parts[0:SPLIT, D * b + 512 * x:D * b + 512 * x + 512],
                                     start=True, stop=False, tile_position=(0, 64 * x))
            for c in range(KC):
                s = expert_slot(c // 2)
                if c % 2 == 0:
                    pe.wait_ge(ring_in[s], ring_value(c // 2, e))
                w = ring[:, s, :].rearrange("p (c n) -> p c n", c=2)[:, c % 2, :]
                for b in range(2):
                    for x in range(2):
                        mm = nc.tensor.matmul(banks[64 * x:64 * x + 64, BG + b, :], xgT[:, c % 4, 64 * (c // 4):64 * (c // 4) + 64],
                                              w[:, D * b + 512 * x:D * b + 512 * x + 512], start=False, stop=(c == KC - 1), tile_position=(0, 64 * x))
                if c % 2:
                    mm.then_inc(S["used"] if c < KC - 1 else S["gu"], 1)
                if scattered is not None and c < 4:
                    scatter(pe, scattered, c)

        def spread(pe, e):
            pe.wait_ge(S["pick_down"], e + 1)
            pe.wait_ge(S["atkept"], e + 1)
            for x, b in enumerate((BT, BA)):
                mm = nc.tensor.matmul(banks[:, b, 0:TOK], pick_down[0:SPLIT, :], by_expert_parts[0:SPLIT, TOK * x:TOK * x + TOK], start=True, stop=True)
            mm.then_inc(S["spread"], 1)

        def turn_product(pe, e):
            pe.wait_ge(S["prod"], e + 1)
            for k in range(4):
                mm = nc.tensor.transpose(banks[:, BA, P * k:P * k + P], act_in[:, P * k:P * k + P], ident)
            mm.then_inc(S["aturned"], 1)

        def down_half(pe, e, part):
            if part == 0:
                unless_first(pe, S["ykept"], e)
                for x in range(2):
                    nc.tensor.matmul(banks[64 * x:64 * x + 64, BY, :], pick_down[0:SPLIT, 0:CAP], bias_parts[0:SPLIT, 2 * D + 512 * x:2 * D + 512 * x + 512],
                                     start=True, stop=False, tile_position=(0, 64 * x))
            s = expert_slot(4 + part)
            pe.wait_ge(ring_in[s], ring_value(4 + part, e))
            for c in range(4):
                w = ring[:, s, :].rearrange("p (c n) -> p c n", c=4)[:, c, :]
                for x in range(2):
                    mm = nc.tensor.matmul(banks[64 * x:64 * x + 64, BY, :], aT[:, c, 64 * part:64 * part + 64],
                                          w[:, 512 * x:512 * x + 512], start=False, stop=(part == 1 and c == 3), tile_position=(0, 64 * x))
            mm.then_inc(S["ydone" if part else "half_down"], 1)

        def load_gate_up(sp, e, done):
            for s in range(4):
                if s < 3:
                    sp.wait_ge(S["used"], 3 * done - 2 + s)
                else:
                    sp.wait_ge(S["gu"], done)
                load_expert_slot(sp, e, s)

        def load_down(sp, e, done):
            sp.wait_ge(S["half_down"], done)
            load_expert_slot(sp, e, 4)
            sp.wait_ge(S["ydone"], done)
            load_expert_slot(sp, e, 5)

        def keep_rows(act, e):
            act.wait_ge(S["gathered"], e + 1)
            nc.scalar.copy(xg, banks[:, BX, :]).then_inc(S["xkept"], 1)

        def keep_rowsT(act, e):
            act.wait_ge(S["xturned"], e + 1)
            nc.scalar.copy(xgT.rearrange("p a b -> p (a b)"), banks[:, BT, :]).then_inc(S["xtkept"], 1)

        def sigmoid(act, e):
            act.wait_ge(S["clip"], 3 * e + 1)
            nc.scalar.activation(sgm, gate, ACT.Sigmoid, scale=ALPHA).then_inc(S["sigm"], 1)

        def keep_productT(act, e):
            act.wait_ge(S["aturned"], e + 1)
            nc.scalar.copy(aT.rearrange("p a b -> p (a b)"), banks[:, BA, :]).then_inc(S["atkept"], 1)

        def keep_out(act, e):
            act.wait_ge(S["ydone"], e + 1)
            unless_first(act, S["scat"], 4 * e)
            nc.scalar.copy(y, banks[:, BY, :]).then_inc(S["ykept"], 1)

        def select(position):
            for i in range(2):
                nc.vector.tensor_scalar(sel[:, i, :], const("iota")[:, 0:CAP], position(i), None, ALU.is_equal)
            nc.vector.tensor_scalar(sel_tail[0:TAIL, :], const("iota")[0:TAIL, 0:CAP], position(2)[0:TAIL], None, ALU.is_equal).then_inc(S["sel"], 1)

        def picked(e, to, name):
            nc.vector.tensor_copy(to[0:SPLIT, :], const("expert_of")[0:SPLIT, bass.ds(e, 1)].broadcast_to([SPLIT, P])).then_inc(S[name], 1)

        def clip_product(dve, e):
            dve.wait_ge(S["gu"], e + 1)
            nc.vector.tensor_scalar(gate, banks[:, BG, :], LIMIT, None, ALU.min).then_inc(S["clip"], 1)
            nc.vector.tensor_scalar(up, banks[:, BU, :], LIMIT, -LIMIT, ALU.min, ALU.max).then_inc(S["clip"], 1)
            dve.wait_ge(S["clip"], 3 * e + 2)
            nc.vector.scalar_tensor_tensor(up, up, 1.0, gate, ALU.add, ALU.mult).then_inc(S["clip"], 1)

        def product(dve, e):
            dve.wait_ge(S["sigm"], e + 1)
            dve.wait_ge(S["clip"], 3 * e + 3)
            nc.vector.tensor_tensor(act_in, up, sgm, ALU.mult).then_inc(S["prod"], 1)

        def select_by_slot(dve, e, slot_number):
            dve.wait_ge(S["spread"], e + 1)
            unless_first(dve, S["scat"], 4 * e)
            nc.vector.tensor_scalar(selT, banks[:, BT, 0:TOK], slot_number, None, ALU.is_equal).then_inc(S["stkept"], 1)
            dve.wait_ge(S["stkept"], 2 * e + 1)
            nc.vector.tensor_tensor(selT, banks[:, BA, 0:TOK], selT, ALU.mult).then_inc(S["stkept"], 1)

        def add(dve, e, k):
            dve.wait_ge(S["scat"], 4 * e + k + 1)
            v = acc[:, k:k + 5:4, :]
            nc.vector.tensor_tensor(v, banks[:, BS:BS + 2, 0:TOK], v, ALU.add).then_inc(S["added"], 1)

        n_items = TOK * TOPK // CAP
        with nc.Block() as block:
            @block.sync
            def _(sp):
                load_gate_up(sp, 1, 1)
                with sp.Fori(2, NEXP) as e:
                    load_gate_up(sp, e, e)
                    load_down(sp, e - 1, e - 1)
                n = sp.value_load(over_i[0:1, 16:17], min_val=0, max_val=n_items)
                with sp.If(n > 0):
                    load_gate_up(sp, sp.value_load(over_i[0:1, 0:1], min_val=0, max_val=NEXP - 1), NEXP)
                load_down(sp, NEXP - 1, NEXP - 1)
                with sp.If(n > 0):
                    load_down(sp, sp.value_load(over_i[0:1, 0:1], min_val=0, max_val=NEXP - 1), NEXP)

            @block.tensor
            def _(pe):
                def step(e, first=False, last=False):
                    gate_up(pe, e, e - 2 if not first else None)
                    spread(pe, e - 1)
                    if not last:
                        gather(pe, e + 1)
                    down_half(pe, e - 1, 0)
                    if not last:
                        pe.wait_ge(S["stkept"], 2 * e)
                        turn_rows(pe, e + 1)
                    down_half(pe, e - 1, 1)
                    if last:
                        pe.wait_ge(S["stkept"], 2 * e)
                    turn_product(pe, e)

                gather(pe, 0)
                turn_rows(pe, 0)
                gate_up(pe, 0, None)
                gather(pe, 1)
                turn_rows(pe, 1)
                turn_product(pe, 0)
                step(1, first=True)
                with pe.Fori(2, NEXP - 1) as e:
                    step(e)
                step(NEXP - 1, last=True)
                for k in range(4):
                    scatter(pe, NEXP - 2, k)
                spread(pe, NEXP - 1)
                down_half(pe, NEXP - 1, 0)
                down_half(pe, NEXP - 1, 1)
                for k in range(4):
                    scatter(pe, NEXP - 1, k)

            @block.scalar
            def _(act):
                def step(e, last=False):
                    sigmoid(act, e)
                    if not last:
                        keep_rows(act, e + 1)
                        keep_rowsT(act, e + 1)
                    keep_out(act, e - 1)
                    keep_productT(act, e)

                keep_rows(act, 0)
                keep_rowsT(act, 0)
                keep_rows(act, 1)
                keep_rowsT(act, 1)
                sigmoid(act, 0)
                keep_productT(act, 0)
                step(1)
                with act.Fori(2, NEXP - 1) as e:
                    step(e)
                step(NEXP - 1, last=True)
                keep_out(act, NEXP - 1)

            @block.vector
            def _(dve):
                ranks = lambda e: (lambda i: rank[:, i, bass.ds(e, 1)])

                def step(e, first=False, last=False):
                    if not first:
                        for k in range(4):
                            add(dve, e - 2, k)
                        dve.wait_ge(S["ydone"], e - 1)
                    picked(e - 1, pick_down, "pick_down")
                    if not last:
                        dve.wait_ge(S["gathered"], e + 1)
                        select(ranks(e + 1))
                    clip_product(dve, e)
                    if not last:
                        picked(e + 1, pick, "pick")
                    select_by_slot(dve, e - 1, const("slot")[:, 0:1])
                    product(dve, e)

                nc.vector.memset(acc, 0.0).then_inc(S["added"], 1)
                select(ranks(0))
                picked(0, pick, "pick")
                dve.wait_ge(S["gathered"], 1)
                select(ranks(1))
                clip_product(dve, 0)
                picked(1, pick, "pick")
                product(dve, 0)
                step(1, first=True)
                with dve.Fori(2, NEXP - 1) as e:
                    step(e)
                step(NEXP - 1, last=True)
                for k in range(4):
                    add(dve, NEXP - 2, k)
                dve.wait_ge(S["ydone"], NEXP - 1)
                picked(NEXP - 1, pick_down, "pick_down")
                select_by_slot(dve, NEXP - 1, const("slot")[:, 0:1])
                for k in range(4):
                    add(dve, NEXP - 1, k)

        def listed(eng):
            return eng.value_load(over_i[0:1, 16:17], min_val=0, max_val=n_items)

        def listed_expert(eng, k):
            return eng.value_load(over_i[0:1, bass.ds(k, 1)], min_val=0, max_val=NEXP - 1)

        with nc.Block() as block:
            @block.sync
            def _(sp):
                n = listed(sp)
                with sp.Fori(1, n_items) as k:
                    with sp.If(n > k):
                        e = listed_expert(sp, k)
                        load_gate_up(sp, e, k + NEXP)
                        load_down(sp, e, k + NEXP)

            @block.tensor
            def _(pe):
                n = listed(pe)
                with pe.Fori(0, n_items) as k:
                    with pe.If(n > k):
                        m = k + NEXP
                        gather(pe, m)
                        turn_rows(pe, m)
                        gate_up(pe, m, None)
                        turn_product(pe, m)
                        spread(pe, m)
                        down_half(pe, m, 0)
                        down_half(pe, m, 1)
                        for c in range(4):
                            scatter(pe, m, c)

            @block.scalar
            def _(act):
                n = listed(act)
                with act.Fori(0, n_items) as k:
                    with act.If(n > k):
                        m = k + NEXP
                        keep_rows(act, m)
                        keep_rowsT(act, m)
                        sigmoid(act, m)
                        keep_productT(act, m)
                        keep_out(act, m)

            @block.vector
            def _(dve):
                n = listed(dve)
                o_past = sem("o_past")
                with dve.Fori(0, n_items) as k:
                    with dve.If(n > k):
                        m = k + NEXP
                        e = listed_expert(dve, k)
                        for i in range(NT):
                            last = nc.vector.tensor_scalar(past[:, i:i + 1], rank[:, i, bass.ds(e, 1)], over_base[:, bass.ds(k, 1)], None, ALU.subtract)
                        last.then_inc(o_past, 1)
                        dve.wait_ge(o_past, k + 1)
                        select(lambda i: past[:, i:i + 1])
                        picked(e, pick, "pick")
                        picked(e, pick_down, "pick_down")
                        clip_product(dve, m)
                        product(dve, m)
                        select_by_slot(dve, m, over_slot[:, bass.ds(k, 1)])
                        for c in range(4):
                            add(dve, m, c)

        f_turned, f_added = sem("f_turned"), sem("f_added")
        with nc.Block() as block:
            @block.tensor
            def _(pe):
                for i in range(NT):
                    r = ROWS[i]
                    for n in range(2):
                        for c in range(4):
                            mm = nc.tensor.transpose(banks[0:r, 2 * i + n, P * c:P * c + P], acc[:, 4 * n + c, P * i:P * i + r], ident)
                        mm.then_inc(f_turned, 1)

            @block.vector
            def _(dve):
                for i in range(NT):
                    r = ROWS[i]
                    for n in range(2):
                        dve.wait_ge(f_turned, 2 * i + n + 1)
                        v = h[0:r, i, 512 * n:512 * n + 512]
                        nc.vector.tensor_tensor(v, banks[0:r, 2 * i + n, :], v, ALU.add).then_inc(f_added, 1)

            @block.sync
            def _(sp):
                for i in range(2):
                    sp.wait_ge(f_added, 2 * i + 2)
                    store(sp, t["y_prompt"][0, P * i:P * i + P, :], h[:, i, :], "y")
                sp.wait_ge(f_added, 6)
                store(sp, t["y_sample"].rearrange("a b d -> (a b) d"), h[0:DB, 2, :], "y")
                for group, s in stored.items():
                    sp.wait_ge(s, store_count[group])


_INPUTS = ["x_prompt", "x_sample", "cache_nsa_cmp_k", "cache_nsa_cmp_v", "cache_nsa_sel_k", "cache_nsa_sel_v",
           "cache_nsa_win_k", "cache_nsa_win_v", "cache_moba_k", "cache_moba_v", "page_table", "norm_attn", "w_in",
           "g_qa", "g_ka", "g_kc", "cmp_pos_k", "cmp_w1_k", "cmp_w2_k", "cmp_pos_v", "cmp_w1_v", "cmp_w2_v", "g_qb",
           "g_kb", "w_up_a", "w_up_b", "w_out", "norm_ffn", "w_router", "b_router", "w_gu", "b_gu", "w_down", "b_down"]
_KV, _KVB = (NSA_G, HD), (MOBA_H, HD)
_OUTPUTS = [("y_prompt", (1, SEQ, D)), ("y_sample", (DB, 1, D))]
for _side, _lead, _win in (("p_", (1, SEQ), (1, SEQ)), ("s_", (DB, 1), (DB, SEQ + 1))):
    _OUTPUTS += [(_side + n, _lead + _KV) for n in ("k_c", "v_c", "k_s", "v_s")]
    _OUTPUTS += [(_side + n, _win + _KV) for n in ("k_w", "v_w")]
    _OUTPUTS += [(_side + n, _lead + _KVB) for n in ("k_b", "v_b")]


def kernel(**inputs):
    import concourse.bacc as _bacc
    from concourse.bass_utils import run_bass_kernel_spmd as _run

    const_at, packed = constants()
    nc = _bacc.Bacc("TRN2", target_bir_lowering=False, num_devices=1)
    arrays, t = {"const": packed}, {}
    for name in _INPUTS:
        arrays[name] = np.ascontiguousarray(inputs[name])
    for name, a in arrays.items():
        t[name] = nc.dram_tensor(name, a.shape, mybir.dt.from_np(a.dtype), kind="ExternalInput").ap()
    for name, shape in _OUTPUTS:
        t[name] = nc.dram_tensor(name, shape, F32, kind="ExternalOutput").ap()
    build(nc, t, const_at, packed.shape[1])
    r = _run(nc, [arrays], core_ids=[0])
    return tuple(r.results[0][name] for name, _ in _OUTPUTS)
```
